# Optimizing a Trainium2 kernel written in Bass

```python
import math
import jax, jax.numpy as jnp
from jax import lax
import numpy as np

D_MODEL = 2048
BATCH = 1
SEQ = 512
DEPTH = 1

MEM_LEN = 256
A_HEADS = 6
A_HEAD_DIM = 128
A_KV_RANK = 256
IDX_HEADS = 16
IDX_DIM = 64
TOPK_MAX = 256
Q_BLOCK = 128
B_HEADS = 12
B_KV_HEADS = 2
B_HEAD_DIM = 64
WINDOW = 128
BAND_BLOCK = 128
C_HEADS = 4
C_HEAD_DIM = 128
NUM_BUCKETS = 32
MAX_DISTANCE = 128
EPS = 1e-6

A_WIDTH = A_HEADS * A_HEAD_DIM
B_WIDTH = B_HEADS * B_HEAD_DIM
B_KV_WIDTH = B_KV_HEADS * B_HEAD_DIM
C_WIDTH = C_HEADS * C_HEAD_DIM
N_BRANCH = 3
IN_SIZES = (A_WIDTH, A_KV_RANK, IDX_HEADS * IDX_DIM, IDX_DIM, IDX_HEADS, A_WIDTH,
            B_WIDTH, B_KV_WIDTH, B_KV_WIDTH, B_WIDTH,
            C_WIDTH, C_WIDTH,
            N_BRANCH * D_MODEL)
IN_COLS = sum(IN_SIZES)


def rmsnorm(x, g):
    xf = x.astype(jnp.float32)
    y = xf * lax.rsqrt(jnp.mean(xf * xf, axis=-1, keepdims=True) + EPS)
    return (y * g.astype(jnp.float32)).astype(x.dtype)

def layernorm(x, g, b):
    xf = x.astype(jnp.float32)
    mu = jnp.mean(xf, axis=-1, keepdims=True)
    var = jnp.mean(jnp.square(xf - mu), axis=-1, keepdims=True)
    y = (xf - mu) * lax.rsqrt(var + EPS)
    return (y * g.astype(jnp.float32) + b.astype(jnp.float32)).astype(x.dtype)

def split_cols(y, sizes):
    cuts = np.cumsum(np.array(sizes))[:-1].tolist()
    return jnp.split(y, cuts, axis=-1)

def t5_bucket(dist):
    n = jnp.maximum(dist, 0)
    max_exact = NUM_BUCKETS // 2
    nf = jnp.maximum(n, 1).astype(jnp.float32)
    large = max_exact + (jnp.log(nf / max_exact) / math.log(MAX_DISTANCE / max_exact)
                         * (NUM_BUCKETS - max_exact)).astype(jnp.int32)
    large = jnp.minimum(large, NUM_BUCKETS - 1)
    return jnp.where(n < max_exact, n, large)

def dsa_attention(q, k, v, iq, ik, iw, bias_tab, topk):
    bsz, seq, nh, dh = q.shape
    nb = seq // Q_BLOCK
    key_pos = jnp.arange(seq, dtype=jnp.int32)

    def to_blocks(t):
        return jnp.moveaxis(t.reshape((bsz, nb, Q_BLOCK) + t.shape[2:]), 1, 0)

    def block_fn(args):
        qb, iqb, iwb, t0 = args
        tpos = t0 + jnp.arange(Q_BLOCK, dtype=jnp.int32)
        rel = jax.nn.relu(jnp.einsum('bthd,bsd->bths', iqb, ik))
        score = jnp.einsum('bths,bth->bts', rel, iwb).astype(jnp.float32)
        causal = key_pos[None, :] <= tpos[:, None]
        score = jnp.where(causal[None], score, -jnp.inf)
        _, idx = lax.top_k(score, topk)
        kg = jax.vmap(lambda kk, ii: kk[ii])(k, idx)
        vg = jax.vmap(lambda vv, ii: vv[ii])(v, idx)
        logits = jnp.einsum('bthd,btkhd->bthk', qb, kg).astype(jnp.float32) * (dh ** -0.5)
        dist = tpos[None, :, None] - idx
        bias = jnp.transpose(bias_tab[t5_bucket(dist)], (0, 1, 3, 2)).astype(jnp.float32)
        logits = jnp.where((dist >= 0)[:, :, None, :], logits + bias, -jnp.inf)
        p = jax.nn.softmax(logits, axis=-1).astype(vg.dtype)
        return jnp.einsum('bthk,btkhd->bthd', p, vg)

    t0s = jnp.arange(nb, dtype=jnp.int32) * Q_BLOCK
    out = lax.map(block_fn, (to_blocks(q), to_blocks(iq), to_blocks(iw), t0s))
    return jnp.moveaxis(out, 0, 1).reshape(bsz, seq, nh * dh)

def sliding_window_attention(q, k, v, sinks, bias_tab):
    bsz, seq, hq, dh = q.shape
    hkv = k.shape[2]
    g = hq // hkv
    blk = BAND_BLOCK
    nb = seq // blk
    qb = q.reshape(bsz, nb, blk, hkv, g, dh)

    def band(t):
        tb = t.reshape(bsz, nb, blk, hkv, dh)
        prev = jnp.concatenate([jnp.zeros_like(tb[:, :1]), tb[:, :-1]], axis=1)
        return jnp.concatenate([prev, tb], axis=2)

    kband, vband = band(k), band(v)
    logits = jnp.einsum('bnqhgd,bnkhd->bnhgqk', qb, kband).astype(jnp.float32) * (dh ** -0.5)
    qi = jnp.arange(blk, dtype=jnp.int32)[:, None]
    kj = jnp.arange(2 * blk, dtype=jnp.int32)[None, :]
    dist = blk + qi - kj
    bias = jnp.transpose(bias_tab[t5_bucket(dist)], (2, 0, 1)).reshape(hkv, g, blk, 2 * blk)
    key_pos = jnp.arange(nb, dtype=jnp.int32)[:, None, None] * blk + kj[None] - blk
    valid = (dist >= 0) & (dist < WINDOW) & (key_pos >= 0)
    logits = jnp.where(valid[None, :, None, None], logits + bias.astype(jnp.float32), -jnp.inf)
    sink = jnp.broadcast_to(sinks.astype(jnp.float32).reshape(hkv, g, 1, 1), logits.shape[:-1] + (1,))
    p = jax.nn.softmax(jnp.concatenate([logits, sink], axis=-1), axis=-1)[..., :-1]
    out = jnp.einsum('bnhgqk,bnkhd->bnqhgd', p.astype(v.dtype), vband)
    return out.reshape(bsz, seq, hq * dh)

def memory_attention(q, k, v):
    bsz, seq, nh, dh = q.shape
    logits = jnp.einsum('bthd,bmhd->bhtm', q, k).astype(jnp.float32) * (dh ** -0.5)
    p = jax.nn.softmax(logits, axis=-1).astype(v.dtype)
    return jnp.einsum('bhtm,bmhd->bthd', p, v).reshape(bsz, seq, nh * dh)

def first_inputs(seed: int = 0) -> dict:
    key = jax.random.key(seed)
    ks = jax.random.split(key, 24)
    f32 = jnp.float32

    def w(k, shape, fan_in):
        return jax.random.normal(k, shape, f32) * (fan_in ** -0.5)

    def gain(k, shape):
        return 1.0 + 0.05 * jax.random.normal(k, shape, f32)

    return {
        "x": jax.random.normal(ks[0], (BATCH, SEQ, D_MODEL), f32),
        "mem": jax.random.normal(ks[1], (BATCH, MEM_LEN, D_MODEL), f32),
        "norm_g": gain(ks[2], (DEPTH, D_MODEL)),
        "w_in": w(ks[3], (DEPTH, D_MODEL, IN_COLS), D_MODEL),
        "kv_norm_g": gain(ks[4], (DEPTH, A_KV_RANK)),
        "w_kv_up": w(ks[5], (DEPTH, A_KV_RANK, 2 * A_WIDTH), A_KV_RANK),
        "idx_k_ln_g": gain(ks[6], (DEPTH, IDX_DIM)),
        "idx_k_ln_b": 0.02 * jax.random.normal(ks[7], (DEPTH, IDX_DIM), f32),
        "q_norm_a": gain(ks[8], (DEPTH, A_HEAD_DIM)),
        "k_norm_a": gain(ks[9], (DEPTH, A_HEAD_DIM)),
        "q_norm_b": gain(ks[10], (DEPTH, B_HEAD_DIM)),
        "k_norm_b": gain(ks[11], (DEPTH, B_HEAD_DIM)),
        "sinks_b": 0.5 * jax.random.normal(ks[12], (DEPTH, B_HEADS), f32),
        "mem_norm_g": gain(ks[13], (DEPTH, D_MODEL)),
        "w_mem_kv": w(ks[14], (DEPTH, D_MODEL, 2 * C_WIDTH), D_MODEL),
        "q_norm_c": gain(ks[15], (DEPTH, C_HEAD_DIM)),
        "k_norm_c": gain(ks[16], (DEPTH, C_HEAD_DIM)),
        "w_up_a": w(ks[17], (DEPTH, A_WIDTH, D_MODEL), A_WIDTH),
        "w_up_b": w(ks[18], (DEPTH, B_WIDTH, D_MODEL), B_WIDTH),
        "w_up_c": w(ks[19], (DEPTH, C_WIDTH, D_MODEL), C_WIDTH),
        "gate_bias": 0.02 * jax.random.normal(ks[20], (DEPTH, N_BRANCH * D_MODEL), f32),
        "w_o": w(ks[21], (DEPTH, D_MODEL, D_MODEL), D_MODEL),
        "rel_bias": 0.5 * jax.random.normal(ks[22], (NUM_BUCKETS, A_HEADS + B_HEADS), f32),
    }

def first_block(x, mem, norm_g, w_in, kv_norm_g, w_kv_up, idx_k_ln_g, idx_k_ln_b,
              q_norm_a, k_norm_a, q_norm_b, k_norm_b, sinks_b, mem_norm_g, w_mem_kv,
              q_norm_c, k_norm_c, w_up_a, w_up_b, w_up_c, gate_bias, w_o, rel_bias):
    bsz, seq, _ = x.shape
    mlen = mem.shape[1]
    topk = min(TOPK_MAX, seq // 4)
    bias_a = rel_bias[:, :A_HEADS]
    bias_b = rel_bias[:, A_HEADS:]
    for l in range(DEPTH):
        h = rmsnorm(x, norm_g[l])
        (a_q, a_ckv, i_q, i_k, i_w, a_gate,
         b_q, b_k, b_v, b_gate,
         c_q, c_gate, mix_gate) = split_cols(h @ w_in[l], IN_SIZES)

        ckv = rmsnorm(a_ckv, kv_norm_g[l])
        a_k, a_v = jnp.split(ckv @ w_kv_up[l], 2, axis=-1)
        qa = rmsnorm(a_q.reshape(bsz, seq, A_HEADS, A_HEAD_DIM), q_norm_a[l])
        ka = rmsnorm(a_k.reshape(bsz, seq, A_HEADS, A_HEAD_DIM), k_norm_a[l])
        va = a_v.reshape(bsz, seq, A_HEADS, A_HEAD_DIM)
        iq = i_q.reshape(bsz, seq, IDX_HEADS, IDX_DIM)
        ik = layernorm(i_k, idx_k_ln_g[l], idx_k_ln_b[l])
        iw = i_w * (IDX_HEADS ** -0.5) * (IDX_DIM ** -0.5)
        oa = dsa_attention(qa, ka, va, iq, ik, iw, bias_a, topk) * jax.nn.silu(a_gate)

        qb = rmsnorm(b_q.reshape(bsz, seq, B_HEADS, B_HEAD_DIM), q_norm_b[l])
        kb = rmsnorm(b_k.reshape(bsz, seq, B_KV_HEADS, B_HEAD_DIM), k_norm_b[l])
        vb = b_v.reshape(bsz, seq, B_KV_HEADS, B_HEAD_DIM)
        ob = sliding_window_attention(qb, kb, vb, sinks_b[l], bias_b) * jax.nn.silu(b_gate)

        m_k, m_v = jnp.split(rmsnorm(mem, mem_norm_g[l]) @ w_mem_kv[l], 2, axis=-1)
        qc = rmsnorm(c_q.reshape(bsz, seq, C_HEADS, C_HEAD_DIM), q_norm_c[l])
        kc = rmsnorm(m_k.reshape(bsz, mlen, C_HEADS, C_HEAD_DIM), k_norm_c[l])
        vc = m_v.reshape(bsz, mlen, C_HEADS, C_HEAD_DIM)
        oc = memory_attention(qc, kc, vc) * jax.nn.silu(c_gate)

        g_a, g_b, g_c = jnp.split(jax.nn.sigmoid(mix_gate + gate_bias[l]), N_BRANCH, axis=-1)
        merged = g_a * (oa @ w_up_a[l]) + g_b * (ob @ w_up_b[l]) + g_c * (oc @ w_up_c[l])
        x = x + merged @ w_o[l]
    return x


HEAD_DIM = 64
MIX_WIDTH = D_MODEL
N_HEADS_A = (MIX_WIDTH // 2) // HEAD_DIM
N_HEADS_B = (MIX_WIDTH // 2) // HEAD_DIM
WIDTH_A = N_HEADS_A * HEAD_DIM
WIDTH_B = N_HEADS_B * HEAD_DIM
IN_WIDTH = 4 * WIDTH_A + 4 * WIDTH_B
DILATED_CONFIGS = ((128, 1), (512, 4), (2048, 16))
T5_MAX_DISTANCE = 1024
GRID_W = 64
NA_ROWS = 8
NA_COLS = 16
NA_COL_BLOCKS = GRID_W // NA_COLS
NA_KEY_COLS = 2 * NA_COLS
DEEPNORM_ALPHA = (2.0 * DEPTH) ** 0.25
DEEPNORM_BETA = (8.0 * DEPTH) ** -0.25
LN_EPS = 1e-5
NEG_INF = -1e30


def _t5_buckets(rel):
    half = NUM_BUCKETS // 2
    max_exact = half // 2
    n = np.abs(rel)
    large = max_exact + (np.log(np.maximum(n, 1) / max_exact)
                         / np.log(T5_MAX_DISTANCE / max_exact)
                         * (half - max_exact)).astype(np.int64)
    large = np.minimum(large, half - 1)
    return ((rel > 0).astype(np.int64) * half + np.where(n < max_exact, n, large)).astype(np.int32)

def _layer_norm(x, g, b):
    xf = x.astype(jnp.float32)
    mu = xf.mean(-1, keepdims=True)
    var = jnp.square(xf - mu).mean(-1, keepdims=True)
    return ((xf - mu) * lax.rsqrt(var + LN_EPS) * g.astype(jnp.float32)
            + b.astype(jnp.float32)).astype(x.dtype)

def _dilated_branch(q, k, v, t5_table, window, dilation):
    B, H, S, hd = q.shape
    blk = window // (2 * dilation)
    L = S // dilation
    nb = -(-L // blk)
    Lp = nb * blk
    scale = HEAD_DIM ** -0.5

    def strided(a):
        return a.reshape(B, H, L, dilation, hd).transpose(0, 1, 3, 2, 4)

    qs = jnp.pad(strided(q), ((0, 0), (0, 0), (0, 0), (0, Lp - L), (0, 0)))
    qs = qs.reshape(B, H, dilation, nb, blk, hd)

    def key_blocks(a):
        a = jnp.pad(strided(a), ((0, 0), (0, 0), (0, 0), (blk, Lp - L + blk), (0, 0)))
        a = a.reshape(B, H, dilation, nb + 2, blk, hd)
        return jnp.concatenate([a[:, :, :, :nb], a[:, :, :, 1:nb + 1], a[:, :, :, 2:]], axis=4)

    ks, vs = key_blocks(k), key_blocks(v)
    rel = np.arange(3 * blk)[None, :] - blk - np.arange(blk)[:, None]
    band = np.abs(rel) <= blk
    key_abs = (np.arange(nb)[:, None] - 1) * blk + np.arange(3 * blk)[None, :]
    valid = (key_abs >= 0) & (key_abs < L)
    mask = band[None] & valid[:, None, :]
    bias = jnp.take(t5_table, _t5_buckets(rel * dilation), axis=0)
    bias = jnp.moveaxis(bias.astype(jnp.float32), -1, 0)

    s = jnp.einsum('bhrnqd,bhrnkd->bhrnqk', qs, ks).astype(jnp.float32) * scale
    s = jnp.where(mask, s + bias[None, :, None, None], NEG_INF)
    m = s.max(-1, keepdims=True)
    p = jnp.exp(s - m)
    den = p.sum(-1, keepdims=True)
    o = jnp.einsum('bhrnqk,bhrnkd->bhrnqd', p, vs.astype(jnp.float32)) / den
    lse = (m + jnp.log(den))[..., 0]
    o = o.reshape(B, H, dilation, Lp, hd)[:, :, :, :L].transpose(0, 1, 3, 2, 4).reshape(B, H, S, hd)
    lse = lse.reshape(B, H, dilation, Lp)[..., :L].transpose(0, 1, 3, 2).reshape(B, H, S)
    return o, lse

def _dilated_attention(q, k, v, t5_table):
    outs, lses = [], []
    for window, dilation in DILATED_CONFIGS:
        o, lse = _dilated_branch(q, k, v, t5_table, window, dilation)
        outs.append(o)
        lses.append(lse)
    wts = jax.nn.softmax(jnp.stack(lses, 0), axis=0)
    return jnp.einsum('cbhs,cbhsd->bhsd', wts, jnp.stack(outs, 0))

def _neighbourhood_attention(q, k, v, rpb):
    B, H, S, hd = q.shape
    rows = S // GRID_W
    kr = min(NA_ROWS, rows)
    scale = HEAD_DIM ** -0.5
    row_start = np.clip(np.arange(rows) - kr // 2, 0, rows - kr)
    row_idx = row_start[:, None] + np.arange(kr)
    qcol = np.arange(GRID_W).reshape(NA_COL_BLOCKS, NA_COLS)
    blk_start = np.clip(qcol[:, 0] - NA_COLS // 2, 0, GRID_W - NA_KEY_COLS)
    col_idx = blk_start[:, None] + np.arange(NA_KEY_COLS)
    q_start = np.clip(qcol - NA_COLS // 2, 0, GRID_W - NA_COLS)
    kcol = col_idx[:, None, :]
    col_mask = (kcol >= q_start[:, :, None]) & (kcol < q_start[:, :, None] + NA_COLS)
    dcol = np.clip(kcol - qcol[:, :, None], -(NA_COLS - 1), NA_COLS - 1)
    drow = row_idx - np.arange(rows)[:, None]
    ri = (drow + NA_ROWS - 1)[None, :, None, :, None]
    ci = (dcol + NA_COLS - 1)[:, None, :, None, :]
    bias = rpb.astype(jnp.float32)[:, ri, ci]
    bias = jnp.where(col_mask[:, None, :, None, :], bias, NEG_INF)
    bias = bias.transpose(1, 0, 2, 3, 4, 5).reshape(NA_COL_BLOCKS, H, rows, NA_COLS, kr * NA_KEY_COLS)

    qb = q.reshape(B, H, rows, NA_COL_BLOCKS, NA_COLS, hd).transpose(3, 0, 1, 2, 4, 5)
    kg = k.reshape(B, H, rows, GRID_W, hd)
    vg = v.reshape(B, H, rows, GRID_W, hd)

    def row_block(args):
        q_blk, cidx, bias_blk = args
        k_blk = jnp.take(kg, cidx, axis=3)[:, :, row_idx].reshape(B, H, rows, kr * NA_KEY_COLS, hd)
        v_blk = jnp.take(vg, cidx, axis=3)[:, :, row_idx].reshape(B, H, rows, kr * NA_KEY_COLS, hd)
        s = jnp.einsum('bhrqd,bhrkd->bhrqk', q_blk, k_blk).astype(jnp.float32) * scale + bias_blk[None]
        p = jax.nn.softmax(s, axis=-1)
        return jnp.einsum('bhrqk,bhrkd->bhrqd', p, v_blk.astype(jnp.float32))

    o = lax.map(row_block, (qb, jnp.asarray(col_idx, jnp.int32), bias))
    return o.transpose(1, 2, 3, 0, 4, 5).reshape(B, H, S, hd)

def second_inputs(seed: int = 0) -> dict:
    key = jax.random.key(seed)
    ks = jax.random.split(key, 7)
    x = jax.random.normal(ks[0], (BATCH, SEQ, D_MODEL), jnp.float32)
    col_scale = np.ones((IN_WIDTH,), np.float32)
    col_scale[2 * WIDTH_A:3 * WIDTH_A] = DEEPNORM_BETA
    col_scale[4 * WIDTH_A + 2 * WIDTH_B:4 * WIDTH_A + 3 * WIDTH_B] = DEEPNORM_BETA
    w_in = (jax.random.normal(ks[1], (DEPTH, D_MODEL, IN_WIDTH), jnp.float32)
            * D_MODEL ** -0.5 * jnp.asarray(col_scale))
    w_out = jax.random.normal(ks[2], (DEPTH, MIX_WIDTH, D_MODEL), jnp.float32) * (MIX_WIDTH ** -0.5 * DEEPNORM_BETA)
    t5_bias = jax.random.normal(ks[3], (NUM_BUCKETS, N_HEADS_A), jnp.float32) * 0.5
    na_rpb = jax.random.normal(ks[4], (DEPTH, N_HEADS_B, 2 * NA_ROWS - 1, 2 * NA_COLS - 1), jnp.float32) * 0.5
    ln_gain = 1.0 + 0.05 * jax.random.normal(ks[5], (DEPTH, D_MODEL), jnp.float32)
    ln_bias = 0.02 * jax.random.normal(ks[6], (DEPTH, D_MODEL), jnp.float32)
    return {"x": x, "w_in": w_in, "w_out": w_out, "t5_bias": t5_bias,
            "na_rpb": na_rpb, "ln_gain": ln_gain, "ln_bias": ln_bias}

def second_block(x, w_in, w_out, t5_bias, na_rpb, ln_gain, ln_bias):
    B, S, _ = x.shape
    splits = np.cumsum([WIDTH_A] * 4 + [WIDTH_B] * 3)

    def heads(a, n):
        return a.reshape(B, S, n, HEAD_DIM).transpose(0, 2, 1, 3)

    def merge(o):
        return o.transpose(0, 2, 1, 3).reshape(B, S, -1)

    for layer in range(DEPTH):
        h = jnp.einsum('bsd,de->bse', x, w_in[layer])
        qa, ka, va, ga, qb, kb, vb, gb = jnp.split(h, splits, axis=-1)
        ya = _dilated_attention(heads(qa, N_HEADS_A), heads(ka, N_HEADS_A), heads(va, N_HEADS_A), t5_bias)
        yb = _neighbourhood_attention(heads(qb, N_HEADS_B), heads(kb, N_HEADS_B), heads(vb, N_HEADS_B), na_rpb[layer])
        ya = merge(ya) * jax.nn.silu(ga.astype(jnp.float32))
        yb = merge(yb) * jax.nn.silu(gb.astype(jnp.float32))
        y = jnp.concatenate([ya, yb], axis=-1).astype(x.dtype)
        out = jnp.einsum('bse,ed->bsd', y, w_out[layer])
        x = _layer_norm(DEEPNORM_ALPHA * x + out, ln_gain[layer], ln_bias[layer])
    return x


def setup_inputs(seed=0):
    out = dict(first_inputs(seed))
    for name, value in second_inputs(seed + 1).items():
        if name != "x":
            out[name + "_2"] = value
    return out


def reference(
    x, mem, norm_g, w_in, kv_norm_g, w_kv_up, idx_k_ln_g, idx_k_ln_b, q_norm_a, k_norm_a,
    q_norm_b, k_norm_b, sinks_b, mem_norm_g, w_mem_kv, q_norm_c, k_norm_c, w_up_a, w_up_b,
    w_up_c, gate_bias, w_o, rel_bias, w_in_2, w_out_2, t5_bias_2, na_rpb_2, ln_gain_2,
    ln_bias_2,
):
    x = first_block(
        x, mem, norm_g, w_in, kv_norm_g, w_kv_up, idx_k_ln_g, idx_k_ln_b, q_norm_a, k_norm_a,
        q_norm_b, k_norm_b, sinks_b, mem_norm_g, w_mem_kv, q_norm_c, k_norm_c, w_up_a, w_up_b,
        w_up_c, gate_bias, w_o, rel_bias,
    )
    return second_block(
        x, w_in_2, w_out_2, t5_bias_2, na_rpb_2, ln_gain_2, ln_bias_2,
    )


_drawn_inputs = setup_inputs


def setup_inputs(seed=0):
    import zlib

    import numpy as np

    out = dict(_drawn_inputs(seed))
    spreads = {}
    factors = {'norm_g': 4.299,
     'kv_norm_g': 8.0,
     'idx_k_ln_g': 7.492,
     'idx_k_ln_b': 8.0,
     'q_norm_a': 8.0,
     'k_norm_a': 8.0,
     'q_norm_b': 8.0,
     'k_norm_b': 8.0,
     'sinks_b': 27.52,
     'mem_norm_g': 8.0,
     'q_norm_c': 8.0,
     'k_norm_c': 8.0,
     'gate_bias': 8.0,
     't5_bias_2': 7.757,
     'na_rpb_2': 6.154,
     'ln_bias_2': 2.842}
    for name, (base, spread) in spreads.items():
        noise = np.random.default_rng([zlib.crc32(name.encode()), seed]).standard_normal(out[name].shape)
        drawn = base * np.exp(spread * noise) if base else spread * noise
        out[name] = __import__('jax').numpy.asarray(drawn.astype(out[name].dtype))
    for name, factor in factors.items():
        out[name] = (out[name] * factor).astype(out[name].dtype)
    return out
```

```python
from contextlib import ExitStack

import numpy as np

import concourse.bass as bass
from concourse import mybir

F32 = mybir.dt.float32
F32R = mybir.dt.float32r
ACT = mybir.ActivationFunctionType
ALU = mybir.AluOpType
AX = mybir.AxisListType

P = 128
D, T, MEM = 2048, 512, 256
KT = D // P
TB = T // P
GC = 256
CK = 8
HEADS_A, HEADS_B, HEADS_C = 6, 12, 4
IDX_HEADS, IDX_DIM, TOPK = 16, 64, 128
KV_RANK, A_W, B_W, C_W = 256, 768, 768, 512
EPS, LN_EPS = 1e-6, 1e-5
ALPHA = 2.0 ** 0.25
NEG = -1.0e30
FILL, TAKEN = -3.0e38, -3.3e38
HD2, HEADS_2 = 64, 16
ROW_A, ROW_B, ROW_2 = 640, 384, 1024
ITEMS_B, ITEMS_C, ITEMS_A = 6, 4, 6
COPIES = 8 + 16 - 1

G_CKV, G_IK, G_BKV, G_MEM, G_KVUP = 0, 1, 2, 3, 7
G_IQ, G_Q, G_GATE, G_MIX = 8, 12, 20, 28
G_UP, G_WO, G_IN2, G_OUT2 = 52, 60, 68, 100
N_GROUPS = 108

PAR = {}
_at = 0
for _n, _w in (("norm_g", 16), ("mem_g", 16), ("kv_g", 2), ("ik_g", 1), ("ik_b", 1), ("k_a", 1),
               ("k_b", 1), ("k_c", 1), ("q_g", 16), ("gate_b", 48), ("sink", 12)):
    PAR[_n] = (_at, _at + _w)
    _at += _w
N_PAR = _at

CON = {}
_at = 0
for _n, _w in (("ident", 128), ("ones", 128), ("aident", 128), ("heads", 32), ("nmask", 128)):
    CON[_n] = (_at, _at + _w)
    _at += _w
N_CON = _at
BLK_START = (0, 8, 24, 32)


def t5_causal(dist):
    n = np.maximum(dist, 0)
    nf = np.maximum(n, 1).astype(np.float32)
    large = 16 + (np.log(nf / np.float32(16)) / np.float32(np.log(8.0)) * np.float32(16)).astype(np.int32)
    return np.where(n < 16, n, np.minimum(large, 31))


def t5_both(rel):
    n = np.abs(rel)
    large = 8 + (np.log(np.maximum(n, 1) / 8) / np.log(1024 / 8) * 8).astype(np.int64)
    return (rel > 0) * 16 + np.where(n < 8, n, np.minimum(large, 15))


def one_hot_rows(bucket, extra):
    rows = np.zeros((33, bucket.size), np.float32)
    rows[bucket, np.arange(bucket.size)] = 1.0
    rows[32] = extra
    return rows


def position_tables():
    m = np.arange(ROW_A)
    dist = 511 - m
    e_a = one_hot_rows(t5_causal(dist), np.where(dist >= 0, 0.0, NEG))
    m = np.arange(ROW_B)
    dist = 255 - m
    e_b = one_hot_rows(t5_causal(dist), np.where((dist >= 0) & (dist < 128), 0.0, NEG))
    rel = np.arange(ROW_2) - 511
    times = sum(((rel % d == 0) & (np.abs(rel) <= 64 * d)).astype(np.int64) for d in (1, 4, 16))
    e_2 = one_hot_rows(t5_both(rel), np.where(times > 0, np.log(np.maximum(times, 1)), NEG))
    return np.ascontiguousarray(np.concatenate([e_a, e_b, e_2], 1), dtype=np.float32)


def constants():
    con = np.zeros((P, N_CON), np.float32)
    eye = np.eye(P, dtype=np.float32)
    con[:, slice(*CON["ident"])] = eye
    con[:, slice(*CON["ones"])] = 1.0
    con[:, slice(*CON["aident"])] = eye * np.float32(ALPHA)
    heads = np.zeros((P, 16, 2), np.float32)
    heads[:64, 0:6, 0] = 1.0
    heads[64:, 0:6, 1] = 1.0
    heads[:, 6:16, 0] = 1.0
    con[:, slice(*CON["heads"])] = heads.reshape(P, 32)
    i = np.arange(P)[:, None] % 16
    j = np.arange(32)[None, :]
    for cb in range(4):
        qc, kc = 16 * cb + i, BLK_START[cb] + j
        first = np.clip(qc - 8, 0, 48)
        a = CON["nmask"][0] + 32 * cb
        con[:, a:a + 32] = np.where((kc >= first) & (kc < first + 16), 0.0, NEG)
    return con


def build_kernel(nc, wst, x_in, mem_in, par_in, con_in, pos_in, tab1_in, tab2_in, rpb_in, lng_in, lnb_in, out):
    x_v = x_in.rearrange("(b p) d -> b p d", p=P)
    mem_v = mem_in.rearrange("(b p) d -> b p d", p=P)
    out_v = out.rearrange("a (b p) d -> (a b) p d", p=P)

    xt_d = nc.dram_tensor("xt_d", [KT, P, T], F32).ap()
    iq_d = nc.dram_tensor("iq_d", [8, P, T], F32).ap()
    q_d = nc.dram_tensor("q_d", [16, P, T], F32).ap()
    k_d = nc.dram_tensor("k_d", [16, P, T], F32).ap()
    v_d = nc.dram_tensor("v_d", [16, P, T], F32).ap()
    g_d = nc.dram_tensor("g_d", [16, P, T], F32).ap()
    o_d = nc.dram_tensor("o_d", [16, P, T], F32).ap()
    mix_d = nc.dram_tensor("mix_d", [24, P, 2 * T], F32).ap()
    x1_d = nc.dram_tensor("x1_d", [8, P, 2, T], F32).ap()
    qkvg_d = nc.dram_tensor("qkvg_d", [8, 4, 2, P, T], F32).ap()
    y_d = nc.dram_tensor("y_d", [16, P, T], F32).ap()
    first_d = nc.dram_tensor("first_d", [6, 16], F32).ap()
    rows_a = nc.dram_tensor("rows_a", [HEADS_A, COPIES, ROW_A], F32)
    rows_b = nc.dram_tensor("rows_b", [ITEMS_B, COPIES, 2 * ROW_B], F32)
    rows_2d = nc.dram_tensor("rows_2d", [HEADS_2, COPIES, ROW_2], F32)
    rows_n = nc.dram_tensor("rows_n", [HEADS_2, COPIES, ROW_2], F32)

    ctx = ExitStack()
    with ctx:
        cursor = [-(-nc.sbuf_base // 64) * 64]

        def region(size):
            at = cursor[0]
            cursor[0] += size
            return at

        def sb_at(name, shape, at, dt=F32):
            return nc.alloc_sbuf_tensor_at(name, shape, dt, offset=at)

        def sem(name):
            return ctx.enter_context(nc.semaphore(name))

        KB = 1024
        W_AT, RA, RB, Y = region(48 * KB), region(64 * KB), region(64 * KB), region(0)
        w_raw = [sb_at(f"w_raw{i}", [P, CK * GC], W_AT + 8 * KB * i) for i in range(2)]
        w_hi = [sb_at(f"w_hi{i}", [P, CK * GC], W_AT + 8 * KB * (2 + i), F32R) for i in range(2)]
        w_lo = [sb_at(f"w_lo{i}", [P, CK * GC], W_AT + 8 * KB * (4 + i), F32R) for i in range(2)]
        act_a = [sb_at(f"act_a{i}", [P, KT, T], RA + 32 * KB * i, F32R) for i in range(2)]
        act_b = [sb_at(f"act_b{i}", [P, KT, T], RB + 32 * KB * i, F32R) for i in range(2)]

        x_nat = sb_at("x_nat", [P, TB, D], RB + 32 * KB)
        mem_t = [sb_at(f"mem_t{i}", [P, KT, MEM], RB + 16 * KB * i, F32R) for i in range(2)]
        rows_1a = sb_at("rows_1a", [HEADS_A, ROW_A], RB + 16 * KB)
        rows_1b = sb_at("rows_1b", [ITEMS_B, 2 * ROW_B], RB + 19 * KB)
        rows_2 = sb_at("rows_2", [HEADS_2, ROW_2], RB + 22 * KB)
        junk = sb_at("junk", [P, D], RA + 56 * KB)
        o = 32 * KB
        ckv_t = [sb_at(f"ckv_t{i}", [P, 2, T], RB + o + 4 * KB * i, F32R) for i in range(2)]
        ckv_f = sb_at("ckv_f", [P, 2, T], RB + o + 8 * KB)
        ckv_n = sb_at("ckv_n", [P, TB, 256], RB + o + 12 * KB)
        bkv_n = sb_at("bkv_n", [P, TB, 256], RB + o + 16 * KB)
        kb_n = sb_at("kb_n", [P, TB, 2, 2, 64], RB + o + 20 * KB)
        ik_n = sb_at("ik_n", [P, TB, 80], RB + o + 24 * KB)
        ik_d = sb_at("ik_d", [P, TB, 2, 64], RB + o + 26 * KB)
        k_nat = sb_at("k_nat", [P, TB, A_W], RB)
        kt_b = sb_at("kt_b", [P, 2, T], RB + o + 8 * KB)
        mem_vn = sb_at("mem_vn", [P, 2, C_W], Y)
        kt_c = sb_at("kt_c", [P, HEADS_C, MEM], Y + 4 * KB)
        mem_kn = sb_at("mem_kn", [P, 2, C_W], Y + 8 * KB)
        v_nat = sb_at("v_nat", [P, TB, A_W], Y + 12 * KB)
        kt_a = sb_at("kt_a", [P, HEADS_A, T], RB + 12 * KB)
        sq_w = sb_at("sq_w", [P, 1024], RB + o + 28 * KB)
        score = sb_at("score", [P, TB, T], RB)
        qb1 = [sb_at(f"qb1{i}", [P, T], RB + 8 * KB + 2 * KB * i) for i in range(2)]
        kb1 = [sb_at(f"kb1{i}", [P, T], RB + 12 * KB + 2 * KB * i) for i in range(2)]
        vb1 = [sb_at(f"vb1{i}", [P, TB, P], RB + 16 * KB + 2 * KB * i) for i in range(2)]
        gb1 = [sb_at(f"gb1{i}", [P, T], RB + 20 * KB + 2 * KB * i) for i in range(2)]
        bb1 = [sb_at(f"bb1{i}", [P, 2 * ROW_B - P], RB + 24 * KB + 3 * KB * i) for i in range(2)]
        qkvg = [[sb_at(f"qkvg{i}{c}", [P, T], RA + 2 * KB * (4 * i + c)) for c in range(4)] for i in range(2)]
        b2 = [sb_at(f"b2_{i}", [P, 896], RA + 16 * KB + 3584 * i) for i in range(2)]
        nl = [sb_at(f"nl{i}", [P, 8, 64], RA + 24 * KB + 2 * KB * i) for i in range(2)]
        nb = [sb_at(f"nb{i}", [P, 4, 8, 32], RA + 28 * KB + 4 * KB * i) for i in range(2)]
        v_tok = [sb_at(f"v_tok{i}", [P, 8, P], RA + 36 * KB + 4 * KB * i) for i in range(2)]
        v_win = [sb_at(f"v_win{i}", [P, 1024], RA + 48 * KB + 4 * KB * i) for i in range(2)]
        th_2 = sb_at("th_2", [P, 2, T], RA + 44 * KB)
        z = sb_at("z", [P, TB, D], RA)
        ln_g = sb_at("ln_g", [P, D], RA + 32 * KB)
        ln_b = sb_at("ln_b", [P, D], RA + 40 * KB)
        stage = [sb_at(f"stage{i}", [P, 2, T], Y + 4 * KB * i) for i in range(2)]
        prob = sb_at("prob", [P, 4, T], Y + 8 * KB)
        prob_t = [sb_at(f"prob_t{i}", [P, 4, P], Y + 16 * KB + 2 * KB * i) for i in range(2)]
        o_st = [sb_at(f"o_st{i}", [P, T], Y + 20 * KB + 2 * KB * i) for i in range(2)]
        mem_nat = sb_at("mem_nat", [P, 2, D], Y)
        tr_f = [sb_at(f"tr_f{i}", [P, T], Y + 16 * KB + 2 * KB * i) for i in range(2)]
        tr_h = [sb_at(f"tr_h{i}", [P, T], Y + 20 * KB + 2 * KB * i) for i in range(2)]
        sq_q = sb_at("sq_q", [P, 2, T], Y + 8 * KB)
        th_g = sb_at("th_g", [P, 2, T], Y + 12 * KB)
        mixg = sb_at("mixg", [P, 3, 2, T], Y)
        m_acc = sb_at("m_acc", [P, 2, T], Y + 12 * KB)
        m_tmp = sb_at("m_tmp", [P, 2, T], Y + 16 * KB)
        o_ld = [sb_at(f"o_ld{i}", [P, T], Y + 2 * KB * i) for i in range(4)]
        xr = [sb_at(f"xr{i}", [P, 2, T], Y + 8 * KB + 4 * KB * i) for i in range(2)]
        s0 = Y + 24 * KB
        params = sb_at("params_sb", [P, N_PAR], s0)
        con = sb_at("con", [P, N_CON], s0 + 512)
        s1 = s0 + 512 + 4 * N_CON + 64
        s1 = -(-s1 // 64) * 64
        small_at = [s1]

        def small(name, shape):
            n = 4
            for d in shape[1:]:
                n *= d
            t = sb_at(name, shape, small_at[0])
            small_at[0] += -(-n // 32) * 32
            return t

        rbc = sb_at("rbc", [P, T + MEM], W_AT + 40 * KB)
        rdiag = sb_at("rdiag", [P, 6, P], W_AT + 43 * KB)
        pos = sb_at("pos", [33, ROW_A + ROW_B + ROW_2], W_AT + 24 * KB)
        tab1 = small("tab1", [33, 18])
        tab2 = small("tab2", [33, 16])
        ssq = small("ssq", [P, 8])
        rstd = small("rstd", [P, 8])
        ssk = small("ssk", [P, 24])
        rsk = small("rsk", [P, 24])
        stats = small("stats", [P, TB, 6])
        st_z = small("st_z", [P, TB, 48])
        mv = small("mv", [P, TB, 2])
        half_b = small("half_b", [P, 48])
        qgs = small("qgs", [P, 16])
        iw = small("iw", [P, TB * 16])
        ik_t = small("ik_t", [P, T])
        ssq_q = small("ssq_q", [P, 128])
        rq = small("rq", [P, 128])
        mx = small("mx", [P, 4, 2])
        mx2 = small("mx2", [P, 4, 2])
        nmx = small("nmx", [P, 4, 2])
        rs = small("rs", [P, 4, 2])
        es = small("es", [P, 4, 2])
        sd = small("sd", [P, 4, 2])
        den = small("den", [P, 4, 2])
        rden = small("rden", [P, 4, 2])
        top8 = small("top8", [P, 3, 8])
        nmr = small("nmr", [P, TB])
        assert small_at[0] <= nc.sbuf_usable_end, (small_at[0], nc.sbuf_usable_end)

        def pcol(name, i=0, n=1):
            a = PAR[name][0] + i
            return params[:, a:a + n]

        ident = con[:, CON["ident"][0]:CON["ident"][1]]
        ones = con[:, CON["ones"][0]:CON["ones"][1]]
        aident = con[:, CON["aident"][0]:CON["aident"][1]]

        bank = [ctx.enter_context(nc.psum_tensor(f"bank{i}", [P, 512], F32)) for i in range(8)]

        w_loaded = [sem(f"w_loaded{i}") for i in range(2)]
        hi_ready, lo_ready = sem("hi_ready"), sem("lo_ready")
        chunk_used = sem("chunk_used")
        ev_act, ev_dve = sem("ev_act"), sem("ev_dve")
        staged_out = [sem(f"staged_out{i}") for i in range(2)]
        barrier = sem("barrier")
        con_s = sem("con_loaded")
        x_s = [sem(f"x_loaded{i}") for i in range(TB)]
        mem_s = [sem(f"mem_loaded{i}") for i in range(2)]
        sq_s, rs_s = sem("squares"), sem("rstd_chain")
        rt_s = sem("roots")
        rd_s, rb_s, rbc_s = sem("rdiag_ready"), sem("rb_psum"), sem("rbc_ready")
        tr_s, tf_s, th_s, tt_s, tl_s = sem("tr_psum"), sem("tr_copied"), sem("tr_scaled"), sem("tr_hi"), sem("tr_lo")
        xt_out = [sem(f"xt_out{i}") for i in range(2)]
        pb_s, pe_s, brow_out = sem("bias_psum"), sem("bias_copied"), sem("brow_out")
        prep = sem("small_parameters")
        sp_v, sp_h, sp_l = sem("special_chain"), sem("latent_hi"), sem("latent_lo")
        ms_s, rt2_s = sem("mean_squares"), sem("special_roots")
        sp_t, sp_c, sp_o = sem("special_transposed"), sem("special_normed"), sem("special_out")
        kv_psum, kv_act, kv_dve = sem("kv_psum"), sem("kv_act"), sem("kv_dve")
        kst_k, kst_v = sem("k_stored"), sem("v_stored")
        qsq, qssq, qcp, rq_s = sem("q_squares"), sem("q_ssq_psum"), sem("q_ssq_copied"), sem("rq_chain")
        gth = sem("gate_tanh")
        it_loaded = [sem(f"item_loaded{i}") for i in range(2)]
        iq_loaded = [sem(f"iq_loaded{i}") for i in range(2)]
        g2_loaded = [sem(f"gate2_loaded{i}") for i in range(2)]
        b_loaded = [sem(f"bias_loaded{i}") for i in range(2)]
        nb_ready = [sem(f"nbias_ready{i}") for i in range(2)]
        s_ready, l_ready, m_ready = sem("logits_psum"), sem("logits_ready"), sem("max_ready")
        e_ready, p_ready, t_ready = sem("exp_ready"), sem("prob_ready"), sem("prob_t_psum")
        half_done = sem("first_head_done")
        va, vb = sem("max_chain"), sem("scale_chain")
        pt_act, pt_dve = sem("prob_t_act"), sem("prob_t_dve")
        pv_ready, o_ready = sem("pv_psum"), sem("o_ready")
        o_out = [sem(f"o_out{i}") for i in range(2)]
        i_psum, i_rel, i_acc = sem("idx_psum"), sem("idx_relu"), sem("idx_acc")
        topk_s, cz_s, zero_s = sem("topk_chain"), sem("causal_fill"), sem("score_zero")
        vt_psum, vt_ready, vw_ready = sem("v_tok_psum"), sem("v_tok_ready"), sem("v_windows")
        ol_s = [sem(f"o_ld{i}") for i in range(4)]
        oh_s, olo_s = sem("o_hi"), sem("o_lo")
        mg_loaded = sem("mixg_loaded")
        up_psum, up_ev, up_ch, up_hi, up_lo = sem("up_psum"), sem("up_read"), sem("up_chain"), sem("up_hi"), sem("up_lo")
        xr_loaded = [sem(f"xr_loaded{i}") for i in range(2)]
        x1f_s, x1h_s, x1l_s = sem("x1_ready"), sem("x1_hi"), sem("x1_lo")
        x1_out = [sem(f"x1_out{i}") for i in range(2)]
        st_s = sem("stats_ready")
        ln_loaded, ln_s, ln_a, ln_v = sem("ln_loaded"), sem("ln_chain"), sem("ln_norm"), sem("ln_done")
        fin_out = sem("fin_out")

        LATENT_READY = 8
        LN_VAR, LN_NMR = 2, 4

        def meet(eng, n):
            eng.drain().then_inc(barrier, 1)
            eng.wait_ge(barrier, 4 * n)

        def split_hi(act, c, s, first=False):
            act.wait_ge(w_loaded[s], 8 * (c - s) + 16)
            if not first:
                act.wait_ge(chunk_used, c - 1)
            act.activation(w_hi[s][:], w_raw[s][:], ACT.Copy).then_inc(hi_ready, 1)

        def split_lo(dve, c, s):
            dve.wait_ge(hi_ready, c + 1)
            dve.tensor_tensor(w_lo[s][:], w_raw[s][:], w_hi[s][:].bitcast(F32), ALU.subtract).then_inc(lo_ready, 1)

        def chunk_ready(pe, c):
            pe.wait_ge(hi_ready, c + 1)
            pe.wait_ge(lo_ready, c + 1)

        def wt(buf, kt, n0, n, width=GC):
            return buf[:, kt * width + n0:kt * width + n0 + n]

        def mm3(pe, out_ap, l_hi, l_lo, r_hi, r_lo, start, stop):
            pe.matmul(out_ap, l_hi, r_hi, start=start, stop=False)
            pe.matmul(out_ap, l_lo, r_hi, start=False, stop=False)
            return pe.matmul(out_ap, l_hi, r_lo, start=False, stop=stop)

        def rows_t(pe, s, kts, act, banks, first_k=0, last_k=KT - 1):
            for kt in kts:
                for n in range(2):
                    k = CK * s + kt
                    last = mm3(pe, bank[banks[n]][:], wt(w_hi[s], kt, n * P, P), wt(w_lo[s], kt, n * P, P),
                               act[0][:, k, :], act[1][:, k, :], start=(k == first_k), stop=(k == last_k))
            return last

        def group_t(pe, g, act, banks):
            for s in range(2):
                chunk_ready(pe, 2 * g + s)
                rows_t(pe, s, range(CK), act, banks).then_inc(chunk_used, 1)

        def group_rows(pe, g, act, blocks, width, banks, w=GC):
            for s in range(2):
                chunk_ready(pe, 2 * g + s)
                for kt in range(CK):
                    for b in range(blocks):
                        k = CK * s + kt
                        last = mm3(pe, bank[banks[b]][:, 0:width], act[0][:, k, b * P:(b + 1) * P],
                                   act[1][:, k, b * P:(b + 1) * P], wt(w_hi[s], kt, 0, width, w),
                                   wt(w_lo[s], kt, 0, width, w), start=(k == 0), stop=(k == KT - 1))
                last.then_inc(chunk_used, 1)

        def tb_of(k):
            return TB - 1 - k

        def width_of(kind, k):
            return {"A": P * (tb_of(k) + 1), "B": 512, "C": 256, "A2": 512, "N2": 256}[kind]

        def blocks_of(kind, k):
            if kind == "B":
                return [0, 1, 2, 3] if tb_of(k) else [1, 3]
            return list(range(width_of(kind, k) // P))

        def pair_loaded(i):
            return 48 * i + 512

        def outs_before(i, par):
            return 2 * i + (16 + par)

        def vt_count(kind, i, par):
            return 2 * i + (par - 1) if kind == "A2" else 4 * i + (2 * par - 10)

        def windows_ready(i, par):
            return 2 * i + (par - 9)

        def q_rows(i, att, dst, src):
            if att == "N2" or (isinstance(i, int) and i == 4):
                return (dst.rearrange("p (b r c) -> p b r c", b=4, r=8),
                        src.rearrange("p (r b c) -> p b r c", b=4, r=8))
            return dst, src

        def staged_before(i, j):
            return 32 * i + (16 * (j // 2) + 368)

        def bias2_loaded(i, j):
            return 32 * i + (80 + 16 * (j // 2))

        def nb_count(i, j):
            return 2 * i + (j // 2 - 9)

        def gate2_tanh(i):
            return i + 9

        Q_BANK, T_BANK, O_BANK, V_BANK = (2, 3), (4, 5), 6, 7
        BAND0 = lambda k: 0 if tb_of(k) else P

        block = ctx.enter_context(nc.Block())

        @block.sync
        def _(sp):
            sp.dma_start(con[:], con_in).then_inc(con_s, 16)
            sp.dma_start(params[:], par_in).then_inc(con_s, 16)
            sp.dma_start(pos[:], pos_in).then_inc(con_s, 16)
            sp.dma_start(tab1[:], tab1_in).then_inc(con_s, 16)
            sp.dma_start(tab2[:], tab2_in).then_inc(con_s, 16)
            for b in range(TB):
                sp.dma_start(x_nat[:, b, :], x_v[b]).then_inc(x_s[b], 16)
            for b in range(2):
                sp.dma_start(mem_nat[:, b, :], mem_v[b]).then_inc(mem_s[b], 16)
            for s in range(2):
                sp.dma_start(w_raw[s][:], wst[s]).then_inc(w_loaded[s], 16)
            with sp.Fori(1, N_GROUPS) as g:
                for s in range(2):
                    sp.wait_ge(lo_ready, 2 * g + s - 1)
                    sp.dma_start(w_raw[s][:], wst[2 * g + s]).then_inc(w_loaded[s], 16)

        B0, N0 = ROW_A, ROW_A + ROW_B
        BIAS_JOBS = [(tab1[:, 0:6], 0, 512, rows_1a[:, 0:512]), (tab1[:, 0:6], 512, ROW_A, rows_1a[:, 512:ROW_A]),
                     (tab1[:, 6:18:2], B0, N0, rows_1b[:, 0:ROW_B]),
                     (tab1[:, 7:18:2], B0, N0, rows_1b[:, ROW_B:2 * ROW_B]),
                     (tab2[:], N0, N0 + 512, rows_2[:, 0:512]), (tab2[:], N0 + 512, N0 + ROW_2, rows_2[:, 512:ROW_2])]

        @block.tensor
        def _(pe):
            for first, n in ((s_ready, 8), (t_ready, 8), (pv_ready, 2), (i_psum, 3), (qssq, 1)):
                pe.sem_inc(first, n)
            pe.wait_ge(con_s, 80)
            for n, (heads, a, b, dst) in enumerate(BIAS_JOBS):
                pe.matmul(bank[n][0:dst.shape[0], 0:b - a], heads, pos[:, a:b], start=True, stop=True).then_inc(pb_s, 1)
            pe.wait_ge(pe_s, 4)
            for i in range(2 * KT):
                kt, blocks = i % KT, TB if i < KT else 2
                if i >= 4:
                    pe.wait_ge(tf_s, i - 3)
                for b in range(blocks):
                    if i % KT == 0:
                        pe.wait_ge(x_s[b] if i < KT else mem_s[b], 16)
                    src = x_nat if i < KT else mem_nat
                    last = pe.transpose(bank[i % 4][:, b * P:(b + 1) * P], src[:, b, kt * P:(kt + 1) * P], ident)
                last.then_inc(tr_s, 1)
                if i in (3, 12):
                    n, bk, b0 = (TB, 6, 0) if i == 3 else (2, 7, TB)
                    pe.wait_ge(rd_s, 1 + i // 12)
                    for b in range(n):
                        last = pe.matmul(bank[bk][:, b * P:(b + 1) * P], ones, rdiag[:, b0 + b, :], start=True, stop=True)
                    last.then_inc(rb_s, 1)
            meet(pe, 1)

            def wait_read(n):
                pe.wait_ge(ev_act, n)
                pe.wait_ge(ev_dve, n)

            group_rows(pe, G_CKV, act_a, TB, 256, range(4))
            wait_read(1)
            group_rows(pe, G_IK, act_a, TB, 80, range(4), 80)
            wait_read(2)
            group_rows(pe, G_BKV, act_a, TB, 256, range(4))
            pe.wait_ge(sp_c, 1)
            for kt in range(2):
                for b in range(TB):
                    last = pe.transpose(bank[4 + kt][:, b * P:(b + 1) * P], ckv_n[:, b, kt * P:(kt + 1) * P], ident)
            last.then_inc(sp_t, 1)
            pe.wait_ge(sp_c, 2)
            for b in range(TB):
                last = pe.transpose(bank[6][:, b * P:(b + 1) * P], ik_d[:, b, :, :].rearrange("p a c -> p (a c)"), ident)
            last.then_inc(sp_t, 1)
            wait_read(3)
            group_rows(pe, G_MEM, mem_t, 2, 256, (0, 1))
            pe.wait_ge(sp_c, 3)
            pe.wait_ge(sp_o, 1)
            for kv in range(2):
                for b in range(TB):
                    last = pe.transpose(bank[4 + kv][:, b * P:(b + 1) * P],
                                        kb_n[:, b, kv, :, :].rearrange("p a c -> p (a c)"), ident)
            last.then_inc(sp_t, 1)
            group_rows(pe, G_MEM + 1, mem_t, 2, 256, (2, 3))
            wait_read(4)
            group_rows(pe, G_MEM + 2, mem_t, 2, 256, (0, 1))
            wait_read(5)
            group_rows(pe, G_MEM + 3, mem_t, 2, 256, (2, 3))
            pe.wait_ge(sp_c, 4)
            pe.wait_ge(sp_o, 3)
            for h in range(HEADS_C):
                for b in range(2):
                    at = (h % 2) * 256 + b * P
                    last = pe.transpose(bank[4 + h // 2][:, at:at + P], mem_kn[:, b, h * P:(h + 1) * P], ident)
            last.then_inc(sp_t, 1)
            pe.wait_ge(sp_h, 1)
            pe.wait_ge(sp_l, 1)
            wait_read(7)
            for kind in range(2):
                chunk_ready(pe, 2 * G_KVUP + kind)
                for b in range(TB):
                    u = kind * TB + b
                    if u >= 2:
                        pe.wait_ge(kv_act, u - 1)
                        pe.wait_ge(kv_dve, u - 1)
                    for half in range(2):
                        for kt in range(2):
                            last = mm3(pe, bank[2 * (u % 2) + half][:, 0:384], ckv_t[0][:, kt, b * P:(b + 1) * P],
                                       ckv_t[1][:, kt, b * P:(b + 1) * P], wt(w_hi[kind], kt, half * 384, 384, A_W),
                                       wt(w_lo[kind], kt, half * 384, 384, A_W), start=(kt == 0), stop=(kt == 1))
                    last.then_inc(chunk_used if b == TB - 1 else kv_psum, 1)
            pe.wait_ge(sp_c, 5)
            pe.wait_ge(sp_o, 4)
            for b in range(TB):
                if b >= 2:
                    pe.wait_ge(sp_o, 4 + b - 1)
                for h in range(HEADS_A):
                    bk = 4 + 2 * (b % 2) + h // 4
                    last = pe.transpose(bank[bk][:, (h % 4) * P:(h % 4 + 1) * P], k_nat[:, b, h * P:(h + 1) * P], ident)
                last.then_inc(sp_t, 1)
            meet(pe, 2)

            for kind, g0, n in (("iq", G_IQ, 4), ("q", G_Q, 8), ("gate", G_GATE, 8)):
                with pe.Fori(0, n // 2) as i:
                    for s in range(2):
                        g = 2 * i + (g0 + s)
                        wait_read(g - 2)
                        group_t(pe, g, act_a, (2 * s, 2 * s + 1))
                        if kind == "q":
                            pe.wait_ge(ev_act, g)
                            pe.wait_ge(qcp, 2 * i + (s + 1))
                            for n_ in range(2):
                                for b in range(TB):
                                    c = (b * 2 + n_) * 2
                                    hd = con[:, bass.ds(4 * (2 * i) + (CON["heads"][0] + 4 * s + 2 * n_), 2)]
                                    last = pe.matmul(bank[4 + s][:, c:c + 2], sq_q[:, n_, b * P:(b + 1) * P], hd,
                                                     start=True, stop=True)
                            last.then_inc(qssq, 1)
            meet(pe, 3)

            def gemm_part(g, hs, act):
                s, kts = hs // 2, range(4 * (hs % 2), 4 * (hs % 2) + 4)
                if hs % 2 == 0:
                    chunk_ready(pe, 2 * g + s)
                last = rows_t(pe, s, kts, act, (0, 1))
                if hs % 2 == 1:
                    last.then_inc(chunk_used, 1)

            def idx_units(t, e):
                for j in range(3):
                    ui = 6 * t + (3 + 3 * e + j)
                    tb, half = 3 - j, slice(64 * e, 64 * e + 64)
                    pe.wait_ge(i_rel, ui - 2)
                    pe.matmul(bank[2 + j][:, 0:P * (tb + 1)], qb1[par][half, tb * P:(tb + 1) * P],
                              ik_t[half, 0:P * (tb + 1)], start=True, stop=True).then_inc(i_psum, 1)

            with pe.Fori(0, 4) as i:
                for par in range(2):
                    g, t = 2 * i + (G_MIX + par), 2 * i + par
                    for hs in range(4):
                        if hs % 2 == 0:
                            if hs == 0:
                                pe.wait_ge(iq_loaded[par], 16 * i + 16)
                            idx_units(t, hs // 2)
                        if hs == 0:
                            pe.wait_ge(ev_act, g - 1)
                        gemm_part(g, hs, act_a)

            def qk(kind, it, k, q, kk):
                u, tb = 4 * it + k, tb_of(k)
                dst = bank[Q_BANK[k % 2]]
                pe.wait_ge(l_ready, u - 1)
                if kind == "B":
                    for e in range(2):
                        half = slice(64 * e, 64 * e + 64)
                        c0 = BAND0(k)
                        last = pe.matmul(dst[:, 256 * e + c0:256 * e + 256], q[half, tb * P:(tb + 1) * P],
                                         kk[half, (tb - 1) * P + c0:(tb + 1) * P], start=True, stop=True)
                        if e == 0:
                            last.then_inc(half_done, 1)
                            pe.wait_ge(half_done, u - 7)
                    last.then_inc(s_ready, 1)
                else:
                    w = width_of(kind, k)
                    pe.matmul(dst[:, 0:w], q[:, tb * P:(tb + 1) * P], kk[:, 0:w], start=True, stop=True)\
                        .then_inc(s_ready, 1)

            def qk2(kind, it, k, e, q, kk):
                u, half = 4 * it + k, slice(64 * e, 64 * e + 64)
                dst = bank[Q_BANK[k % 2]]
                pe.wait_ge(l_ready, u - 1)
                if kind == "A2":
                    tb = tb_of(k)
                    ins = pe.matmul(dst[:], q[half, tb * P:(tb + 1) * P], kk[half, :], start=True, stop=True)
                else:
                    kv = kk[half, :].rearrange("p (r c) -> p r c", c=64)[:, :, BLK_START[k]:BLK_START[k] + 32]
                    ins = pe.matmul(dst[:, 0:256], q[half, k * P:(k + 1) * P], kv, start=True, stop=True)
                ins.then_inc(s_ready, 1)

            def turn(kind, it, k):
                u = 4 * it + k
                pe.wait_ge(p_ready, u + 1)
                pe.wait_ge(pt_act if k % 2 else pt_dve, 2 * it + k // 2)
                for b in blocks_of(kind, k):
                    last = pe.transpose(bank[T_BANK[k % 2]][:, b * P:(b + 1) * P], prob[:, k, b * P:(b + 1) * P], ident)
                last.then_inc(t_ready, 1)

            def pv(kind, it, k, e=0, v=None):
                tb = tb_of(k)
                pe.wait_ge(pt_act if k % 2 else pt_dve, 2 * it + k // 2 + 1)
                if k == 0 and kind in ("A", "B", "C"):
                    pe.wait_ge(o_ready, it)
                pt = prob_t[k % 2]
                if kind == "B":
                    for e_ in range(2):
                        bs = [b for b in blocks_of(kind, k) if b // 2 == e_]
                        for b in bs:
                            last = pe.matmul(bank[O_BANK][64 * e_:64 * e_ + 64, tb * P:(tb + 1) * P],
                                             v[:, tb - 1 + b % 2, 64:128], pt[:, b, :], start=(b == bs[0]), stop=(b == bs[-1]))
                elif kind in ("A", "C"):
                    bs = blocks_of(kind, k)
                    for b in bs:
                        last = pe.matmul(bank[O_BANK][:, tb * P:(tb + 1) * P], v[:, b, :], pt[:, b, :],
                                         start=(b == 0), stop=(b == bs[-1]))
                else:
                    bs = blocks_of(kind, k)
                    c = tb if kind == "A2" else k
                    for b in bs:
                        vb = b if kind == "A2" else 2 * k + b
                        last = pe.matmul(bank[O_BANK][64 * e:64 * e + 64, c * P:(c + 1) * P],
                                         v[:, vb, 64 * e:64 * e + 64], pt[:, b, :], start=(b == 0), stop=(b == bs[-1]))
                if k == 3:
                    last.then_inc(pv_ready, 1)

            def att1_part(kind, it, hs, par):
                q, kk, v = qb1[par], kb1[par], vb1[par]
                if hs == 0:
                    qk(kind, it, 0, q, kk)
                    qk(kind, it, 1, q, kk)
                elif hs == 1:
                    qk(kind, it, 2, q, kk)
                    qk(kind, it, 3, q, kk)
                    turn(kind, it, 0)
                    turn(kind, it, 1)
                elif hs == 2:
                    pv(kind, it, 0, 0, v)
                    pv(kind, it, 1, 0, v)
                    turn(kind, it, 2)
                    turn(kind, it, 3)
                else:
                    pv(kind, it, 2, 0, v)
                    pv(kind, it, 3, 0, v)

            pe.wait_ge(i_rel, 51)
            for kind, it0, n in (("B", 2, ITEMS_B), ("C", 8, ITEMS_C), ("A", 12, ITEMS_A)):
                with pe.Fori(0, n // 2) as i:
                    for par in range(2):
                        it = 2 * i + (it0 + par)
                        g = 2 * i + (G_MIX + 8 + it0 - 2 + par)
                        pe.wait_ge(it_loaded[par], 64 * i + 32 * it0)
                        for hs in range(4):
                            att1_part(kind, it, hs, par)
                            if hs == 0:
                                pe.wait_ge(ev_act, g - 1)
                            gemm_part(g, hs, act_a)
            meet(pe, 4)

            UP = ((0, 6, (0, 1)), (6, 10, (2, 3)), (10, 16, (4, 5)))
            pe.wait_ge(oh_s, KT)
            pe.wait_ge(olo_s, KT)
            with pe.Fori(0, 8) as j:
                for s in range(2):
                    chunk_ready(pe, 2 * j + (2 * G_UP + s))
                    for kt in range(CK):
                        k = CK * s + kt
                        c = 0 if k < 6 else 1 if k < 10 else 2
                        k0, k1, bk = UP[c]
                        if k == k0:
                            pe.wait_ge(up_ev, 3 * j + c + 1)
                        last = rows_t(pe, s, [kt], act_b, bk, k0, k1 - 1)
                        if k == k1 - 1 and c < 2:
                            last.then_inc(up_psum, 1)
                        if k == CK - 1:
                            last.then_inc(chunk_used, 1)
                    if s == 1:
                        last.then_inc(chunk_used, 1)
            meet(pe, 5)

            with pe.Fori(0, 4) as i:
                for s in range(2):
                    g = 2 * i + (G_WO + s)
                    pe.wait_ge(x1f_s, 4 * i + (2 * s + 2))
                    group_t(pe, g, act_a, (2 * s, 2 * s + 1))
            meet(pe, 6)

            def v_turn(kind, v, v_w, part):
                for x in range(4):
                    if kind == "A2":
                        src = v[:, x * P:(x + 1) * P]
                    else:
                        src = v_w[:, (4 * part + x) * P:(4 * part + x + 1) * P]
                    last = pe.transpose(bank[V_BANK][:, x * P:(x + 1) * P], src, ident)
                last.then_inc(vt_psum, 1)

            def att2_part(kind, i, it, hs, par, e):
                q, kk, v = qkvg[par][0], qkvg[par][1], v_tok[par]
                if hs == 0:
                    if e == 0:
                        pe.wait_ge(it_loaded[par], pair_loaded(i))
                        pe.wait_ge(vt_ready, vt_count(kind, i, par))
                    qk2(kind, it, 0, e, q, kk)
                    qk2(kind, it, 1, e, q, kk)
                elif hs == 1:
                    qk2(kind, it, 2, e, q, kk)
                    qk2(kind, it, 3, e, q, kk)
                    turn(kind, it, 0)
                    turn(kind, it, 1)
                elif hs == 2:
                    if e == 0:
                        pe.wait_ge(o_ready, outs_before(i, par))
                    pv(kind, it, 0, e, v)
                    pv(kind, it, 1, e, v)
                    turn(kind, it, 2)
                    turn(kind, it, 3)
                else:
                    pv(kind, it, 2, e, v)
                    pv(kind, it, 3, e, v)

            def quad(i, att, vt_next, gemm=True):
                for j in range(4):
                    par, e = j // 2, j % 2
                    nxt = (att, i, 1) if j == 1 and att else (vt_next, i + 1, 0) if j == 3 and vt_next else None
                    for hs in range(4):
                        if att:
                            att2_part(att, i, 4 * i + (14 + j), hs, par, e)
                        if nxt and (hs == 3 or (hs == 2 and nxt[0] == "N2")):
                            kind_n, i_n, par_n = nxt
                            if kind_n == "N2" and hs == 3:
                                pe.wait_ge(vt_ready, vt_count(kind_n, i_n, par_n) - 1)
                            elif kind_n == "N2":
                                pe.wait_ge(vw_ready, windows_ready(i_n, par_n))
                            else:
                                pe.wait_ge(it_loaded[par_n], pair_loaded(i_n))
                            v_turn(kind_n, qkvg[par_n][2], v_win[par_n], hs - 2 if kind_n == "N2" else 0)
                        if gemm:
                            g = 4 * i + (G_IN2 + j)
                            if hs == 0:
                                pe.wait_ge(ev_act, g - 17)
                                pe.wait_ge(ev_dve, g - 41)
                            gemm_part(g, hs, act_b)

            quad(0, None, "A2")
            with pe.Fori(1, 4) as i:
                quad(i, "A2", "A2")
            quad(4, "A2", "N2")
            with pe.Fori(5, 8) as i:
                quad(i, "N2", "N2")
            quad(8, "N2", None, gemm=False)
            meet(pe, 7)

            pe.wait_ge(oh_s, 2 * KT)
            pe.wait_ge(olo_s, 2 * KT)
            with pe.Fori(0, 4) as i:
                for s in range(2):
                    g = 2 * i + (G_OUT2 + s)
                    pe.wait_ge(ev_act, g - 18)
                    pe.wait_ge(ev_dve, g - 42)
                    pe.wait_ge(xr_loaded[s], 16 * i + 80)
                    for b in range(TB):
                        for n in range(2):
                            pe.matmul(bank[4 * s + b][:, n * P:(n + 1) * P], xr[s][:, n, b * P:(b + 1) * P], aident,
                                      start=(n == 0), stop=False, skip_group_check=True)
                    for c in range(2):
                        chunk_ready(pe, 2 * g + c)
                        for kt in range(CK):
                            k = CK * c + kt
                            for b in range(TB):
                                dst = bank[4 * s + b][:, 0:GC]
                                for l, r in ((0, w_hi), (1, w_hi), (0, w_lo)):
                                    last = pe.matmul(dst, act_b[l][:, k, b * P:(b + 1) * P], wt(r[c], kt, 0, GC),
                                                     start=False, stop=(k == KT - 1), skip_group_check=True)
                        last.then_inc(chunk_used, 1)
            meet(pe, 8)


        @block.scalar
        def _(act):
            for first, n in ((e_ready, 8), (pt_act, 4), (i_rel, 3), (x1h_s, 2)):
                act.sem_inc(first, n)

            def copy(dst, src, **kw):
                return act.activation(dst, src, ACT.Copy, **kw)

            def squares(src, b, c):
                if c:
                    act.wait_ge(sq_s, c)
                act.activation(junk[:], src[:, b, :], ACT.Square, accum_out=ssq[:, c:c + 1]).then_inc(sq_s, 1)

            for b in range(TB):
                act.wait_ge(x_s[b], 16)
                squares(x_nat, b, b)
            act.wait_ge(rs_s, 1)
            act.activation(ssq[:, 0:TB], rstd[:, 0:TB], ACT.Sqrt).then_inc(rt_s, 1)

            def tr_copy(i):
                w = T if i < KT else MEM
                act.wait_ge(tr_s, i + 1)
                if i >= 2:
                    act.wait_ge(th_s, i - 1)
                    act.wait_ge(xt_out[i % 2], 16 * min(i // 2, KT // 2))
                copy(tr_f[i % 2][:, 0:w], bank[i % 4][:, 0:w]).then_inc(tf_s, 1)

            def tr_hi(i):
                act.wait_ge(th_s, i + 1)
                if i < KT:
                    copy(act_a[0][:, i, :], tr_h[i % 2][:]).then_inc(tt_s, 1)
                else:
                    copy(mem_t[0][:, i - KT, :], tr_h[i % 2][:, 0:MEM]).then_inc(tt_s, 1)

            tr_copy(0)
            for i in range(2 * KT):
                if i == 8:
                    for b in range(2):
                        act.wait_ge(mem_s[b], 16)
                        squares(mem_nat, b, TB + b)
                    act.wait_ge(rs_s, 3)
                    act.activation(ssq[:, TB:TB + 2], rstd[:, TB:TB + 2], ACT.Sqrt).then_inc(rt_s, 1)
                if i + 1 < 2 * KT:
                    tr_copy(i + 1)
                tr_hi(i)
            split_hi(act, 0, 0, first=True)
            meet(act, 1)

            def hi2(g, first=False):
                split_hi(act, 2 * g + 1, 1, first=first)
                split_hi(act, 2 * g + 2, 0)

            def summed(g):
                act.wait_ge(chunk_used, 2 * g + 2)

            def root(n, width):
                act.wait_ge(ms_s, n)
                act.activation(ssk[:, 0:width], rsk[:, 0:width], ACT.Sqrt).then_inc(rt2_s, 1)

            def upper(g, dst, w):
                summed(g)
                copy(dst[:, 2, 0:w], bank[2][:, 0:w])
                copy(dst[:, 3, 0:w], bank[3][:, 0:w]).then_inc(ev_act, 1)

            hi2(G_CKV, first=True)
            upper(G_CKV, ckv_n, 256)
            root(1, 4)
            hi2(G_IK)
            upper(G_IK, ik_n, 80)
            root(2, 4)
            hi2(G_BKV)
            upper(G_BKV, bkv_n, 256)
            act.wait_ge(sp_v, LATENT_READY)
            copy(ckv_t[0][:], ckv_f[:]).then_inc(sp_h, 1)
            root(3, 8)
            for m in range(4):
                g = G_MEM + m
                hi2(g)
                summed(g)
                dst = mem_kn if m < 2 else mem_vn
                copy(dst[:, 1, 256 * (m % 2):256 * (m % 2) + 256], bank[2 * (m % 2) + 1][:, 0:256]).then_inc(ev_act, 1)
                if m == 1:
                    root(4, 8)
            split_hi(act, 2 * G_KVUP + 1, 1)
            for u in range(2 * TB):
                kind, b = u // TB, u % TB
                if b < TB - 1:
                    act.wait_ge(kv_psum, 3 * kind + b + 1)
                else:
                    act.wait_ge(chunk_used, 2 * G_KVUP + kind + 1)
                copy((v_nat if kind else k_nat)[:, b, 384:768], bank[2 * (u % 2) + 1][:, 0:384]).then_inc(kv_act, 1)
            split_hi(act, 2 * G_KVUP + 2, 0)
            root(5, 24)
            meet(act, 2)

            for kind, g0, n in (("iq", G_IQ, 4), ("q", G_Q, 8), ("gate", G_GATE, 8)):
                with act.Fori(0, n // 2) as i:
                    for s in range(2):
                        g = 2 * i + (g0 + s)
                        hi2(g)
                        b0, b1 = bank[2 * s], bank[2 * s + 1]
                        summed(g)
                        if kind == "iq":
                            act.wait_ge(staged_out[s], 16 * i + (8 * g0 - 48))
                            copy(stage[s][:, 0, :], b0[:]).then_inc(ev_act, 1)
                        elif kind == "q":
                            act.wait_ge(qssq, 2 * i + (s + 1))
                            act.activation(sq_q[:, 0, :], b0[:], ACT.Square).then_inc(qsq, 1)
                            act.activation(sq_q[:, 1, :], b1[:], ACT.Square).then_inc(ev_act, 1)
                        else:
                            act.wait_ge(ev_dve, g - 1)
                            act.activation(th_g[:, 0, :], b0[:], ACT.Tanh, scale=0.5).then_inc(gth, 1)
                            act.activation(th_g[:, 1, :], b1[:], ACT.Tanh, scale=0.5).then_inc(ev_act, 1)
            act.wait_ge(rq_s, 1)
            act.activation(ssq_q[:], rq[:], ACT.Sqrt).then_inc(rt_s, 1)
            meet(act, 3)

            def mix_out(g, i, par, t0):
                summed(g)
                act.wait_ge(staged_out[par], 8 * (g - par) - 48)
                for n in range(2):
                    last = act.activation(stage[par][:, n, :], bank[n][:], ACT.Tanh, scale=0.5,
                                          bias=half_b[:, bass.ds(4 * i + (2 * t0 + 2 * par + n), 1)])
                last.then_inc(ev_act, 1)

            with act.Fori(0, 4) as i:
                for par in range(2):
                    g, t = 2 * i + (G_MIX + par), 2 * i + par
                    for e in range(2):
                        for j in range(3):
                            ui = 6 * t + (3 + 3 * e + j)
                            w = P * (4 - j)
                            act.wait_ge(i_psum, ui + 1)
                            act.wait_ge(i_acc, ui - 2)
                            act.activation(prob[:, j, 0:w], bank[2 + j][:, 0:w], ACT.Relu).then_inc(i_rel, 1)
                        split_hi(act, 2 * g + (1 + e), 1 - e)
                    mix_out(g, i, par, 0)

            def exp(kind, it, k):
                u = 4 * it + k
                act.wait_ge(m_ready, u + 1)
                if kind == "B":
                    for e in range(2):
                        c0 = 256 * e + BAND0(k)
                        act.activation(prob[:, k, c0:256 * e + 256], prob[:, k, c0:256 * e + 256], ACT.Exp,
                                       bias=nmx[:, k, e:e + 1], accum_out=rs[:, k, e:e + 1])
                    act.activation(es[:, k, :], sd[:, k, :], ACT.Exp).then_inc(e_ready, 1)
                else:
                    w = width_of(kind, k)
                    act.activation(prob[:, k, 0:w], prob[:, k, 0:w], ACT.Exp, bias=nmx[:, k, 0:1],
                                   accum_out=rs[:, k, 0:1]).then_inc(e_ready, 1)

            def turned_act(kind, it, k):
                act.wait_ge(t_ready, 4 * it + k + 1)
                if kind == "B" and not tb_of(k):
                    for b in (1, 3):
                        last = copy(prob_t[1][:, b, :], bank[T_BANK[1]][:, b * P:(b + 1) * P])
                else:
                    n = len(blocks_of(kind, k))
                    last = copy(prob_t[1][:, 0:n, :], bank[T_BANK[1]][:, 0:n * P].rearrange("p (a b) -> p a b", b=P))
                last.then_inc(pt_act, 1)

            def att_act(kind, it, hs):
                if hs == 0:
                    exp(kind, it, 0)
                    exp(kind, it, 1)
                elif hs == 1:
                    exp(kind, it, 2)
                    exp(kind, it, 3)
                    turned_act(kind, it, 1)
                elif hs == 2:
                    turned_act(kind, it, 3)

            for kind, it0, n in (("B", 2, ITEMS_B), ("C", 8, ITEMS_C), ("A", 12, ITEMS_A)):
                with act.Fori(0, n // 2) as i:
                    for par in range(2):
                        it = 2 * i + (it0 + par)
                        g = 2 * i + (G_MIX + 6 + it0 + par)
                        for hs in range(4):
                            att_act(kind, it, hs)
                            if hs == 0:
                                split_hi(act, 2 * g + 1, 1)
                            elif hs == 2:
                                split_hi(act, 2 * g + 2, 0)
                        mix_out(g, i, par, 6 + it0)
            meet(act, 4)

            def tiles_hi(n0):
                for n in range(KT):
                    act.wait_ge(ol_s[n % 4], 64 * (n0 // KT) + 16 * (n // 4 + 1))
                    copy(act_b[0][:, n, :], o_ld[n % 4][:]).then_inc(oh_s, 1)

            tiles_hi(0)
            with act.Fori(0, 8) as j:
                g = j + G_UP
                hi2(g)
                act.wait_ge(up_ch, 5 * j + 5)
                copy(act_a[0][:, bass.ds(2 * j, 2), :], m_acc[:], scale=0.5).then_inc(up_hi, 1)
            meet(act, 5)

            with act.Fori(0, 4) as i:
                for s in range(2):
                    g = 2 * i + (G_WO + s)
                    hi2(g)
                    act.wait_ge(x1f_s, 4 * i + (2 * s + 6))
                    copy(act_b[0][:, bass.ds(4 * i + 2 * s, 2), :], stage[s][:]).then_inc(x1h_s, 1)
            meet(act, 6)

            def proj2_out(g, i, j, att):
                s = j % 2
                summed(g)
                if j < 3:
                    act.wait_ge(staged_out[s], staged_before(i, j))
                    dst, src = stage[s][:, 0, :], bank[0][:]
                    if j == 0:
                        dst, src = q_rows(i, att, dst, src)
                    copy(dst, src, scale=HD2 ** -0.5 if j == 0 else 1.0).then_inc(ev_act, 1)
                else:
                    act.activation(th_2[:, 0, :], bank[0][:], ACT.Tanh, scale=0.5).then_inc(gth, 1)
                    act.activation(th_2[:, 1, :], bank[1][:], ACT.Tanh, scale=0.5).then_inc(ev_act, 1)

            def v_turned(kind_n, i_n, par_n, part):
                act.wait_ge(vt_psum, vt_count(kind_n, i_n, par_n) - (1 - part if kind_n == "N2" else 0))
                copy(v_tok[par_n][:, 4 * part:4 * part + 4, :],
                     bank[V_BANK][:].rearrange("p (a b) -> p a b", b=P)).then_inc(vt_ready, 1)

            def quad(i, att, vt_next, gemm=True):
                for j in range(4):
                    g = 4 * i + (G_IN2 + j)
                    nxt = (att, i, 1) if j == 1 and att else (vt_next, i + 1, 0) if j == 3 and vt_next else None
                    for hs in range(4):
                        if att:
                            att_act(att, 4 * i + (14 + j), hs)
                        if nxt and nxt[0] == "N2" and hs >= 2:
                            v_turned(*nxt, hs - 2)
                        elif nxt and hs == 3:
                            v_turned(*nxt, 0)
                        if gemm and hs == 0:
                            split_hi(act, 2 * g + 1, 1)
                        elif gemm and hs == 2:
                            split_hi(act, 2 * g + 2, 0)
                    if gemm:
                        proj2_out(g, i, j, att)

            quad(0, None, "A2")
            with act.Fori(1, 4) as i:
                quad(i, "A2", "A2")
            quad(4, "A2", "N2")
            with act.Fori(5, 8) as i:
                quad(i, "N2", "N2")
            quad(8, "N2", None, gemm=False)
            meet(act, 7)

            tiles_hi(KT)

            def rows_out(i, s, last_group=False):
                g = 2 * i + (G_OUT2 + s)
                split_hi(act, 2 * g + 1, 1)
                if not last_group:
                    split_hi(act, 2 * g + 2, 0)
                summed(g)
                for b in range(2):
                    last = copy(z[:, b, bass.ds(512 * i + 256 * s, 256)], bank[4 * s + b][:, 0:GC])
                last.then_inc(ev_act, 1)

            with act.Fori(0, 3) as i:
                for s in range(2):
                    rows_out(i, s)
            rows_out(3, 0)
            rows_out(3, 1, last_group=True)
            act.wait_ge(ln_s, LN_VAR)
            act.activation(ssk[:, 0:TB], rsk[:, 0:TB], ACT.Sqrt).then_inc(rt2_s, 1)
            for b in range(TB):
                act.wait_ge(ln_s, LN_NMR)
                act.activation(z[:, b, :], z[:, b, :], ACT.Identity, scale=rsk[:, b:b + 1],
                               bias=nmr[:, b:b + 1]).then_inc(ln_a, 1)
            meet(act, 8)

        @block.vector
        def _(dve):
            for first, n in ((l_ready, 8), (m_ready, 8), (p_ready, 8), (pt_dve, 4), (o_ready, 2), (i_acc, 3),
                             (up_ev, 3), (up_lo, 1), (x1f_s, 4), (qcp, 2)):
                dve.sem_inc(first, n)

            def scaled(dst, src, by):
                return dve.tensor_scalar(dst, src, by, None, ALU.mult)

            for n, (heads, a, b, dst) in enumerate(BIAS_JOBS):
                dve.wait_ge(pb_s, n + 1)
                dve.tensor_copy(dst, bank[n][0:dst.shape[0], 0:b - a]).then_inc(pe_s, 1)
            dve.wait_ge(con_s, 80)
            scaled(half_b[:], pcol("gate_b", 0, 48), 0.5)
            scaled(qgs[:, 0:6], pcol("q_g", 0, 6), 64 ** -0.5)
            scaled(qgs[:, 6:16], pcol("q_g", 6, 10), 128 ** -0.5)

            def token_rstd(c0, n, base, squares):
                dve.wait_ge(sq_s, squares)
                dve.tensor_scalar(rstd[:, c0:c0 + n], ssq[:, c0:c0 + n], 1.0 / D, EPS, ALU.mult, ALU.add).then_inc(rs_s, 1)
                dve.wait_ge(rt_s, base // 2 + 1)
                dve.reciprocal(rstd[:, c0:c0 + n], ssq[:, c0:c0 + n]).then_inc(rs_s, 1)
                dve.wait_ge(rs_s, base + 2)
                for b in range(n):
                    last = scaled(rdiag[:, c0 + b, :], ident, rstd[:, c0 + b:c0 + b + 1])
                last.then_inc(rd_s, 1)

            token_rstd(0, TB, 0, TB)
            dve.wait_ge(rb_s, 1)
            dve.tensor_copy(rbc[:, 0:T], bank[6][:]).then_inc(rbc_s, 1)

            def tr_scale(i):
                w, r0 = (T, 0) if i < KT else (MEM, T)
                gain = pcol("norm_g", i) if i < KT else pcol("mem_g", i - KT)
                dve.wait_ge(tf_s, i + 1)
                dve.wait_ge(rbc_s, 1 if i < KT else 2)
                if i >= 2:
                    dve.wait_ge(tt_s, i - 1)
                    dve.wait_ge(tl_s, i - 1)
                dve.scalar_tensor_tensor(out=tr_h[i % 2][:, 0:w], in0=tr_f[i % 2][:, 0:w], scalar=gain,
                                         in1=rbc[:, r0:r0 + w], op0=ALU.mult, op1=ALU.mult).then_inc(th_s, 1)

            def tr_lo(i):
                dve.wait_ge(tt_s, i + 1)
                hi, lo, w = (act_a[0][:, i, :], act_a[1][:, i, :], T) if i < KT else \
                    (mem_t[0][:, i - KT, :], mem_t[1][:, i - KT, :], MEM)
                dve.tensor_tensor(lo, tr_h[i % 2][:, 0:w], hi.bitcast(F32), ALU.subtract).then_inc(tl_s, 1)

            tr_scale(0)
            for i in range(2 * KT):
                if i == 8:
                    token_rstd(TB, 2, 2, TB + 2)
                if i == 15:
                    dve.wait_ge(rb_s, 2)
                    dve.tensor_copy(rbc[:, T:T + MEM], bank[7][:, 0:MEM]).then_inc(rbc_s, 1)
                if i + 1 < 2 * KT:
                    tr_scale(i + 1)
                if i == KT:
                    dve.wait_ge(brow_out, 64)
                tr_lo(i)
            split_lo(dve, 0, 0)
            meet(dve, 1)

            n_sp = [0]

            def link(ins):
                n_sp[0] += 1
                ins.then_inc(sp_v, 1)
                dve.wait_ge(sp_v, n_sp[0])

            def lo2(g):
                split_lo(dve, 2 * g + 1, 1)
                split_lo(dve, 2 * g + 2, 0)

            def summed(g):
                dve.wait_ge(chunk_used, 2 * g + 2)

            def lower(g, dst, w):
                summed(g)
                dve.tensor_copy(dst[:, 0, 0:w], bank[0][:, 0:w])
                dve.tensor_copy(dst[:, 1, 0:w], bank[1][:, 0:w]).then_inc(ev_dve, 1)

            def both_read(n):
                dve.wait_ge(ev_dve, n)
                dve.wait_ge(ev_act, n)

            def inv_root(n, width, count):
                dve.tensor_scalar(rsk[:, 0:width], ssk[:, 0:width], 1.0 / count, EPS, ALU.mult, ALU.add).then_inc(ms_s, 1)
                dve.wait_ge(rt2_s, n)
                link(dve.reciprocal(rsk[:, 0:width], ssk[:, 0:width]))

            def sum_sq(src, heads, dim, c0=0):
                sq = sq_w[:, 0:heads * dim].rearrange("p (h d) -> p h d", d=dim)
                link(dve.tensor_tensor(sq, src, src, ALU.mult))
                link(dve.tensor_reduce(ssk[:, c0:c0 + heads], sq, AX.X, ALU.add))

            lo2(G_CKV)
            lower(G_CKV, ckv_n, 256)
            both_read(1)
            sum_sq(ckv_n[:], TB, 256)
            inv_root(1, TB, KV_RANK)
            for b in range(TB):
                last = scaled(ckv_n[:, b, :], ckv_n[:, b, :], rsk[:, b:b + 1])
            last.then_inc(sp_c, 1)

            lo2(G_IK)
            lower(G_IK, ik_n, 80)
            both_read(2)
            for b in range(TB):
                last = dve.bn_stats(stats[:, b, :], ik_n[:, b, 0:64])
            link(last)
            for b in range(TB):
                last = dve.bn_aggr(mv[:, b, :], stats[:, b, :])
            link(last)
            link(dve.tensor_copy(ssk[:, 0:TB], mv[:, :, 1]))
            inv_root(2, TB, 1)
            for b in range(TB):
                scaled(iw[:, 16 * b:16 * b + 16], ik_n[:, b, 64:80], (IDX_HEADS * IDX_DIM) ** -0.5)
                for e in range(2):
                    last = dve.tensor_scalar(ik_d[:, b, e, :], ik_n[:, b, 0:64], mv[:, b, 0:1], rsk[:, b:b + 1],
                                             ALU.subtract, ALU.mult)
            last.then_inc(sp_c, 1)

            lo2(G_BKV)
            lower(G_BKV, bkv_n, 256)
            dve.wait_ge(sp_t, 1)
            for kt in range(2):
                last = scaled(ckv_f[:, kt, :], bank[4 + kt][:], pcol("kv_g", kt))
            last.then_inc(sp_o, 1)
            dve.wait_ge(sp_o, 1)
            link(dve.memset(nmr[:], 0.0))
            assert n_sp[0] == LATENT_READY, n_sp
            dve.wait_ge(sp_h, 1)
            dve.tensor_tensor(ckv_t[1][:], ckv_f[:], ckv_t[0][:].bitcast(F32), ALU.subtract).then_inc(sp_l, 1)
            both_read(3)
            sq = sq_w[:, 0:512].rearrange("p (b c) -> p b c", c=128)
            link(dve.tensor_tensor(sq, bkv_n[:, :, 0:128], bkv_n[:, :, 0:128], ALU.mult))
            link(dve.tensor_reduce(ssk[:, 0:8], sq_w[:, 0:512].rearrange("p (h d) -> p h d", d=64), AX.X, ALU.add))
            inv_root(3, 8, 64)
            for b in range(TB):
                for kv in range(2):
                    for e in range(2):
                        last = scaled(kb_n[:, b, kv, e, :], bkv_n[:, b, 64 * kv:64 * kv + 64], rsk[:, 2 * b + kv:2 * b + kv + 1])
            last.then_inc(sp_c, 1)
            dve.wait_ge(sp_t, 2)
            dve.tensor_scalar(ik_t[:], bank[6][:], pcol("ik_g"), pcol("ik_b"), ALU.mult, ALU.add).then_inc(sp_o, 1)

            for m in range(4):
                g = G_MEM + m
                lo2(g)
                if m == 1:
                    dve.wait_ge(sp_t, 3)
                    dve.wait_ge(sp_l, 1)
                    for kv in range(2):
                        last = scaled(kt_b[:, kv, :], bank[4 + kv][:], pcol("k_b"))
                    last.then_inc(sp_o, 1)
                summed(g)
                dst = mem_kn if m < 2 else mem_vn
                dve.tensor_copy(dst[:, 0, 256 * (m % 2):256 * (m % 2) + 256], bank[2 * (m % 2)][:, 0:256]).then_inc(ev_dve, 1)
                if m == 1:
                    both_read(5)
                    sum_sq(mem_kn[:].rearrange("p b (h d) -> p (b h) d", d=P), 8, P)
                    inv_root(4, 8, P)
                    for b in range(2):
                        for h in range(HEADS_C):
                            c = mem_kn[:, b, h * P:(h + 1) * P]
                            last = scaled(c, c, rsk[:, 4 * b + h:4 * b + h + 1])
                    last.then_inc(sp_c, 1)
            split_lo(dve, 2 * G_KVUP + 1, 1)
            dve.wait_ge(sp_t, 4)
            for n in range(2):
                last = scaled(kt_c[:, 2 * n:2 * n + 2, :], bank[4 + n][:].rearrange("p (h t) -> p h t", t=MEM), pcol("k_c"))
            last.then_inc(sp_o, 1)
            for u in range(2 * TB):
                kind, b = u // TB, u % TB
                if b < TB - 1:
                    dve.wait_ge(kv_psum, 3 * kind + b + 1)
                else:
                    dve.wait_ge(chunk_used, 2 * G_KVUP + kind + 1)
                dve.tensor_copy((v_nat if kind else k_nat)[:, b, 0:384], bank[2 * (u % 2)][:, 0:384]).then_inc(kv_dve, 1)
            split_lo(dve, 2 * G_KVUP + 2, 0)
            dve.wait_ge(kv_act, TB)
            dve.wait_ge(kv_dve, TB)
            for b in range(TB):
                sum_sq(k_nat[:, b, :].rearrange("p (h d) -> p h d", d=P), HEADS_A, P, HEADS_A * b)
            inv_root(5, 24, P)
            for b in range(TB):
                for h in range(HEADS_A):
                    c = k_nat[:, b, h * P:(h + 1) * P]
                    last = scaled(c, c, rsk[:, 6 * b + h:6 * b + h + 1])
            last.then_inc(sp_c, 1)
            for b in range(TB):
                dve.wait_ge(sp_t, 5 + b)
                bk = 4 + 2 * (b % 2)
                cols = slice(b * P, (b + 1) * P)
                scaled(kt_a[:, 0:4, cols], bank[bk][:].rearrange("p (h t) -> p h t", t=P), pcol("k_a"))
                scaled(kt_a[:, 4:6, cols], bank[bk + 1][:, 0:256].rearrange("p (h t) -> p h t", t=P), pcol("k_a"))\
                    .then_inc(sp_o, 1)
            meet(dve, 2)

            dve.memset(score[:], 0.0).then_inc(zero_s, 1)
            for kind, g0, n in (("iq", G_IQ, 4), ("q", G_Q, 8), ("gate", G_GATE, 8)):
                with dve.Fori(0, n // 2) as i:
                    for s in range(2):
                        g = 2 * i + (g0 + s)
                        lo2(g)
                        summed(g)
                        dve.wait_ge(staged_out[s], 16 * i + (8 * g0 - 48))
                        b0, b1 = bank[2 * s], bank[2 * s + 1]
                        if kind == "iq":
                            dve.tensor_copy(stage[s][:, 1, :], b1[:]).then_inc(ev_dve, 1)
                        elif kind == "q":
                            dve.wait_ge(qsq, 2 * i + (s + 1))
                            scaled(stage[s][:, 0, :], b0[:], qgs[:, bass.ds(4 * i + 2 * s, 1)])
                            dve.wait_ge(ev_act, g)
                            scaled(stage[s][:, 1, :], b1[:], qgs[:, bass.ds(4 * i + (2 * s + 1), 1)]).then_inc(ev_dve, 1)
                            dve.wait_ge(qssq, 2 * i + (s + 2))
                            dve.tensor_copy(ssq_q[:, bass.ds(32 * i + 16 * s, 16)], bank[4 + s][:, 0:16]).then_inc(qcp, 1)
                        else:
                            for n_, (sm, v) in enumerate(((gth, 2 * i + (s + 1)), (ev_act, g))):
                                dve.wait_ge(sm, v)
                                last = dve.scalar_tensor_tensor(out=stage[s][:, n_, :], in0=th_g[:, n_, :], scalar=1.0,
                                                                in1=(b0, b1)[n_][:], op0=ALU.add, op1=ALU.mult)
                            last.then_inc(ev_dve, 1)
            dve.wait_ge(qcp, 10)
            dve.tensor_scalar(rq[:, 0:48], ssq_q[:, 0:48], 1.0 / 64, EPS, ALU.mult, ALU.add)
            dve.tensor_scalar(rq[:, 48:128], ssq_q[:, 48:128], 1.0 / 128, EPS, ALU.mult, ALU.add).then_inc(rq_s, 1)
            dve.wait_ge(rt_s, 3)
            dve.reciprocal(rq[:], ssq_q[:]).then_inc(rq_s, 1)
            meet(dve, 3)

            dve.wait_ge(zero_s, 1)
            with dve.Fori(0, 4) as i:
                for par in range(2):
                    g, t = 2 * i + (G_MIX + par), 2 * i + par
                    for e in range(2):
                        for j in range(3):
                            ui, tb = 6 * t + (3 + 3 * e + j), 3 - j
                            w = P * (tb + 1)
                            dve.wait_ge(i_rel, ui + 1)
                            dve.wait_ge(i_acc, ui - 2)
                            dve.scalar_tensor_tensor(out=score[:, tb, 0:w], in0=prob[:, j, 0:w],
                                                     scalar=iw[:, bass.ds(4 * i + (16 * tb + 2 * par + e), 1)],
                                                     in1=score[:, tb, 0:w], op0=ALU.mult, op1=ALU.add).then_inc(i_acc, 1)
                        split_lo(dve, 2 * g + (1 + e), 1 - e)

            def pick(n_rounds, base):
                for r in range(n_rounds):
                    dve.wait_ge(topk_s, base + 6 * r)
                    dve.nop(nofuse=True)
                    for tb in range(1, TB):
                        dve.max(top8[:, tb - 1, :], score[:, tb, 0:P * (tb + 1)]).then_inc(topk_s, 1)
                    dve.wait_ge(topk_s, base + (6 * r + 3))
                    dve.nop(nofuse=True)
                    for tb in range(1, TB):
                        w = P * (tb + 1)
                        dve.match_replace(score[:, tb, 0:w], top8[:, tb - 1, :], score[:, tb, 0:w], TAKEN).then_inc(topk_s, 1)

            def soft_a(kind, it, k, rqc=None, par=0, sink=None):
                u, tb = 4 * it + k, tb_of(k)
                w, dst, src = width_of(kind, k), prob[:, k, :], bank[Q_BANK[k % 2]]
                dve.wait_ge(s_ready, u + 1)
                if kind in ("A2", "N2"):
                    dve.nop(nofuse=True)
                if kind == "B":
                    c0 = BAND0(k)
                    for e in range(2):
                        c, cb = slice(256 * e + c0, 256 * e + 256), slice(ROW_B * e + c0, ROW_B * e + 256)
                        last = dve.scalar_tensor_tensor(out=dst[:, c], in0=src[:, c], scalar=rqc(tb, e), in1=bb1[par][:, cb],
                                                        op0=ALU.mult, op1=ALU.add)
                    last.then_inc(l_ready, 1)
                    dve.wait_ge(l_ready, u + 1)
                    b0 = 3 * (u - 8) if isinstance(u, int) else 3 * u - 24
                    dve.tensor_reduce(mx[:, k, :], dst.rearrange("p (e c) -> p e c", e=2)[:, :, c0:256], AX.X, ALU.max)\
                        .then_inc(va, 1)
                    dve.wait_ge(va, b0 + 1)
                    dve.tensor_tensor(mx2[:, k, :], mx[:, k, :], sink, ALU.max).then_inc(va, 1)
                    dve.wait_ge(va, b0 + 2)
                    scaled(nmx[:, k, :], mx2[:, k, :], -1.0).then_inc(va, 1)
                    dve.wait_ge(va, b0 + 3)
                    dve.tensor_tensor(sd[:, k, :], sink, nmx[:, k, :], ALU.add).then_inc(m_ready, 1)
                    return
                if kind == "A":
                    dve.scalar_tensor_tensor(out=dst[:, 0:w], in0=src[:, 0:w], scalar=rqc(tb, 0),
                                             in1=bb1[par][:, 384 - P * tb:384 - P * tb + w], op0=ALU.mult, op1=ALU.add).then_inc(va, 1)
                    dve.wait_ge(va, u + 25)
                    dve.nop(nofuse=True)
                    dve.tensor_tensor_reduce(out=dst[:, 0:w], in0=dst[:, 0:w], in1=score[:, tb, 0:w], scale=1.0,
                                             scalar=-3.4e38, op0=ALU.add, op1=ALU.max, accum_out=mx[:, k, 0:1]).then_inc(l_ready, 1)
                elif kind == "C":
                    dve.tensor_scalar(dst[:, 0:w], src[:, 0:w], rqc(tb, 0), -3.4e38, ALU.mult, ALU.max,
                                      accum_out=mx[:, k, 0:1]).then_inc(l_ready, 1)
                elif kind == "A2":
                    dve.tensor_tensor_reduce(out=dst, in0=src[:], in1=b2[par][:, 384 - P * tb:896 - P * tb], scale=1.0,
                                             scalar=-3.4e38, op0=ALU.add, op1=ALU.max, accum_out=mx[:, k, 0:1]).then_inc(l_ready, 1)
                else:
                    dve.tensor_tensor_reduce(out=dst[:, 0:w], in0=src[:, 0:w],
                                             in1=nb[par][:, k, :, :].rearrange("p a b -> p (a b)"), scale=1.0,
                                             scalar=-3.4e38, op0=ALU.add, op1=ALU.max, accum_out=mx[:, k, 0:1]).then_inc(l_ready, 1)
                dve.wait_ge(l_ready, u + 1)
                scaled(nmx[:, k, 0:1], mx[:, k, 0:1], -1.0).then_inc(m_ready, 1)

            def soft_b(kind, it, k):
                u = 4 * it + k
                dve.wait_ge(e_ready, u + 1)
                if kind == "B":
                    dve.tensor_tensor(den[:, k, :], rs[:, k, :], es[:, k, :], ALU.add).then_inc(vb, 1)
                    dve.wait_ge(vb, 2 * u - 15)
                    dve.reciprocal(rden[:, k, :], den[:, k, :]).then_inc(vb, 1)
                    dve.wait_ge(vb, 2 * u - 14)
                    for e in range(2):
                        c = slice(256 * e + BAND0(k), 256 * e + 256)
                        last = scaled(prob[:, k, c], prob[:, k, c], rden[:, k, e:e + 1])
                else:
                    w = width_of(kind, k)
                    dve.reciprocal(rden[:, k, 0:1], rs[:, k, 0:1]).then_inc(vb, 1)
                    dve.wait_ge(vb, u + 17)
                    last = scaled(prob[:, k, 0:w], prob[:, k, 0:w], rden[:, k, 0:1])
                last.then_inc(p_ready, 1)

            def turned_dve(kind, it, k):
                dve.wait_ge(t_ready, 4 * it + k + 1)
                n = len(blocks_of(kind, k))
                dve.tensor_copy(prob_t[0][:, 0:n, :], bank[T_BANK[0]][:, 0:n * P].rearrange("p (a b) -> p a b", b=P))\
                    .then_inc(pt_dve, 1)

            def att_dve(kind, it, hs, **kw):
                if hs == 0:
                    soft_a(kind, it, 0, **kw)
                    soft_a(kind, it, 1, **kw)
                    soft_b(kind, it, 0)
                    soft_b(kind, it, 1)
                elif hs == 1:
                    soft_a(kind, it, 2, **kw)
                    soft_a(kind, it, 3, **kw)
                    turned_dve(kind, it, 0)
                    soft_b(kind, it, 2)
                    soft_b(kind, it, 3)
                elif hs == 2:
                    turned_dve(kind, it, 2)

            for kind, it0, n in (("B", 2, ITEMS_B), ("C", 8, ITEMS_C), ("A", 12, ITEMS_A)):
                if kind == "B":
                    dve.wait_ge(cz_s, 3)
                    dve.sem_inc(topk_s, 1)
                if kind == "A":
                    dve.wait_ge(topk_s, 97)
                    for tb in range(1, TB):
                        w = P * (tb + 1)
                        last = dve.tensor_scalar(score[:, tb, 0:w], score[:, tb, 0:w], -3.2e38, NEG, ALU.is_gt, ALU.mult)
                    last.then_inc(topk_s, 1)
                    dve.wait_ge(topk_s, 98)
                with dve.Fori(0, n // 2) as i:
                    for par in range(2):
                        it = 2 * i + (it0 + par)
                        g = 2 * i + (G_MIX + 6 + it0 + par)
                        ri = 16 * i + (8 * (it0 - 2))
                        dve.wait_ge(it_loaded[par], 64 * i + 32 * it0)
                        if kind == "B":
                            dve.wait_ge(b_loaded[par], 16 * i + 16)
                        if kind == "A":
                            dve.wait_ge(b_loaded[par], 16 * i + 64)
                        kw = {"par": par, "rqc": lambda tb, e: rq[:, bass.ds(ri + (4 * tb + 2 * par + e), 1)],
                              "sink": params[:, bass.ds(4 * i + (PAR["sink"][0] + 2 * par), 2)]}
                        for hs in range(4):
                            att_dve(kind, it, hs, **kw)
                            if hs == 0:
                                split_lo(dve, 2 * g + 1, 1)
                                if kind == "B":
                                    pick(1, 24 * i + (12 * par + 1))
                            elif hs == 2:
                                split_lo(dve, 2 * g + 2, 0)
                                if kind == "B":
                                    pick(1, 24 * i + (12 * par + 7))
                                if kind == "C":
                                    pick(1, 12 * i + (6 * par + 73))
                        dve.wait_ge(pv_ready, it + 1)
                        dve.wait_ge(o_out[par], 16 * i + 8 * it0)
                        dve.scalar_tensor_tensor(out=o_st[par][:], in0=bank[O_BANK][:], scalar=0.5, in1=gb1[par][:],
                                                 op0=ALU.mult, op1=ALU.mult).then_inc(o_ready, 1)
            meet(dve, 4)

            def tiles_lo(n0):
                for n in range(KT):
                    dve.wait_ge(oh_s, n0 + n + 1)
                    dve.tensor_tensor(act_b[1][:, n, :], o_ld[n % 4][:], act_b[0][:, n, :].bitcast(F32), ALU.subtract)\
                        .then_inc(olo_s, 1)

            tiles_lo(0)
            with dve.Fori(0, 8) as j:
                g = j + G_UP

                def gated(c, dst):
                    for n in range(2):
                        last = dve.scalar_tensor_tensor(out=dst[:, n, :], in0=mixg[:, c, n, :], scalar=1.0,
                                                        in1=bank[2 * c + n][:], op0=ALU.add, op1=ALU.mult)
                    last.then_inc(up_ev, 1)

                split_lo(dve, 2 * g + 1, 1)
                dve.wait_ge(mg_loaded, 16 * j + 16)
                dve.wait_ge(up_psum, 2 * j + 1)
                dve.wait_ge(up_lo, j + 1)
                gated(0, m_acc)
                split_lo(dve, 2 * g + 2, 0)
                dve.wait_ge(up_psum, 2 * j + 2)
                gated(1, m_tmp)
                dve.wait_ge(up_ev, 3 * j + 5)
                dve.tensor_tensor(m_acc[:], m_acc[:], m_tmp[:], ALU.add).then_inc(up_ch, 1)
                dve.wait_ge(up_ch, 5 * j + 1)
                summed(g)
                gated(2, m_tmp)
                dve.wait_ge(up_ev, 3 * j + 6)
                dve.tensor_tensor(m_acc[:], m_acc[:], m_tmp[:], ALU.add).then_inc(up_ch, 4)
                dve.wait_ge(up_hi, j + 1)
                dve.scalar_tensor_tensor(out=act_a[1][:, bass.ds(2 * j, 2), :].rearrange("p a b -> p (a b)"),
                                         in0=m_acc[:].rearrange("p a b -> p (a b)"), scalar=0.5,
                                         in1=act_a[0][:, bass.ds(2 * j, 2), :].rearrange("p a b -> p (a b)").bitcast(F32),
                                         op0=ALU.mult, op1=ALU.subtract).then_inc(up_lo, 1)
            meet(dve, 5)

            with dve.Fori(0, 4) as i:
                for s in range(2):
                    g = 2 * i + (G_WO + s)
                    lo2(g)
                    summed(g)
                    dve.wait_ge(xr_loaded[s], 16 * i + 16)
                    dve.wait_ge(x1_out[s], 16 * i + 16)
                    dve.wait_ge(x1h_s, 2 * i + (s + 1))
                    for n in range(2):
                        dve.tensor_tensor(stage[s][:, n, :], bank[2 * s + n][:], xr[s][:, n, :], ALU.add).then_inc(x1f_s, 1)
                    dve.wait_ge(x1h_s, 2 * i + (s + 3))
                    dve.tensor_tensor(act_b[1][:, bass.ds(4 * i + 2 * s, 2), :], stage[s][:],
                                      act_b[0][:, bass.ds(4 * i + 2 * s, 2), :].bitcast(F32), ALU.subtract).then_inc(x1l_s, 1)
            meet(dve, 6)

            def proj2_out(g, i, j, att):
                s = j % 2
                summed(g)
                dve.wait_ge(staged_out[s], staged_before(i, j))
                if j < 3:
                    ins = scaled(*q_rows(i, att, stage[s][:, 1, :], bank[1][:]), HD2 ** -0.5) if j == 0 else \
                        dve.tensor_copy(stage[s][:, 1, :], bank[1][:])
                    ins.then_inc(ev_dve, 1)
                else:
                    for n, (sm, v) in enumerate(((gth, gate2_tanh(i)), (ev_act, g - 16))):
                        dve.wait_ge(sm, v)
                        last = dve.scalar_tensor_tensor(out=stage[s][:, n, :], in0=th_2[:, n, :], scalar=1.0,
                                                        in1=bank[n][:], op0=ALU.add, op1=ALU.mult)
                    last.then_inc(ev_dve, 1)

            def quad(i, att, gemm=True):
                for j in range(4):
                    par, e = j // 2, j % 2
                    it = 4 * i + (14 + j)
                    g = 4 * i + (G_IN2 + j)
                    if att:
                        if att == "A2":
                            dve.wait_ge(b_loaded[e], bias2_loaded(i, j))
                        else:
                            dve.wait_ge(nb_ready[e], nb_count(i, j))
                    for hs in range(4):
                        if att:
                            att_dve(att, it, hs, par=e)
                        if gemm and hs == 0:
                            split_lo(dve, 2 * g + 1, 1)
                        elif gemm and hs == 2:
                            split_lo(dve, 2 * g + 2, 0)
                    if att and e == 1:
                        dve.wait_ge(pv_ready, it + 1)
                        dve.wait_ge(g2_loaded[par], 16 * i)
                        dve.wait_ge(o_out[par], 16 * i + 128)
                        if att == "A2":
                            last = dve.scalar_tensor_tensor(out=o_st[par][:], in0=bank[O_BANK][:], scalar=0.5,
                                                            in1=qkvg[par][3][:], op0=ALU.mult, op1=ALU.mult)
                        else:
                            for cb in range(4):
                                ov, gv = (t[:].rearrange("p (r c) -> p r c", c=64)[:, :, 16 * cb:16 * cb + 16]
                                          for t in (o_st[par], qkvg[par][3]))
                                last = dve.scalar_tensor_tensor(
                                    out=ov, in0=bank[O_BANK][:, P * cb:P * cb + P].rearrange("p (r c) -> p r c", c=16),
                                    scalar=0.5, in1=gv, op0=ALU.mult, op1=ALU.mult)
                        last.then_inc(o_ready, 1)
                    if gemm:
                        proj2_out(g, i, j, att)

            quad(0, None)
            with dve.Fori(1, 4) as i:
                quad(i, "A2")
            quad(4, "A2")
            with dve.Fori(5, 8) as i:
                quad(i, "N2")
            quad(8, "N2", gemm=False)
            meet(dve, 7)

            tiles_lo(KT)

            def rows_out(i, s, last_group=False):
                g = 2 * i + (G_OUT2 + s)
                split_lo(dve, 2 * g + 1, 1)
                if not last_group:
                    split_lo(dve, 2 * g + 2, 0)
                summed(g)
                for b in range(2, TB):
                    last = dve.tensor_copy(z[:, b, bass.ds(512 * i + 256 * s, 256)], bank[4 * s + b][:, 0:GC])
                last.then_inc(ev_dve, 1)
                dve.wait_ge(ev_dve, g - 40)
                dve.wait_ge(ev_act, g - 16)
                for b in range(TB):
                    last = dve.bn_stats(st_z[:, b, bass.ds(12 * i + 6 * s, 6)], z[:, b, bass.ds(512 * i + 256 * s, 256)])
                last.then_inc(st_s, 1)

            with dve.Fori(0, 3) as i:
                for s in range(2):
                    rows_out(i, s)
            rows_out(3, 0)
            rows_out(3, 1, last_group=True)
            dve.wait_ge(st_s, 8)
            for b in range(TB):
                last = dve.bn_aggr(mv[:, b, :], st_z[:, b, :])
            last.then_inc(ln_s, 1)
            dve.wait_ge(ln_s, 1)
            dve.tensor_scalar(rsk[:, 0:TB], mv[:, :, 1], LN_EPS, None, ALU.add).then_inc(ln_s, 1)
            dve.wait_ge(rt2_s, 6)
            dve.reciprocal(rsk[:, 0:TB], ssk[:, 0:TB]).then_inc(ln_s, 1)
            dve.wait_ge(ln_s, 3)
            dve.scalar_tensor_tensor(out=nmr[:], in0=mv[:, :, 0], scalar=-1.0, in1=rsk[:, 0:TB], op0=ALU.mult,
                                     op1=ALU.mult).then_inc(ln_s, 1)
            dve.wait_ge(ln_loaded, 32)
            for b in range(TB):
                dve.wait_ge(ln_a, b + 1)
                dve.tensor_tensor(z[:, b, :], z[:, b, :], ln_g[:], ALU.mult).then_inc(ln_v, 1)
                dve.wait_ge(ln_v, 2 * b + 1)
                dve.tensor_tensor(z[:, b, :], z[:, b, :], ln_b[:], ALU.add).then_inc(ln_v, 1)
            meet(dve, 8)

        @block.gpsimd
        def _(pool):
            for n, done in enumerate(staged_out + o_out + x1_out):
                pool.dma_start(first_d[n:n + 1, :], con_in[n:n + 1, 0:16]).then_inc(done, 16)
            pool.wait_ge(pe_s, 6)
            for dst, src in ((rows_a, rows_1a[:]), (rows_b, rows_1b[:]), (rows_2d, rows_2[:]),
                             (rows_n, rpb_in.rearrange("h r c -> h (r c)"))):
                pool.dma_start(dst.ap(), src.unsqueeze(1).to_broadcast(list(dst.shape))).then_inc(brow_out, 16)
            for i in range(KT):
                pool.wait_ge(tf_s, i + 1)
                pool.nop(nofuse=True)
                pool.dma_start(xt_d[i], tr_f[i % 2][:]).then_inc(xt_out[i % 2], 16)
            for i in range(2):
                pool.wait_ge(xt_out[i], 8 * KT)
            pool.wait_ge(brow_out, 64)
            meet(pool, 1)

            pool.wait_ge(ev_act, 3)
            pool.wait_ge(ev_dve, 3)
            for j in range(ITEMS_B):
                pool.dma_start(v_d[j].rearrange("p (b c) -> p b c", c=P),
                               bkv_n[:, :, 64 + 64 * (j // 3):192 + 64 * (j // 3)]).then_inc(kst_v, 16)
            pool.wait_ge(sp_o, 3)
            for j in range(ITEMS_B):
                pool.dma_start(k_d[j], kt_b[:, j // 3, :]).then_inc(kst_k, 16)
            pool.wait_ge(ev_act, 7)
            pool.wait_ge(ev_dve, 7)
            for h in range(HEADS_C):
                pool.dma_start(v_d[6 + h, :, 0:256].rearrange("p (b c) -> p b c", c=P),
                               mem_vn[:, :, h * P:(h + 1) * P]).then_inc(kst_v, 16)
            pool.wait_ge(sp_o, 4)
            for h in range(HEADS_C):
                pool.dma_start(k_d[6 + h, :, 0:256], kt_c[:, h, :]).then_inc(kst_k, 16)
            pool.wait_ge(kv_act, 8)
            pool.wait_ge(kv_dve, 8)
            for h in range(HEADS_A):
                pool.dma_start(v_d[10 + h].rearrange("p (b c) -> p b c", c=P),
                               v_nat[:, :, h * P:(h + 1) * P]).then_inc(kst_v, 16)
            pool.wait_ge(sp_o, 8)
            for h in range(HEADS_A):
                pool.dma_start(k_d[10 + h], kt_a[:, h, :]).then_inc(kst_k, 16)
            pool.wait_ge(kst_v, 256)
            pool.wait_ge(kst_k, 256)
            meet(pool, 2)

            def tiles(dst, i):
                return dst[bass.ds(i, 2)].rearrange("n p t -> p n t")

            for dst, g0, n in ((iq_d, G_IQ, 4), (q_d, G_Q, 8), (g_d, G_GATE, 8)):
                with pool.Fori(0, n // 2) as i:
                    for s in range(2):
                        g = 2 * i + (g0 + s)
                        pool.wait_ge(ev_act, g)
                        pool.wait_ge(ev_dve, g)
                        pool.nop(nofuse=True)
                        pool.dma_start(tiles(dst, 4 * i + 2 * s), stage[s][:]).then_inc(staged_out[s], 16)
            for s in range(2):
                pool.wait_ge(staged_out[s], 176)
            for par in range(2):
                pool.dma_start(qb1[par][:], iq_d[par]).then_inc(iq_loaded[par], 16)
            meet(pool, 3)

            def mix_store(g, i, par, t0):
                pool.wait_ge(ev_act, g)
                pool.nop(nofuse=True)
                pool.dma_start(mix_d[2 * i + (t0 + par)], stage[par][:].rearrange("p n t -> p (n t)")).then_inc(staged_out[par], 16)

            def load_item(n, par):
                pool.dma_start(qb1[par][:], q_d[n]).then_inc(it_loaded[par], 16)
                pool.dma_start(kb1[par][:], k_d[n]).then_inc(it_loaded[par], 16)
                pool.dma_start(vb1[par][:].rearrange("p a b -> p (a b)"), v_d[n]).then_inc(it_loaded[par], 16)
                pool.dma_start(gb1[par][:], g_d[n]).then_inc(it_loaded[par], 16)

            def load_c(n, par):
                pool.dma_start(qb1[par][:], q_d[n]).then_inc(it_loaded[par], 16)
                pool.dma_start(kb1[par][:, 0:MEM], k_d[n, :, 0:MEM]).then_inc(it_loaded[par], 16)
                pool.dma_start(vb1[par][:, 0:2, :].rearrange("p a b -> p (a b)"), v_d[n, :, 0:2 * P]).then_inc(it_loaded[par], 16)
                pool.dma_start(gb1[par][:], g_d[n]).then_inc(it_loaded[par], 16)

            def shifted(rows, h, at, width, row_step):
                L = rows.shape[2]
                return bass.AP(rows, at + h * (COPIES * L), [[L - row_step, 8], [L - 1, 16], [1, width]])

            def bias_b(j, par):
                pool.dma_start(bb1[par][:], shifted(rows_b, j, 127, 2 * ROW_B - P, 16)).then_inc(b_loaded[par], 16)

            def bias_a(h, par):
                pool.dma_start(bb1[par][:, 0:T], shifted(rows_a, h, 127, T, 16)).then_inc(b_loaded[par], 16)

            def iq_step(i, par, load=True):
                t = 2 * i + par
                if load:
                    pool.wait_ge(i_psum, 6 * t + 9)
                    pool.dma_start(qb1[par][:], iq_d[2 * i + (par + 2)]).then_inc(iq_loaded[par], 16)
                mix_store(2 * i + (G_MIX + par), i, par, 0)

            with pool.Fori(0, 3) as i:
                for par in range(2):
                    iq_step(i, par)
            bias_b(0, 0)
            bias_b(1, 1)
            for par in range(2):
                pool.wait_ge(i_psum, 45 + 6 * par)
                pool.nop(nofuse=True)
                load_item(par, par)
                iq_step(3, par, load=False)
            pool.wait_ge(i_acc, 51)
            for tb in range(1, TB):
                d = score[:, tb, tb * P:(tb + 1) * P]
                pool.affine_select(out=d, in_=d, compare_op=ALU.is_ge, fill=FILL, base=0, pattern=[[-1, P]],
                                   channel_multiplier=1).then_inc(cz_s, 1)

            def step(n_it, i, par, g, nxt):
                mix_store(g, i, par, n_it)
                pool.wait_ge(o_ready, 2 * i + (n_it - 5 + par))
                pool.nop(nofuse=True)
                pool.dma_start(o_d[2 * i + (n_it - 8 + par)], o_st[par][:]).then_inc(o_out[par], 16)
                if nxt:
                    nxt(2 * i + (n_it - 6 + par), par)

            def next_b(n, par):
                load_item(n, par)
                bias_b(n, par)

            def next_a(n, par):
                load_item(n, par)
                bias_a(n - 10, par)

            for n_it, count, same, after in ((8, ITEMS_B, next_b, load_c), (14, ITEMS_C, load_c, next_a),
                                             (18, ITEMS_A, next_a, None)):
                with pool.Fori(0, count // 2 - 1) as i:
                    for par in range(2):
                        step(n_it, i, par, 2 * i + (G_MIX + n_it + par), same)
                i = count // 2 - 1
                for par in range(2):
                    step(n_it, i, par, 2 * i + (G_MIX + n_it + par), after)
            for s in range(2):
                pool.wait_ge(o_out[s], 144)
                pool.wait_ge(staged_out[s], 368)
            meet(pool, 4)

            def load_tiles(src, n0):
                for n in range(KT):
                    if n >= 4:
                        pool.wait_ge(olo_s, n0 + n - 3)
                    pool.dma_start(o_ld[n % 4][:], src[n]).then_inc(ol_s[n % 4], 16)

            load_tiles(o_d, 0)
            pool.wait_ge(olo_s, KT)
            with pool.Fori(0, 8) as j:
                pool.wait_ge(up_ev, 3 * j + 3)
                pool.nop(nofuse=True)
                pool.dma_start(mixg[:].rearrange("p c n t -> p c (n t)"),
                               mix_d[bass.ds(3 * j, 3)].rearrange("c p t -> p c t")).then_inc(mg_loaded, 16)
            meet(pool, 5)

            with pool.Fori(0, 4) as i:
                for s in range(2):
                    pool.wait_ge(x1f_s, 4 * i + (2 * s + 2))
                    pool.nop(nofuse=True)
                    pool.dma_start(xr[s][:], tiles(xt_d, 4 * i + 2 * s)).then_inc(xr_loaded[s], 16)
                for s in range(2):
                    pool.wait_ge(x1f_s, 4 * i + (2 * s + 6))
                    pool.nop(nofuse=True)
                    pool.dma_start(x1_d[2 * i + s], stage[s][:]).then_inc(x1_out[s], 16)
            for s in range(2):
                pool.wait_ge(x1_out[s], 80)
            meet(pool, 6)

            def load_pair(quad_, p):
                for c in range(3):
                    pool.dma_start(qkvg[p][c][:], qkvg_d[quad_, c, p]).then_inc(it_loaded[p], 16)

            def next_bias(kind, i, j):
                e = (j + 1) % 2
                h = 4 * i + (j - 3)
                pool.wait_ge(l_ready, 16 * i + (56 + 4 * j))
                pool.nop(nofuse=True)
                if kind == "A2":
                    pool.dma_start(b2[e][:], shifted(rows_2d, h, 127, 896, 16)).then_inc(b_loaded[e], 16)
                else:
                    pool.dma_start(nl[e][:].rearrange("p a b -> p (a b)"),
                                   shifted(rows_n, h - HEADS_2, 7 * 64 + 15, T, 64)).then_inc(b_loaded[e], 16)
                    pool.wait_ge(b_loaded[e], bias2_loaded(i, j + 1))
                    pool.nop(nofuse=True)
                    for cb in range(4):
                        c0 = BLK_START[cb] - 16 * cb + 16
                        m = con[:, CON["nmask"][0] + 32 * cb:CON["nmask"][0] + 32 * cb + 32]
                        last = pool.tensor_tensor(nb[e][:, cb, :, :], nl[e][:, :, c0:c0 + 32],
                                                  m.unsqueeze(1).to_broadcast([P, 8, 32]), ALU.add)
                    last.then_inc(nb_ready[e], 1)

            def windows(i, p):
                pool.wait_ge(it_loaded[p], pair_loaded(i))
                pool.nop(nofuse=True)
                for cb in range(4):
                    last = pool.tensor_copy(v_win[p][:, 256 * cb:256 * cb + 256].rearrange("p (r c) -> p r c", c=32),
                                            qkvg[p][2][:].rearrange("p (r c) -> p r c", c=64)[:, :, BLK_START[cb]:BLK_START[cb] + 32])
                last.then_inc(vw_ready, 1)

            def stored(i, j):
                pool.wait_ge(staged_out[j % 2], 32 * i + (16 * (j // 2) + 384))
                pool.nop(nofuse=True)

            def quad(i, att, bias_next, gemm=True):
                for j in range(4):
                    par, e = j // 2, j % 2
                    g = 4 * i + (G_IN2 + j)
                    if j == 0 and att:
                        stored(i - 1, 3)
                        pool.dma_start(qkvg[0][3][:], qkvg_d[i - 1, 3, 0]).then_inc(g2_loaded[0], 16)
                        pool.wait_ge(o_ready, outs_before(i, 0))
                        pool.nop(nofuse=True)
                        load_pair(i - 1, 1)
                        pool.dma_start(qkvg[1][3][:], qkvg_d[i - 1, 3, 1]).then_inc(g2_loaded[1], 16)
                    if j == 3 and gemm:
                        stored(i, 0)
                        stored(i, 1)
                        stored(i, 2)
                        load_pair(i, 0)
                        if bias_next == "N2":
                            windows(i + 1, 0)
                    if j < 3 and att:
                        next_bias(att, i, j)
                    if j == 0 and att == "N2":
                        windows(i, 1)
                    if j == 3 and bias_next:
                        next_bias(bias_next, i, j)
                    if att and e == 1:
                        pool.wait_ge(o_ready, outs_before(i, par) + 1)
                        pool.nop(nofuse=True)
                        pool.dma_start(y_d[2 * i + (par - 2)], o_st[par][:]).then_inc(o_out[par], 16)
                    if gemm:
                        pool.wait_ge(ev_act, g - 16)
                        pool.wait_ge(ev_dve, g - 40)
                        pool.nop(nofuse=True)
                        pool.dma_start(qkvg_d[i, j].rearrange("n p t -> p n t"), stage[j % 2][:]).then_inc(staged_out[j % 2], 16)

            quad(0, None, "A2")
            with pool.Fori(1, 4) as i:
                quad(i, "A2", "A2")
            quad(4, "A2", "N2")
            with pool.Fori(5, 8) as i:
                quad(i, "N2", "N2")
            quad(8, "N2", None, gemm=False)
            for s in range(2):
                pool.wait_ge(o_out[s], 272)
            meet(pool, 7)

            load_tiles(y_d, KT)
            pool.dma_start(ln_g[:], lng_in.partition_broadcast(P)).then_inc(ln_loaded, 16)
            pool.dma_start(ln_b[:], lnb_in.partition_broadcast(P)).then_inc(ln_loaded, 16)
            with pool.Fori(0, 4) as i:
                for s in range(2):
                    pool.wait_ge(chunk_used, 4 * i + (2 * (G_OUT2 + s) - 2))
                    pool.nop(nofuse=True)
                    pool.dma_start(xr[s][:], x1_d[2 * i + s]).then_inc(xr_loaded[s], 16)
            for b in range(TB):
                pool.wait_ge(ln_v, 2 * b + 2)
                pool.dma_start(out_v[b], z[:, b, :]).then_inc(fin_out, 16)
            pool.wait_ge(fin_out, 64)
            meet(pool, 8)


def chunks_of(w):
    n = w.shape[1] // GC
    return w.reshape(2, CK, P, n, GC).transpose(3, 0, 2, 1, 4).reshape(2 * n, P, CK * GC)


def padded(w):
    return np.pad(w, ((0, 0), (0, 0), (0, CK * GC - w.shape[2])))


def weight_stream(a):
    w_in, w_in2 = a["w_in"][0], a["w_in_2"][0]
    cut = np.cumsum([0, A_W, KV_RANK, 1024, 64, 16, A_W, B_W, 128, 128, B_W, C_W, C_W, 3 * D]).tolist()
    a_q, ckv, i_q, i_k, i_w, a_g, b_q, b_k, b_v, b_g, c_q, c_g, mix = (w_in[:, p:q] for p, q in zip(cut, cut[1:]))
    ik = np.concatenate([i_k, i_w], 1).reshape(2, CK, P, 80).transpose(0, 2, 1, 3).reshape(2, P, CK * 80)
    kv_up = a["w_kv_up"][0].reshape(2, P, 2, A_W).transpose(2, 1, 0, 3).reshape(2, P, 2 * A_W)
    mix = mix.reshape(D, 3, 8, GC)[:, [1, 2, 0]].transpose(0, 2, 1, 3).reshape(D, 3 * D)
    up = np.concatenate([a["w_up_b"][0], a["w_up_c"][0], a["w_up_a"][0]], 0)
    in2 = w_in2.reshape(D, 2, 4, 4, GC).transpose(0, 1, 3, 2, 4).reshape(D, 4 * D)
    return np.concatenate([
        chunks_of(ckv), padded(ik), chunks_of(np.concatenate([b_k, b_v], 1)), chunks_of(a["w_mem_kv"][0]), padded(kv_up),
        chunks_of(i_q), chunks_of(np.concatenate([b_q, c_q, a_q], 1)), chunks_of(np.concatenate([b_g, c_g, a_g], 1)),
        chunks_of(mix), chunks_of(up), chunks_of(a["w_o"][0]), chunks_of(in2), chunks_of(a["w_out_2"][0])], 0)


def parameters(a):
    twice = lambda g: np.concatenate([g, g]).reshape(P, 1)
    col = lambda g: g.reshape(P, 1)
    tiles = lambda g: g.reshape(-1, P).T
    q_g = np.concatenate([np.repeat(twice(a["q_norm_b"][0]), 6, 1), np.repeat(col(a["q_norm_c"][0]), 4, 1),
                          np.repeat(col(a["q_norm_a"][0]), 6, 1)], 1)
    gate_b = a["gate_bias"][0].reshape(3, 8, GC)[[1, 2, 0]].transpose(1, 0, 2).reshape(-1)
    return np.concatenate([
        tiles(a["norm_g"][0]), tiles(a["mem_norm_g"][0]), tiles(a["kv_norm_g"][0]), twice(a["idx_k_ln_g"][0]),
        twice(a["idx_k_ln_b"][0]), col(a["k_norm_a"][0]), twice(a["k_norm_b"][0]), col(a["k_norm_c"][0]), q_g,
        tiles(gate_b), np.repeat(a["sinks_b"][0].reshape(1, HEADS_B), P, 0)], 1)


def kernel(**inputs):
    from concourse import bacc
    from concourse.bass_utils import run_bass_kernel_spmd

    a = {n: np.asarray(v) for n, v in inputs.items()}
    with_one = lambda t: np.concatenate([t, np.ones((1, t.shape[1]), t.dtype)], 0)
    arrays = {
        "wst": weight_stream(a), "x_rows": a["x"][0], "mem_rows": a["mem"][0], "params": parameters(a),
        "consts": constants(), "positions": position_tables(), "tab_1": with_one(a["rel_bias"]),
        "tab_2": with_one(a["t5_bias_2"]), "rpb": np.pad(a["na_rpb_2"][0], ((0, 0), (0, 1), (16, 17))),
        "ln_gain": a["ln_gain_2"][0], "ln_bias": a["ln_bias_2"][0],
    }
    arrays = {n: np.ascontiguousarray(v) for n, v in arrays.items()}
    nc = bacc.Bacc("TRN2", target_bir_lowering=False, num_devices=1)
    aps = [nc.dram_tensor(n, v.shape, mybir.dt.from_np(v.dtype), kind="ExternalInput").ap() for n, v in arrays.items()]
    out = nc.dram_tensor("out", (1, T, D), F32, kind="ExternalOutput").ap()
    build_kernel(nc, *aps, out)
    r = run_bass_kernel_spmd(nc, [arrays], core_ids=[0])
    return r.results[0]["out"]
```

```python
from contextlib import ExitStack

import numpy as np

import concourse.bass as bass
from concourse import mybir

F32 = mybir.dt.float32
F32R = mybir.dt.float32r
ACT = mybir.ActivationFunctionType
ALU = mybir.AluOpType
AX = mybir.AxisListType

P = 128
D, T, MEM = 2048, 512, 256
KT = D // P
TB = T // P
GC = 256
CK = 8
HEADS_A, HEADS_B, HEADS_C = 6, 12, 4
IDX_HEADS, IDX_DIM, TOPK = 16, 64, 128
KV_RANK, A_W, B_W, C_W = 256, 768, 768, 512
EPS, LN_EPS = 1e-6, 1e-5
ALPHA = 2.0 ** 0.25
NEG = -1.0e30
FILL, TAKEN = -3.0e38, -3.3e38
HD2, HEADS_2 = 64, 16
ROW_A, ROW_B, ROW_2 = 640, 384, 1024
ITEMS_B, ITEMS_C, ITEMS_A = 6, 4, 6
COPIES = 8 + 16 - 1

G_CKV, G_IK, G_BKV, G_KVUP, G_MEM = 0, 1, 2, 3, 4
G_IQ, G_Q, G_GATE, G_MIX = 8, 12, 20, 28
G_UP, G_WO, G_IN2, G_OUT2 = 52, 60, 68, 100
N_GROUPS = 108

PAR = {}
_at = 0
for _n, _w in (("norm_g", 16), ("mem_g", 16), ("kv_g", 2), ("ik_g", 1), ("ik_b", 1), ("k_a", 1),
               ("k_b", 1), ("k_c", 1), ("q_g", 16), ("gate_b", 48), ("sink", 12)):
    PAR[_n] = (_at, _at + _w)
    _at += _w
N_PAR = _at

CON = {}
_at = 0
for _n, _w in (("ident", 128), ("ones", 128), ("aident", 128), ("heads", 32), ("nmask", 128)):
    CON[_n] = (_at, _at + _w)
    _at += _w
N_CON = _at
BLK_START = (0, 8, 24, 32)


def t5_causal(dist):
    n = np.maximum(dist, 0)
    nf = np.maximum(n, 1).astype(np.float32)
    large = 16 + (np.log(nf / np.float32(16)) / np.float32(np.log(8.0)) * np.float32(16)).astype(np.int32)
    return np.where(n < 16, n, np.minimum(large, 31))


def t5_both(rel):
    n = np.abs(rel)
    large = 8 + (np.log(np.maximum(n, 1) / 8) / np.log(1024 / 8) * 8).astype(np.int64)
    return (rel > 0) * 16 + np.where(n < 8, n, np.minimum(large, 15))


def one_hot_rows(bucket, extra):
    rows = np.zeros((33, bucket.size), np.float32)
    rows[bucket, np.arange(bucket.size)] = 1.0
    rows[32] = extra
    return rows


def position_tables():
    m = np.arange(ROW_A)
    dist = 511 - m
    e_a = one_hot_rows(t5_causal(dist), np.where(dist >= 0, 0.0, NEG))
    m = np.arange(ROW_B)
    dist = 255 - m
    e_b = one_hot_rows(t5_causal(dist), np.where((dist >= 0) & (dist < 128), 0.0, NEG))
    rel = np.arange(ROW_2) - 511
    times = sum(((rel % d == 0) & (np.abs(rel) <= 64 * d)).astype(np.int64) for d in (1, 4, 16))
    e_2 = one_hot_rows(t5_both(rel), np.where(times > 0, np.log(np.maximum(times, 1)), NEG))
    return np.ascontiguousarray(np.concatenate([e_a, e_b, e_2], 1), dtype=np.float32)


def constants():
    con = np.zeros((P, N_CON), np.float32)
    eye = np.eye(P, dtype=np.float32)
    con[:, slice(*CON["ident"])] = eye
    con[:, slice(*CON["ones"])] = 1.0
    con[:, slice(*CON["aident"])] = eye * np.float32(ALPHA)
    heads = np.zeros((P, 16, 2), np.float32)
    heads[:64, 0:6, 0] = 1.0
    heads[64:, 0:6, 1] = 1.0
    heads[:, 6:16, 0] = 1.0
    con[:, slice(*CON["heads"])] = heads.reshape(P, 32)
    i = np.arange(P)[:, None] % 16
    j = np.arange(32)[None, :]
    for cb in range(4):
        qc, kc = 16 * cb + i, BLK_START[cb] + j
        first = np.clip(qc - 8, 0, 48)
        a = CON["nmask"][0] + 32 * cb
        con[:, a:a + 32] = np.where((kc >= first) & (kc < first + 16), 0.0, NEG)
    return con


def build_kernel(nc, wst, x_in, mem_in, par_in, con_in, pos_in, tab1_in, tab2_in, rpb_in, lng_in, lnb_in, out):
    x_cols = x_in.rearrange("(b p) d -> p b d", p=P)
    x_v = x_in.rearrange("(b p) d -> b p d", p=P)
    mem_v = mem_in.rearrange("(b p) d -> b p d", p=P)
    out_v = out.rearrange("a (b p) d -> (a b) p d", p=P)

    iq_d = nc.dram_tensor("iq_d", [8, P, T], F32).ap()
    q_d = nc.dram_tensor("q_d", [16, P, T], F32).ap()
    k_d = nc.dram_tensor("k_d", [16, P, T], F32).ap()
    v_d = nc.dram_tensor("v_d", [16, P, T], F32).ap()
    g_d = nc.dram_tensor("g_d", [16, P, T], F32).ap()
    o_d = nc.dram_tensor("o_d", [16, P, T], F32).ap()
    mix_d = nc.dram_tensor("mix_d", [24, P, 2 * T], F32).ap()
    x1_d = nc.dram_tensor("x1_d", [8, P, 2, T], F32).ap()
    qkvg_d = nc.dram_tensor("qkvg_d", [8, 4, 2, P, T], F32).ap()
    y_d = nc.dram_tensor("y_d", [16, P, T], F32).ap()
    first_d = nc.dram_tensor("first_d", [6, 16], F32).ap()
    rows_a = nc.dram_tensor("rows_a", [HEADS_A, COPIES, ROW_A], F32)
    rows_b = nc.dram_tensor("rows_b", [ITEMS_B, COPIES, 2 * ROW_B], F32)
    rows_2d = nc.dram_tensor("rows_2d", [HEADS_2, COPIES, ROW_2], F32)
    rows_n = nc.dram_tensor("rows_n", [HEADS_2, COPIES, ROW_2], F32)

    ctx = ExitStack()
    with ctx:
        cursor = [-(-nc.sbuf_base // 64) * 64]

        def region(size):
            at = cursor[0]
            cursor[0] += size
            return at

        def sb_at(name, shape, at, dt=F32):
            return nc.alloc_sbuf_tensor_at(name, shape, dt, offset=at)

        def sem(name):
            return ctx.enter_context(nc.semaphore(name))

        KB = 1024
        W_AT, RA, RB, Y = region(48 * KB), region(64 * KB), region(64 * KB), region(0)
        w_raw = [sb_at(f"w_raw{i}", [P, CK * GC], W_AT + 8 * KB * i) for i in range(2)]
        w_hi = [sb_at(f"w_hi{i}", [P, CK * GC], W_AT + 8 * KB * (2 + i), F32R) for i in range(2)]
        w_lo = [sb_at(f"w_lo{i}", [P, CK * GC], W_AT + 8 * KB * (4 + i), F32R) for i in range(2)]
        act_a = [sb_at(f"act_a{i}", [P, KT, T], RA + 32 * KB * i, F32R) for i in range(2)]
        act_b = [sb_at(f"act_b{i}", [P, KT, T], RB + 32 * KB * i, F32R) for i in range(2)]

        o_raw = sb_at("o_raw", [P, KT, T], RB + 32 * KB)

        x_nat = sb_at("x_nat", [P, TB, D], RB + 32 * KB)
        mem_t = [sb_at(f"mem_t{i}", [P, KT, MEM], RB + 16 * KB * i, F32R) for i in range(2)]
        rows_1a = sb_at("rows_1a", [HEADS_A, ROW_A], RB + 16 * KB)
        rows_1b = sb_at("rows_1b", [ITEMS_B, 2 * ROW_B], RB + 19 * KB)
        rows_2 = sb_at("rows_2", [HEADS_2, ROW_2], RB + 22 * KB)
        junk = sb_at("junk", [P, D], RB)
        o = 32 * KB
        ckv_t = [sb_at(f"ckv_t{i}", [P, 2, T], RB + o + 4 * KB * i, F32R) for i in range(2)]
        ckv_n = sb_at("ckv_n", [P, TB, 256], RB + o + 8 * KB)
        ckv_f = sb_at("ckv_f", [P, 2, T], RB + o + 12 * KB)
        bkv_n = sb_at("bkv_n", [P, TB, 256], RB + o + 16 * KB)
        kb_n = sb_at("kb_n", [P, TB, 2, 2, 64], RB + o + 20 * KB)
        ik_n = sb_at("ik_n", [P, TB, 80], RB + o + 24 * KB)
        ik_d = sb_at("ik_d", [P, TB, 2, 64], RB + o + 26 * KB)
        kt_b = sb_at("kt_b", [P, 2, T], RB + o + 12 * KB)
        kt_a = sb_at("kt_a", [P, HEADS_A, T], RB + o)
        mem_kn = sb_at("mem_kn", [P, 2, C_W], RB + o + 24 * KB)
        mem_vn = sb_at("mem_vn", [P, 2, C_W], RB + o + 20 * KB)
        k_nat = sb_at("k_nat", [P, TB, A_W], Y)
        v_nat = sb_at("v_nat", [P, TB, A_W], Y + 12 * KB)
        kt_c = sb_at("kt_c", [P, HEADS_C, MEM], Y + 8 * KB)
        sq_w = sb_at("sq_w", [P, 1024], RB + o + 28 * KB)
        score = sb_at("score", [P, TB, T], RB)
        qb1 = [sb_at(f"qb1{i}", [P, T], RB + 8 * KB + 2 * KB * i) for i in range(2)]
        kb1 = [sb_at(f"kb1{i}", [P, T], RB + 12 * KB + 2 * KB * i) for i in range(2)]
        vb1 = [sb_at(f"vb1{i}", [P, TB, P], RB + 16 * KB + 2 * KB * i) for i in range(2)]
        gb1 = [sb_at(f"gb1{i}", [P, T], RB + 20 * KB + 2 * KB * i) for i in range(2)]
        bb1 = [sb_at(f"bb1{i}", [P, 2 * ROW_B - P], RB + 24 * KB + 3 * KB * i) for i in range(2)]
        qkvg = [[sb_at(f"qkvg{i}{c}", [P, T], RA + 2 * KB * (4 * i + c)) for c in range(4)] for i in range(2)]
        b2 = [sb_at(f"b2_{i}", [P, 896], RA + 16 * KB + 3584 * i) for i in range(2)]
        nl = [sb_at(f"nl{i}", [P, 8, 64], RA + 24 * KB + 2 * KB * i) for i in range(2)]
        nb = [sb_at(f"nb{i}", [P, 4, 8, 32], RA + 28 * KB + 4 * KB * i) for i in range(2)]
        v_tok = [sb_at(f"v_tok{i}", [P, 8, P], RA + 36 * KB + 4 * KB * i) for i in range(2)]
        v_win = [sb_at(f"v_win{i}", [P, 1024], RA + 48 * KB + 4 * KB * i) for i in range(2)]
        th_2 = sb_at("th_2", [P, 2, T], RA + 44 * KB)
        z = sb_at("z", [P, TB, D], RA)
        ln_g = sb_at("ln_g", [P, D], RA + 32 * KB)
        ln_b = sb_at("ln_b", [P, D], RA + 40 * KB)
        stage = [sb_at(f"stage{i}", [P, 2, T], Y + 4 * KB * i) for i in range(2)]
        prob = sb_at("prob", [P, 4, T], Y + 8 * KB)
        prob_t = [sb_at(f"prob_t{i}", [P, 4, P], Y + 16 * KB + 2 * KB * i) for i in range(2)]
        o_st = [sb_at(f"o_st{i}", [P, T], Y + 20 * KB + 2 * KB * i) for i in range(2)]
        mem_nat = sb_at("mem_nat", [P, 2, D], Y)
        rbc = sb_at("rbc", [P, T + MEM], Y + 16 * KB)
        tr_h = [sb_at(f"tr_h{i}", [P, T], Y + 20 * KB + 2 * KB * i) for i in range(2)]
        sq_q = sb_at("sq_q", [P, 2, T], Y + 8 * KB)
        th_g = sb_at("th_g", [P, 2, T], Y + 12 * KB)
        mixg = sb_at("mixg", [P, 3, 2, T], Y)
        m_acc = sb_at("m_acc", [P, 2, T], Y + 12 * KB)
        m_tmp = sb_at("m_tmp", [P, 2, T], Y + 16 * KB)
        xr = [sb_at(f"xr{i}", [P, 2, T], Y + 8 * KB + 4 * KB * i) for i in range(2)]
        xc = [sb_at(f"xc{i}", [P, TB, GC], Y + 8 * KB + 4 * KB * i) for i in range(2)]
        s0 = Y + 24 * KB
        params = sb_at("params_sb", [P, N_PAR], s0)
        con = sb_at("con", [P, N_CON], s0 + 512)
        s1 = s0 + 512 + 4 * N_CON + 64
        s1 = -(-s1 // 64) * 64
        small_at = [s1]

        def small(name, shape):
            n = 4
            for d in shape[1:]:
                n *= d
            t = sb_at(name, shape, small_at[0])
            small_at[0] += -(-n // 32) * 32
            return t

        rdiag = sb_at("rdiag", [P, 6, P], RB + 28 * KB)
        pos = sb_at("pos", [33, ROW_A + ROW_B + ROW_2], W_AT + 24 * KB)
        tab1 = small("tab1", [33, 18])
        tab2 = small("tab2", [33, 16])
        ssq = small("ssq", [P, 8])
        rstd = small("rstd", [P, 8])
        ssk = small("ssk", [P, 24])
        rsk = small("rsk", [P, 24])
        stats = small("stats", [P, TB, 6])
        st_z = small("st_z", [P, TB, 48])
        mv = small("mv", [P, TB, 2])
        half_b = small("half_b", [P, 48])
        qgs = small("qgs", [P, 16])
        iw = small("iw", [P, TB * 16])
        ik_t = small("ik_t", [P, T])
        ssq_q = small("ssq_q", [P, 128])
        rq = small("rq", [P, 128])
        mx = small("mx", [P, 4, 2])
        mx2 = small("mx2", [P, 4, 2])
        nmx = small("nmx", [P, 4, 2])
        rs = small("rs", [P, 4, 2])
        es = small("es", [P, 4, 2])
        sd = small("sd", [P, 4, 2])
        den = small("den", [P, 4, 2])
        rden = small("rden", [P, 4, 2])
        top8 = small("top8", [P, 3, 8])
        nmr = small("nmr", [P, TB])
        assert small_at[0] <= nc.sbuf_usable_end, (small_at[0], nc.sbuf_usable_end)

        def pcol(name, i=0, n=1):
            a = PAR[name][0] + i
            return params[:, a:a + n]

        ident = con[:, CON["ident"][0]:CON["ident"][1]]
        ones = con[:, CON["ones"][0]:CON["ones"][1]]
        aident = con[:, CON["aident"][0]:CON["aident"][1]]

        bank = [ctx.enter_context(nc.psum_tensor(f"bank{i}", [P, 512], F32)) for i in range(8)]

        w_loaded = [sem(f"w_loaded{i}") for i in range(2)]
        hi_ready, lo_ready = sem("hi_ready"), sem("lo_ready")
        chunk_used = sem("chunk_used")
        ev_act, ev_dve = sem("ev_act"), sem("ev_dve")
        staged_out = [sem(f"staged_out{i}") for i in range(2)]
        barrier = sem("barrier")
        con_s = sem("con_loaded")
        x_s = [sem(f"x_loaded{i}") for i in range(TB)]
        mem_s = [sem(f"mem_loaded{i}") for i in range(2)]
        sq_s, rs_s = sem("squares"), sem("rstd_chain")
        rt_s = sem("roots")
        rd_s, rb_s, rbc_s = sem("rdiag_ready"), sem("rb_psum"), sem("rbc_ready")
        tr_s, th_s, tt_s, tl_s, ml_s = sem("tr_psum"), sem("tr_scaled"), sem("tr_hi"), sem("tr_lo"), sem("mem_lo")
        pb_s, pe_s, brow_out = sem("bias_psum"), sem("bias_copied"), sem("brow_out")
        sp_v, sp_h, sp_l = sem("special_chain"), sem("latent_hi"), sem("latent_lo")
        ms_s, rt2_s = sem("mean_squares"), sem("special_roots")
        sp_t, sp_c, sp_o = sem("special_transposed"), sem("special_normed"), sem("special_out")
        kv_psum, kv_act, kv_dve = sem("kv_psum"), sem("kv_act"), sem("kv_dve")
        kst_k, kst_v = sem("k_stored"), sem("v_stored")
        qsq, qssq, qcp, rq_s = sem("q_squares"), sem("q_ssq_psum"), sem("q_ssq_copied"), sem("rq_chain")
        gth = sem("gate_tanh")
        it_loaded = [sem(f"item_loaded{i}") for i in range(2)]
        iq_loaded = [sem(f"iq_loaded{i}") for i in range(2)]
        g2_loaded = [sem(f"gate2_loaded{i}") for i in range(2)]
        b_loaded = [sem(f"bias_loaded{i}") for i in range(2)]
        nb_ready = [sem(f"nbias_ready{i}") for i in range(2)]
        s_ready, l_ready, m_ready = sem("logits_psum"), sem("logits_ready"), sem("max_ready")
        e_ready, p_ready, t_ready = sem("exp_ready"), sem("prob_ready"), sem("prob_t_psum")
        half_done = sem("first_head_done")
        va, vb = sem("max_chain"), sem("scale_chain")
        pt_act, pt_dve = sem("prob_t_act"), sem("prob_t_dve")
        pv_ready, o_ready = sem("pv_psum"), sem("o_ready")
        o_out = [sem(f"o_out{i}") for i in range(2)]
        i_psum, i_rel, i_acc = sem("idx_psum"), sem("idx_relu"), sem("idx_acc")
        topk_s, cz_s, zero_s = sem("topk_chain"), sem("causal_fill"), sem("score_zero")
        vt_psum, vt_ready, vw_ready = sem("v_tok_psum"), sem("v_tok_ready"), sem("v_windows")
        ol_s = [sem(f"o_loaded{i}") for i in range(6)]
        oh_s, olo_s = sem("o_hi"), sem("o_lo")
        mg_loaded = sem("mixg_loaded")
        up_psum, up_ev, up_ch, up_hi, up_lo = sem("up_psum"), sem("up_read"), sem("up_chain"), sem("up_hi"), sem("up_lo")
        xr_loaded = [sem(f"xr_loaded{i}") for i in range(2)]
        x1f_s, x1h_s, x1l_s = sem("x1_ready"), sem("x1_hi"), sem("x1_lo")
        x1_out = [sem(f"x1_out{i}") for i in range(2)]
        st_s = sem("stats_ready")
        ln_loaded, ln_s, ln_a, ln_v = sem("ln_loaded"), sem("ln_chain"), sem("ln_norm"), sem("ln_done")
        ln_m, ln_p = sem("ln_scaled"), sem("ln_done_pool")
        fin_out = sem("fin_out")

        LATENT_READY = 8
        LN_VAR, LN_NMR = 2, 4

        def meet(eng, n):
            eng.drain().then_inc(barrier, 1)
            eng.wait_ge(barrier, 4 * n)

        def split_hi(act, c, s, first=False):
            act.wait_ge(w_loaded[s], 8 * (c - s) + 16)
            if not first:
                act.wait_ge(chunk_used, c - 1)
            act.activation(w_hi[s][:], w_raw[s][:], ACT.Copy).then_inc(hi_ready, 1)

        def split_lo(dve, c, s):
            dve.wait_ge(hi_ready, c + 1)
            dve.tensor_tensor(w_lo[s][:], w_raw[s][:], w_hi[s][:].bitcast(F32), ALU.subtract).then_inc(lo_ready, 1)

        def chunk_ready(pe, c):
            pe.wait_ge(hi_ready, c + 1)
            pe.wait_ge(lo_ready, c + 1)

        def wt(buf, kt, n0, n, width=GC):
            return buf[:, kt * width + n0:kt * width + n0 + n]

        def mm3(pe, out_ap, l_hi, l_lo, r_hi, r_lo, start, stop):
            pe.matmul(out_ap, l_hi, r_hi, start=start, stop=False)
            pe.matmul(out_ap, l_lo, r_hi, start=False, stop=False)
            return pe.matmul(out_ap, l_hi, r_lo, start=False, stop=stop)

        def rows_t(pe, s, kts, act, banks, first_k=0, last_k=KT - 1):
            for kt in kts:
                for n in range(2):
                    k = CK * s + kt
                    last = mm3(pe, bank[banks[n]][:], wt(w_hi[s], kt, n * P, P), wt(w_lo[s], kt, n * P, P),
                               act[0][:, k, :], act[1][:, k, :], start=(k == first_k), stop=(k == last_k))
            return last

        def rows_kt(pe, s, kt, act, blocks, width, banks, w):
            k = CK * s + kt
            for b in range(blocks):
                last = mm3(pe, bank[banks[b]][:, 0:width], act[0][:, k, b * P:(b + 1) * P],
                           act[1][:, k, b * P:(b + 1) * P], wt(w_hi[s], kt, 0, width, w),
                           wt(w_lo[s], kt, 0, width, w), start=(k == 0), stop=(k == KT - 1))
            return last

        def group_rows(pe, g, act, blocks, width, banks, w=GC, between=None):
            for s in range(2):
                chunk_ready(pe, 2 * g + s)
                for kt in range(CK):
                    last = rows_kt(pe, s, kt, act, blocks, width, banks, w)
                last.then_inc(chunk_used, 1)
                if s == 0 and between:
                    between()

        def tb_of(k):
            return TB - 1 - k

        def width_of(kind, k):
            return {"A": P * (tb_of(k) + 1), "B": 512, "C": 256, "A2": 512, "N2": 256}[kind]

        def blocks_of(kind, k):
            if kind == "B":
                return [0, 1, 2, 3] if tb_of(k) else [1, 3]
            return list(range(width_of(kind, k) // P))

        def pair_loaded(i):
            return 48 * i + 512

        def outs_before(i, par):
            return 2 * i + (16 + par)

        def vt_count(kind, i, par):
            return 2 * i + (par - 1) if kind == "A2" else 4 * i + (2 * par - 10)

        def windows_ready(i, par):
            return 2 * i + (par - 9)

        PARTS_1 = ((0, 3), (3, 6), (6, 10), (10, 14), (14, 15), (15, 16))
        PARTS_2 = ((0, 5), (5, 10), (10, 14), (14, 15), (15, 16))

        def q_rows(i, att, dst, src):
            if att == "N2" or (isinstance(i, int) and i == 4):
                return (dst.rearrange("p (b r c) -> p b r c", b=4, r=8),
                        src.rearrange("p (r b c) -> p b r c", b=4, r=8))
            return dst, src

        def staged_before(i, j):
            return 32 * i + (16 * (j // 2) + 368)

        def bias2_loaded(i, j):
            return 32 * i + (80 + 16 * (j // 2))

        def nb_count(i, j):
            return 2 * i + (j // 2 - 9)

        def gate2_tanh(i):
            return i + 9

        Q_BANK, T_BANK, O_BANK, V_BANK = (2, 3), (4, 5), 6, 7
        BAND0 = lambda k: 0 if tb_of(k) else P

        block = ctx.enter_context(nc.Block())

        @block.sync
        def _(sp):
            sp.dma_start(con[:], con_in).then_inc(con_s, 16)
            sp.dma_start(params[:], par_in).then_inc(con_s, 16)
            sp.dma_start(pos[:], pos_in).then_inc(con_s, 16)
            sp.dma_start(tab1[:], tab1_in).then_inc(con_s, 16)
            sp.dma_start(tab2[:], tab2_in).then_inc(con_s, 16)
            for b in range(TB):
                sp.dma_start(x_nat[:, b, :], x_v[b]).then_inc(x_s[b], 16)
            for s in range(2):
                sp.dma_start(w_raw[s][:], wst[s]).then_inc(w_loaded[s], 16)
            for b in range(2):
                sp.dma_start(mem_nat[:, b, :], mem_v[b]).then_inc(mem_s[b], 16)
            with sp.Fori(1, N_GROUPS) as g:
                for s in range(2):
                    sp.wait_ge(lo_ready, 2 * g + s - 1)
                    sp.dma_start(w_raw[s][:], wst[2 * g + s]).then_inc(w_loaded[s], 16)

        B0, N0 = ROW_A, ROW_A + ROW_B
        BIAS_JOBS = [(tab1[:, 0:6], 0, 512, rows_1a[:, 0:512]), (tab1[:, 0:6], 512, ROW_A, rows_1a[:, 512:ROW_A]),
                     (tab1[:, 6:18:2], B0, N0, rows_1b[:, 0:ROW_B]),
                     (tab1[:, 7:18:2], B0, N0, rows_1b[:, ROW_B:2 * ROW_B]),
                     (tab2[:], N0, N0 + 512, rows_2[:, 0:512]), (tab2[:], N0 + 512, N0 + ROW_2, rows_2[:, 512:ROW_2])]

        @block.tensor
        def _(pe):
            for first, n in ((s_ready, 8), (t_ready, 8), (pv_ready, 2), (i_psum, 3), (qssq, 1)):
                pe.sem_inc(first, n)
            pe.wait_ge(con_s, 80)
            for n, (heads, a, b, dst) in enumerate(BIAS_JOBS):
                pe.matmul(bank[n][0:dst.shape[0], 0:b - a], heads, pos[:, a:b], start=True, stop=True).then_inc(pb_s, 1)
            pe.wait_ge(pe_s, 6)
            for i in range(KT + 4):
                if i < KT:
                    if i >= 4:
                        pe.wait_ge(th_s, i - 3)
                    for b in range(TB):
                        if i == 0:
                            pe.wait_ge(x_s[b], 16)
                        last = pe.transpose(bank[i % 4][:, b * P:(b + 1) * P], x_nat[:, b, i * P:(i + 1) * P], ident)
                    last.then_inc(tr_s, 1)
                if i == 1:
                    pe.wait_ge(rd_s, 1)
                    for b in range(TB):
                        last = pe.matmul(bank[6][:, b * P:(b + 1) * P], ones, rdiag[:, b, :], start=True, stop=True)
                    last.then_inc(rb_s, 1)
                if i >= 4:
                    k = i - 4
                    if k == 0:
                        pe.wait_ge(rbc_s, 1)
                    if k % CK == 0:
                        chunk_ready(pe, k // CK)
                    pe.wait_ge(tt_s, k + 1)
                    pe.wait_ge(tl_s, k + 1)
                    last = rows_kt(pe, k // CK, k % CK, act_a, TB, 256, (4, 5, 6, 7), GC)
                    if k % CK == CK - 1:
                        last.then_inc(chunk_used, 1)

            def wait_read(n):
                pe.wait_ge(ev_act, n)
                pe.wait_ge(ev_dve, n)

            def turn_mem(m):
                if m >= 3:
                    pe.wait_ge(th_s, KT + m - 2)
                for n in range(2):
                    for b in range(2):
                        at, kt = n * MEM + b * P, 2 * m + n
                        last = pe.transpose(bank[5 + m % 3][:, at:at + P], mem_nat[:, b, kt * P:(kt + 1) * P], ident)
                last.then_inc(tr_s, 1)

            def mem_first():
                wait_read(1)
                pe.wait_ge(rd_s, 2)
                for b in range(2):
                    last = pe.matmul(bank[4][:, b * P:(b + 1) * P], ones, rdiag[:, TB + b, :], start=True, stop=True)
                last.then_inc(rb_s, 1)
                for m in range(3):
                    turn_mem(m)

            def turn_latent():
                for m in range(6, 8):
                    turn_mem(m)
                pe.wait_ge(th_s, KT + 7)
                pe.wait_ge(sp_c, 1)
                for kt in range(2):
                    for b in range(TB):
                        last = pe.transpose(bank[4 + kt][:, b * P:(b + 1) * P], ckv_n[:, b, kt * P:(kt + 1) * P], ident)
                last.then_inc(sp_t, 1)

            pe.wait_ge(th_s, KT)
            group_rows(pe, G_IK, act_a, TB, 80, range(4), 80, mem_first)
            for m in range(3, 6):
                turn_mem(m)
            wait_read(2)
            group_rows(pe, G_BKV, act_a, TB, 256, range(4), between=turn_latent)
            pe.wait_ge(th_s, KT + 8)
            pe.wait_ge(sp_c, 2)
            for b in range(TB):
                last = pe.transpose(bank[6][:, b * P:(b + 1) * P], ik_d[:, b, :, :].rearrange("p a c -> p (a c)"), ident)
            last.then_inc(sp_t, 1)
            pe.wait_ge(sp_h, 1)
            pe.wait_ge(sp_l, 1)
            wait_read(3)
            for kind in range(2):
                chunk_ready(pe, 2 * G_KVUP + kind)
                for b in range(TB):
                    u = kind * TB + b
                    if u >= 2:
                        pe.wait_ge(kv_act, u - 1)
                        pe.wait_ge(kv_dve, u - 1)
                    for half in range(2):
                        for kt in range(2):
                            last = mm3(pe, bank[2 * (u % 2) + half][:, 0:384], ckv_t[0][:, kt, b * P:(b + 1) * P],
                                       ckv_t[1][:, kt, b * P:(b + 1) * P], wt(w_hi[kind], kt, half * 384, 384, A_W),
                                       wt(w_lo[kind], kt, half * 384, 384, A_W), start=(kt == 0), stop=(kt == 1))
                    last.then_inc(chunk_used if b == TB - 1 else kv_psum, 1)
            pe.wait_ge(tt_s, KT + 8)
            pe.wait_ge(ml_s, 8)
            pe.wait_ge(kv_act, 7)
            pe.wait_ge(kv_dve, 7)
            group_rows(pe, G_MEM, mem_t, 2, 256, (0, 1))
            pe.wait_ge(kv_act, 8)
            pe.wait_ge(kv_dve, 8)
            group_rows(pe, G_MEM + 1, mem_t, 2, 256, (2, 3))
            pe.wait_ge(sp_c, 3)
            pe.wait_ge(sp_o, 1)
            for kv in range(2):
                for b in range(TB):
                    last = pe.transpose(bank[4 + kv][:, b * P:(b + 1) * P],
                                        kb_n[:, b, kv, :, :].rearrange("p a c -> p (a c)"), ident)
            last.then_inc(sp_t, 1)
            wait_read(4)
            group_rows(pe, G_MEM + 2, mem_t, 2, 256, (0, 1))
            wait_read(5)
            group_rows(pe, G_MEM + 3, mem_t, 2, 256, (2, 3))
            pe.wait_ge(sp_c, 4)
            for b in range(TB):
                pe.wait_ge(sp_o, 3 + max(b - 1, 0))
                for h in range(HEADS_A):
                    bk = 4 + 2 * (b % 2) + h // 4
                    last = pe.transpose(bank[bk][:, (h % 4) * P:(h % 4 + 1) * P], k_nat[:, b, h * P:(h + 1) * P], ident)
                last.then_inc(sp_t, 1)

            def proj(g, s, between=None):
                wait_read(g - 2)
                for c in range(2):
                    chunk_ready(pe, 2 * g + c)
                    rows_t(pe, c, range(CK), act_a, (2 * s, 2 * s + 1)).then_inc(chunk_used, 1)
                    if c == 0 and between:
                        between()

            def turn_mem_keys():
                pe.wait_ge(sp_c, 5)
                pe.wait_ge(sp_o, 6)
                for h in range(HEADS_C):
                    for b in range(2):
                        at = (h % 2) * 256 + b * P
                        last = pe.transpose(bank[4 + h // 2][:, at:at + P], mem_kn[:, b, h * P:(h + 1) * P], ident)
                last.then_inc(sp_t, 1)

            def ssq(i, s):
                pe.wait_ge(ev_act, 2 * i + (G_Q + s))
                pe.wait_ge(qcp, 2 * i + (s + 1))
                for n_ in range(2):
                    for b in range(TB):
                        c = (b * 2 + n_) * 2
                        hd = con[:, bass.ds(4 * (2 * i) + (CON["heads"][0] + 4 * s + 2 * n_), 2)]
                        last = pe.matmul(bank[4 + s][:, c:c + 2], sq_q[:, n_, b * P:(b + 1) * P], hd,
                                         start=True, stop=True)
                last.then_inc(qssq, 1)

            proj(G_IQ, 0)
            proj(G_IQ + 1, 1, turn_mem_keys)
            proj(G_IQ + 2, 0)
            proj(G_IQ + 3, 1)
            pe.wait_ge(sp_o, 8)
            proj(G_Q, 0)
            proj(G_Q + 1, 1, lambda: ssq(0, 0))
            with pe.Fori(1, 4) as i:
                proj(2 * i + G_Q, 0, lambda: ssq(i - 1, 1))
                proj(2 * i + (G_Q + 1), 1, lambda: ssq(i, 0))
            proj(G_GATE, 0, lambda: ssq(3, 1))
            proj(G_GATE + 1, 1)
            with pe.Fori(1, 4) as i:
                for s in range(2):
                    proj(2 * i + (G_GATE + s), s)
            meet(pe, 1)

            def gemm_part(g, hs, act):
                s, kts = hs // 2, range(4 * (hs % 2), 4 * (hs % 2) + 4)
                if hs % 2 == 0:
                    chunk_ready(pe, 2 * g + s)
                last = rows_t(pe, s, kts, act, (0, 1))
                if hs % 2 == 1:
                    last.then_inc(chunk_used, 1)

            def idx_units(t, e):
                for j in range(3):
                    ui = 6 * t + (3 + 3 * e + j)
                    tb, half = 3 - j, slice(64 * e, 64 * e + 64)
                    pe.wait_ge(i_rel, ui - 2)
                    pe.matmul(bank[2 + j][:, 0:P * (tb + 1)], qb1[par][half, tb * P:(tb + 1) * P],
                              ik_t[half, 0:P * (tb + 1)], start=True, stop=True).then_inc(i_psum, 1)

            with pe.Fori(0, 4) as i:
                for par in range(2):
                    g, t = 2 * i + (G_MIX + par), 2 * i + par
                    for hs in range(4):
                        if hs % 2 == 0:
                            if hs == 0:
                                pe.wait_ge(iq_loaded[par], 16 * i + 16)
                            idx_units(t, hs // 2)
                        if hs == 0:
                            pe.wait_ge(ev_act, g - 1)
                        gemm_part(g, hs, act_a)

            def qk(kind, it, k, q, kk):
                u, tb = 4 * it + k, tb_of(k)
                dst = bank[Q_BANK[k % 2]]
                pe.wait_ge(l_ready, u - 1)
                if kind == "B":
                    for e in range(2):
                        half = slice(64 * e, 64 * e + 64)
                        c0 = BAND0(k)
                        last = pe.matmul(dst[:, 256 * e + c0:256 * e + 256], q[half, tb * P:(tb + 1) * P],
                                         kk[half, (tb - 1) * P + c0:(tb + 1) * P], start=True, stop=True)
                        if e == 0:
                            last.then_inc(half_done, 1)
                            pe.wait_ge(half_done, u - 7)
                    last.then_inc(s_ready, 1)
                else:
                    w = width_of(kind, k)
                    pe.matmul(dst[:, 0:w], q[:, tb * P:(tb + 1) * P], kk[:, 0:w], start=True, stop=True)\
                        .then_inc(s_ready, 1)

            def qk2(kind, it, k, e, q, kk):
                u, half = 4 * it + k, slice(64 * e, 64 * e + 64)
                dst = bank[Q_BANK[k % 2]]
                pe.wait_ge(l_ready, u - 1)
                if kind == "A2":
                    tb = tb_of(k)
                    ins = pe.matmul(dst[:], q[half, tb * P:(tb + 1) * P], kk[half, :], start=True, stop=True)
                else:
                    kv = kk[half, :].rearrange("p (r c) -> p r c", c=64)[:, :, BLK_START[k]:BLK_START[k] + 32]
                    ins = pe.matmul(dst[:, 0:256], q[half, k * P:(k + 1) * P], kv, start=True, stop=True)
                ins.then_inc(s_ready, 1)

            def turn(kind, it, k):
                u = 4 * it + k
                pe.wait_ge(p_ready, u + 1)
                pe.wait_ge(pt_act if k % 2 else pt_dve, 2 * it + k // 2)
                for b in blocks_of(kind, k):
                    last = pe.transpose(bank[T_BANK[k % 2]][:, b * P:(b + 1) * P], prob[:, k, b * P:(b + 1) * P], ident)
                last.then_inc(t_ready, 1)

            def pv(kind, it, k, e=0, v=None):
                tb = tb_of(k)
                pe.wait_ge(pt_act if k % 2 else pt_dve, 2 * it + k // 2 + 1)
                if k == 0 and kind in ("A", "B", "C"):
                    pe.wait_ge(o_ready, it)
                pt = prob_t[k % 2]
                if kind == "B":
                    for e_ in range(2):
                        bs = [b for b in blocks_of(kind, k) if b // 2 == e_]
                        for b in bs:
                            last = pe.matmul(bank[O_BANK][64 * e_:64 * e_ + 64, tb * P:(tb + 1) * P],
                                             v[:, tb - 1 + b % 2, 64:128], pt[:, b, :], start=(b == bs[0]), stop=(b == bs[-1]))
                elif kind in ("A", "C"):
                    bs = blocks_of(kind, k)
                    for b in bs:
                        last = pe.matmul(bank[O_BANK][:, tb * P:(tb + 1) * P], v[:, b, :], pt[:, b, :],
                                         start=(b == 0), stop=(b == bs[-1]))
                else:
                    bs = blocks_of(kind, k)
                    c = tb if kind == "A2" else k
                    for b in bs:
                        vb = b if kind == "A2" else 2 * k + b
                        last = pe.matmul(bank[O_BANK][64 * e:64 * e + 64, c * P:(c + 1) * P],
                                         v[:, vb, 64 * e:64 * e + 64], pt[:, b, :], start=(b == 0), stop=(b == bs[-1]))
                if k == 3:
                    last.then_inc(pv_ready, 1)

            def att1_part(kind, it, hs, par):
                q, kk, v = qb1[par], kb1[par], vb1[par]
                if hs == 0:
                    qk(kind, it, 0, q, kk)
                    qk(kind, it, 1, q, kk)
                elif hs == 1:
                    qk(kind, it, 2, q, kk)
                    qk(kind, it, 3, q, kk)
                    turn(kind, it, 0)
                    turn(kind, it, 1)
                elif hs == 2:
                    pv(kind, it, 0, 0, v)
                    pv(kind, it, 1, 0, v)
                    turn(kind, it, 2)
                    turn(kind, it, 3)
                else:
                    pv(kind, it, 2, 0, v)
                    pv(kind, it, 3, 0, v)

            pe.wait_ge(i_rel, 51)
            for kind, it0, n in (("B", 2, ITEMS_B), ("C", 8, ITEMS_C), ("A", 12, ITEMS_A)):
                with pe.Fori(0, n // 2) as i:
                    for par in range(2):
                        it = 2 * i + (it0 + par)
                        g = 2 * i + (G_MIX + 8 + it0 - 2 + par)
                        pe.wait_ge(it_loaded[par], 64 * i + 32 * it0)
                        for hs in range(4):
                            att1_part(kind, it, hs, par)
                            if hs == 0:
                                pe.wait_ge(ev_act, g - 1)
                            gemm_part(g, hs, act_a)
            meet(pe, 2)

            UP = ((0, 6, (0, 1)), (6, 10, (2, 3)), (10, 16, (4, 5)))
            def up_group(j, first=False):
                for s in range(2):
                    chunk_ready(pe, 2 * j + (2 * G_UP + s))
                    for kt in range(CK):
                        k = CK * s + kt
                        if first:
                            parts_split(pe, k, PARTS_1, 0)
                        c = 0 if k < 6 else 1 if k < 10 else 2
                        k0, k1, bk = UP[c]
                        if k == k0:
                            pe.wait_ge(up_ev, 3 * j + c + 1)
                        last = rows_t(pe, s, [kt], act_b, bk, k0, k1 - 1)
                        if k == k1 - 1 and c < 2:
                            last.then_inc(up_psum, 1)
                        if k == CK - 1:
                            last.then_inc(chunk_used, 1)
                    if s == 1:
                        last.then_inc(chunk_used, 1)

            def parts_split(pe, k, parts, before):
                for n, (k0, k1) in enumerate(parts):
                    if k == k0:
                        pe.wait_ge(oh_s, before + n + 1)
                        pe.wait_ge(olo_s, before + n + 1)

            up_group(0, first=True)
            with pe.Fori(1, 8) as j:
                up_group(j)

            def wo_group(i, s, last_tiles=False):
                g = 2 * i + (G_WO + s)
                pe.wait_ge(x1f_s, 4 * i + (2 * s + 2))
                for c in range(2):
                    if c == 1:
                        pe.wait_ge(xr_loaded[s], 16 * i + 16)
                        for n in range(2):
                            for b in range(TB):
                                pe.matmul(bank[2 * s + n][:, b * P:(b + 1) * P], xc[s][:, b, n * P:(n + 1) * P],
                                          ident, start=False, stop=False, skip_group_check=True)
                    chunk_ready(pe, 2 * g + c)
                    rows_t(pe, c, range(6), act_a, (2 * s, 2 * s + 1))
                    if c == 1 and last_tiles:
                        pe.wait_ge(up_hi, 8)
                        pe.wait_ge(up_lo, 9)
                    rows_t(pe, c, range(6, 8), act_a, (2 * s, 2 * s + 1)).then_inc(chunk_used, 1)

            pe.wait_ge(up_ev, 26)
            pe.wait_ge(up_hi, 7)
            pe.wait_ge(up_lo, 8)
            for s in range(2):
                wo_group(0, s, last_tiles=(s == 0))
            with pe.Fori(1, 4) as i:
                for s in range(2):
                    wo_group(i, s)

            def v_turn(kind, v, v_w, part):
                for x in range(4):
                    if kind == "A2":
                        src = v[:, x * P:(x + 1) * P]
                    else:
                        src = v_w[:, (4 * part + x) * P:(4 * part + x + 1) * P]
                    last = pe.transpose(bank[V_BANK][:, x * P:(x + 1) * P], src, ident)
                last.then_inc(vt_psum, 1)

            def att2_part(kind, i, it, hs, par, e):
                q, kk, v = qkvg[par][0], qkvg[par][1], v_tok[par]
                if hs == 0:
                    if e == 0:
                        pe.wait_ge(it_loaded[par], pair_loaded(i))
                        pe.wait_ge(vt_ready, vt_count(kind, i, par))
                    qk2(kind, it, 0, e, q, kk)
                    qk2(kind, it, 1, e, q, kk)
                elif hs == 1:
                    qk2(kind, it, 2, e, q, kk)
                    qk2(kind, it, 3, e, q, kk)
                    turn(kind, it, 0)
                    turn(kind, it, 1)
                elif hs == 2:
                    if e == 0:
                        pe.wait_ge(o_ready, outs_before(i, par))
                    pv(kind, it, 0, e, v)
                    pv(kind, it, 1, e, v)
                    turn(kind, it, 2)
                    turn(kind, it, 3)
                else:
                    pv(kind, it, 2, e, v)
                    pv(kind, it, 3, e, v)

            pe.wait_ge(x1f_s, 18)
            pe.wait_ge(x1h_s, 9)
            pe.wait_ge(x1l_s, 7)

            def quad(i, att, vt_next, gemm=True):
                for j in range(4):
                    par, e = j // 2, j % 2
                    nxt = (att, i, 1) if j == 1 and att else (vt_next, i + 1, 0) if j == 3 and vt_next else None
                    for hs in range(4):
                        if att:
                            att2_part(att, i, 4 * i + (14 + j), hs, par, e)
                        if nxt and (hs == 3 or (hs == 2 and nxt[0] == "N2")):
                            kind_n, i_n, par_n = nxt
                            if kind_n == "N2" and hs == 3:
                                pe.wait_ge(vt_ready, vt_count(kind_n, i_n, par_n) - 1)
                            elif kind_n == "N2":
                                pe.wait_ge(vw_ready, windows_ready(i_n, par_n))
                            else:
                                pe.wait_ge(it_loaded[par_n], pair_loaded(i_n))
                            v_turn(kind_n, qkvg[par_n][2], v_win[par_n], hs - 2 if kind_n == "N2" else 0)
                        if gemm:
                            g = 4 * i + (G_IN2 + j)
                            if hs == 0:
                                pe.wait_ge(ev_act, g - 17)
                                pe.wait_ge(ev_dve, g - 41)
                            if hs == 3 and j == 0 and not att:
                                pe.wait_ge(x1h_s, 10)
                                pe.wait_ge(x1l_s, 8)
                            gemm_part(g, hs, act_b)

            quad(0, None, "A2")
            with pe.Fori(1, 4) as i:
                quad(i, "A2", "A2")
            quad(4, "A2", "N2")
            with pe.Fori(5, 8) as i:
                quad(i, "N2", "N2")
            quad(8, "N2", None, gemm=False)
            meet(pe, 3)

            def out_group(g, s, i, first=False):
                pe.wait_ge(ev_act, g - 18)
                pe.wait_ge(ev_dve, g - 42)
                for c in range(2):
                    if c == 1:
                        pe.wait_ge(xr_loaded[s], 16 * i + 80)
                        for b in range(TB):
                            for n in range(2):
                                pe.matmul(bank[4 * s + b][:, n * P:(n + 1) * P], xr[s][:, n, b * P:(b + 1) * P], aident,
                                          start=False, stop=False, skip_group_check=True)
                    chunk_ready(pe, 2 * g + c)
                    for kt in range(CK):
                        k = CK * c + kt
                        if first:
                            parts_split(pe, k, PARTS_2, len(PARTS_1))
                        for b in range(TB):
                            dst = bank[4 * s + b][:, 0:GC]
                            for n, (l, r) in enumerate(((0, w_hi), (1, w_hi), (0, w_lo))):
                                last = pe.matmul(dst, act_b[l][:, k, b * P:(b + 1) * P], wt(r[c], kt, 0, GC),
                                                 start=(k == 0 and n == 0), stop=(k == KT - 1 and n == 2),
                                                 skip_group_check=True)
                    last.then_inc(chunk_used, 1)

            for s in range(2):
                out_group(G_OUT2 + s, s, 0, first=(s == 0))
            with pe.Fori(1, 4) as i:
                for s in range(2):
                    out_group(2 * i + (G_OUT2 + s), s, i)
            meet(pe, 4)


        @block.scalar
        def _(act):
            for first, n in ((e_ready, 8), (pt_act, 4), (i_rel, 3), (x1h_s, 2)):
                act.sem_inc(first, n)

            def copy(dst, src, **kw):
                return act.activation(dst, src, ACT.Copy, **kw)

            def squares(src, b, c):
                if c:
                    act.wait_ge(sq_s, c)
                act.activation(junk[:], src[:, b, :], ACT.Square, accum_out=ssq[:, c:c + 1]).then_inc(sq_s, 1)

            for b in range(TB):
                act.wait_ge(x_s[b], 16)
                squares(x_nat, b, b)
            act.wait_ge(rs_s, 1)
            act.activation(ssq[:, 0:TB], rstd[:, 0:TB], ACT.Sqrt).then_inc(rt_s, 1)

            def tr_hi(i):
                act.wait_ge(th_s, i + 1)
                m = i - KT
                dst = act_a[0][:, i, :] if m < 0 else mem_t[0][:, 2 * m:2 * m + 2, :].rearrange("p a b -> p (a b)")
                copy(dst, tr_h[i % 2][:]).then_inc(tt_s, 1)

            for i in range(KT):
                tr_hi(i)
                if i == 2:
                    split_hi(act, 0, 0, first=True)
                if i == 6:
                    split_hi(act, 1, 1, first=True)
                if i == 11:
                    for b in range(2):
                        act.wait_ge(mem_s[b], 16)
                        squares(mem_nat, b, TB + b)
                    act.wait_ge(rs_s, 3)
                    act.activation(ssq[:, TB:TB + 2], rstd[:, TB:TB + 2], ACT.Sqrt).then_inc(rt_s, 1)

            def hi2(g):
                split_hi(act, 2 * g + 1, 1)
                split_hi(act, 2 * g + 2, 0)

            def summed(g):
                act.wait_ge(chunk_used, 2 * g + 2)

            def root(n, width):
                act.wait_ge(ms_s, n)
                act.activation(ssk[:, 0:width], rsk[:, 0:width], ACT.Sqrt).then_inc(rt2_s, 1)

            def upper(g, dst, w, b0=2):
                summed(g)
                copy(dst[:, 2, 0:w], bank[b0][:, 0:w])
                copy(dst[:, 3, 0:w], bank[b0 + 1][:, 0:w]).then_inc(ev_act, 1)

            split_hi(act, 2, 0)
            upper(G_CKV, ckv_n, 256, 6)
            root(1, 4)
            split_hi(act, 3, 1)
            for m in range(3):
                tr_hi(KT + m)
            split_hi(act, 4, 0)
            upper(G_IK, ik_n, 80)
            for m in range(3, 6):
                tr_hi(KT + m)
            root(2, 4)
            split_hi(act, 5, 1)
            for m in range(6, 8):
                tr_hi(KT + m)
            act.wait_ge(sp_v, LATENT_READY)
            copy(ckv_t[0][:], ckv_f[:]).then_inc(sp_h, 1)
            split_hi(act, 6, 0)
            upper(G_BKV, bkv_n, 256)

            def kv_out(kind):
                for b in range(TB):
                    u = kind * TB + b
                    if b < TB - 1:
                        act.wait_ge(kv_psum, 3 * kind + b + 1)
                    else:
                        act.wait_ge(chunk_used, 2 * G_KVUP + kind + 1)
                    copy((v_nat if kind else k_nat)[:, b, 384:768], bank[2 * (u % 2) + 1][:, 0:384]).then_inc(kv_act, 1)

            split_hi(act, 7, 1)
            kv_out(0)
            split_hi(act, 8, 0)
            act.wait_ge(ml_s, 8)
            kv_out(1)
            root(3, 8)
            for m in range(4):
                g = G_MEM + m
                hi2(g)
                if m == 2:
                    root(4, 24)
                summed(g)
                dst = mem_kn if m < 2 else mem_vn
                copy(dst[:, 1, 256 * (m % 2):256 * (m % 2) + 256], bank[2 * (m % 2) + 1][:, 0:256]).then_inc(ev_act, 1)

            def proj_out(kind, g, i, s):
                hi2(g)
                b0, b1 = bank[2 * s], bank[2 * s + 1]
                if kind == "iq" and i == 0 and s == 0:
                    root(5, 8)
                summed(g)
                if kind == "iq":
                    act.wait_ge(staged_out[s], 16 * i + 16)
                    copy(stage[s][:, 0, :], b0[:]).then_inc(ev_act, 1)
                elif kind == "q":
                    act.wait_ge(qssq, 2 * i + (s + 1))
                    act.activation(sq_q[:, 0, :], b0[:], ACT.Square).then_inc(qsq, 1)
                    act.activation(sq_q[:, 1, :], b1[:], ACT.Square).then_inc(ev_act, 1)
                else:
                    act.wait_ge(qssq, 9)
                    act.wait_ge(ev_dve, g - 1)
                    act.activation(th_g[:, 0, :], b0[:], ACT.Tanh, scale=0.5).then_inc(gth, 1)
                    act.activation(th_g[:, 1, :], b1[:], ACT.Tanh, scale=0.5).then_inc(ev_act, 1)

            for i in range(2):
                for s in range(2):
                    proj_out("iq", 2 * i + (G_IQ + s), i, s)
            act.wait_ge(kst_v, 256)
            act.wait_ge(kst_k, 256)
            for kind, g0 in (("q", G_Q), ("gate", G_GATE)):
                with act.Fori(0, 4) as i:
                    for s in range(2):
                        proj_out(kind, 2 * i + (g0 + s), i, s)
            meet(act, 1)
            act.wait_ge(rq_s, 1)
            act.activation(ssq_q[:], rq[:], ACT.Sqrt).then_inc(rt_s, 1)

            def mix_out(g, i, par, t0):
                summed(g)
                act.wait_ge(staged_out[par], 8 * (g - par) - 48)
                for n in range(2):
                    last = act.activation(stage[par][:, n, :], bank[n][:], ACT.Tanh, scale=0.5,
                                          bias=half_b[:, bass.ds(4 * i + (2 * t0 + 2 * par + n), 1)])
                last.then_inc(ev_act, 1)

            with act.Fori(0, 4) as i:
                for par in range(2):
                    g, t = 2 * i + (G_MIX + par), 2 * i + par
                    for e in range(2):
                        for j in range(3):
                            ui = 6 * t + (3 + 3 * e + j)
                            w = P * (4 - j)
                            act.wait_ge(i_psum, ui + 1)
                            act.wait_ge(i_acc, ui - 2)
                            act.activation(prob[:, j, 0:w], bank[2 + j][:, 0:w], ACT.Relu).then_inc(i_rel, 1)
                        split_hi(act, 2 * g + (1 + e), 1 - e)
                    mix_out(g, i, par, 0)

            def exp(kind, it, k):
                u = 4 * it + k
                act.wait_ge(m_ready, u + 1)
                if kind == "B":
                    for e in range(2):
                        c0 = 256 * e + BAND0(k)
                        act.activation(prob[:, k, c0:256 * e + 256], prob[:, k, c0:256 * e + 256], ACT.Exp,
                                       bias=nmx[:, k, e:e + 1], accum_out=rs[:, k, e:e + 1])
                    act.activation(es[:, k, :], sd[:, k, :], ACT.Exp).then_inc(e_ready, 1)
                else:
                    w = width_of(kind, k)
                    act.activation(prob[:, k, 0:w], prob[:, k, 0:w], ACT.Exp, bias=nmx[:, k, 0:1],
                                   accum_out=rs[:, k, 0:1]).then_inc(e_ready, 1)

            def turned_act(kind, it, k):
                act.wait_ge(t_ready, 4 * it + k + 1)
                if kind == "B" and not tb_of(k):
                    for b in (1, 3):
                        last = copy(prob_t[1][:, b, :], bank[T_BANK[1]][:, b * P:(b + 1) * P])
                else:
                    n = len(blocks_of(kind, k))
                    last = copy(prob_t[1][:, 0:n, :], bank[T_BANK[1]][:, 0:n * P].rearrange("p (a b) -> p a b", b=P))
                last.then_inc(pt_act, 1)

            def att_act(kind, it, hs):
                if hs == 0:
                    exp(kind, it, 0)
                    exp(kind, it, 1)
                elif hs == 1:
                    exp(kind, it, 2)
                    exp(kind, it, 3)
                    turned_act(kind, it, 1)
                elif hs == 2:
                    turned_act(kind, it, 3)

            for kind, it0, n in (("B", 2, ITEMS_B), ("C", 8, ITEMS_C), ("A", 12, ITEMS_A)):
                with act.Fori(0, n // 2) as i:
                    for par in range(2):
                        it = 2 * i + (it0 + par)
                        g = 2 * i + (G_MIX + 6 + it0 + par)
                        for hs in range(4):
                            att_act(kind, it, hs)
                            if hs == 0:
                                split_hi(act, 2 * g + 1, 1)
                            elif hs == 2:
                                split_hi(act, 2 * g + 2, 0)
                        mix_out(g, i, par, 6 + it0)
            meet(act, 2)

            def part_hi(parts, p, loads):
                k0, k1 = parts[p]
                act.wait_ge(ol_s[p], 16 * loads)
                copy(act_b[0][:, k0:k1, :], o_raw[:, k0:k1, :]).then_inc(oh_s, 1)

            for p in range(len(PARTS_1)):
                part_hi(PARTS_1, p, 1)
            with act.Fori(0, 8) as j:
                g = j + G_UP
                hi2(g)
                act.wait_ge(up_ch, 5 * j + 5)
                copy(act_a[0][:, bass.ds(2 * j, 2), :], m_acc[:], scale=0.5).then_inc(up_hi, 1)

            with act.Fori(0, 4) as i:
                for s in range(2):
                    g = 2 * i + (G_WO + s)
                    hi2(g)
                    act.wait_ge(x1f_s, 4 * i + (2 * s + 6))
                    copy(act_b[0][:, bass.ds(4 * i + 2 * s, 2), :], stage[s][:]).then_inc(x1h_s, 1)

            def proj2_out(g, i, j, att):
                s = j % 2
                summed(g)
                if j < 3:
                    act.wait_ge(staged_out[s], staged_before(i, j))
                    dst, src = stage[s][:, 0, :], bank[0][:]
                    if j == 0:
                        dst, src = q_rows(i, att, dst, src)
                    copy(dst, src, scale=HD2 ** -0.5 if j == 0 else 1.0).then_inc(ev_act, 1)
                else:
                    act.activation(th_2[:, 0, :], bank[0][:], ACT.Tanh, scale=0.5).then_inc(gth, 1)
                    act.activation(th_2[:, 1, :], bank[1][:], ACT.Tanh, scale=0.5).then_inc(ev_act, 1)

            def v_turned(kind_n, i_n, par_n, part):
                act.wait_ge(vt_psum, vt_count(kind_n, i_n, par_n) - (1 - part if kind_n == "N2" else 0))
                copy(v_tok[par_n][:, 4 * part:4 * part + 4, :],
                     bank[V_BANK][:].rearrange("p (a b) -> p a b", b=P)).then_inc(vt_ready, 1)

            def quad(i, att, vt_next, gemm=True):
                for j in range(4):
                    g = 4 * i + (G_IN2 + j)
                    nxt = (att, i, 1) if j == 1 and att else (vt_next, i + 1, 0) if j == 3 and vt_next else None
                    for hs in range(4):
                        if att:
                            att_act(att, 4 * i + (14 + j), hs)
                        if nxt and nxt[0] == "N2" and hs >= 2:
                            v_turned(*nxt, hs - 2)
                        elif nxt and hs == 3:
                            v_turned(*nxt, 0)
                        if gemm and hs == 0:
                            split_hi(act, 2 * g + 1, 1)
                        elif gemm and hs == 2:
                            split_hi(act, 2 * g + 2, 0)
                    if gemm:
                        proj2_out(g, i, j, att)
                    elif j:
                        part_hi(PARTS_2, j - 1, 2)

            for s in range(2):
                act.wait_ge(x1_out[s], 80)
            quad(0, None, "A2")
            with act.Fori(1, 4) as i:
                quad(i, "A2", "A2")
            quad(4, "A2", "N2")
            with act.Fori(5, 8) as i:
                quad(i, "N2", "N2")
            quad(8, "N2", None, gemm=False)
            meet(act, 3)

            for p in (3, 4):
                part_hi(PARTS_2, p, 2)

            def rows_out(i, s, last_group=False):
                g = 2 * i + (G_OUT2 + s)
                split_hi(act, 2 * g + 1, 1)
                if not last_group:
                    split_hi(act, 2 * g + 2, 0)
                summed(g)
                for b in range(2):
                    last = copy(z[:, b, bass.ds(512 * i + 256 * s, 256)], bank[4 * s + b][:, 0:GC])
                last.then_inc(ev_act, 1)

            with act.Fori(0, 3) as i:
                for s in range(2):
                    rows_out(i, s)
            rows_out(3, 0)
            rows_out(3, 1, last_group=True)
            act.wait_ge(ln_s, LN_VAR)
            act.activation(ssk[:, 0:TB], rsk[:, 0:TB], ACT.Sqrt).then_inc(rt2_s, 1)
            for b in range(TB):
                act.wait_ge(ln_s, LN_NMR)
                act.activation(z[:, b, :], z[:, b, :], ACT.Identity, scale=rsk[:, b:b + 1],
                               bias=nmr[:, b:b + 1]).then_inc(ln_a, 1)
            meet(act, 4)

        @block.vector
        def _(dve):
            for first, n in ((l_ready, 8), (m_ready, 8), (p_ready, 8), (pt_dve, 4), (o_ready, 2), (i_acc, 3),
                             (up_ev, 3), (up_lo, 1), (x1f_s, 4), (qcp, 2)):
                dve.sem_inc(first, n)

            def scaled(dst, src, by):
                return dve.tensor_scalar(dst, src, by, None, ALU.mult)

            for n, (heads, a, b, dst) in enumerate(BIAS_JOBS):
                dve.wait_ge(pb_s, n + 1)
                dve.tensor_copy(dst, bank[n][0:dst.shape[0], 0:b - a]).then_inc(pe_s, 1)
            dve.wait_ge(con_s, 80)
            scaled(half_b[:], pcol("gate_b", 0, 48), 0.5)
            scaled(qgs[:, 0:6], pcol("q_g", 0, 6), 64 ** -0.5)
            scaled(qgs[:, 6:16], pcol("q_g", 6, 10), 128 ** -0.5)

            def token_rstd(c0, n, base, squares):
                dve.wait_ge(sq_s, squares)
                dve.tensor_scalar(rstd[:, c0:c0 + n], ssq[:, c0:c0 + n], 1.0 / D, EPS, ALU.mult, ALU.add).then_inc(rs_s, 1)
                dve.wait_ge(rt_s, base // 2 + 1)
                dve.reciprocal(rstd[:, c0:c0 + n], ssq[:, c0:c0 + n]).then_inc(rs_s, 1)
                dve.wait_ge(rs_s, base + 2)
                for b in range(n):
                    last = scaled(rdiag[:, c0 + b, :], ident, rstd[:, c0 + b:c0 + b + 1])
                last.then_inc(rd_s, 1)

            token_rstd(0, TB, 0, TB)
            dve.wait_ge(rb_s, 1)
            dve.tensor_copy(rbc[:, 0:T], bank[6][:]).then_inc(rbc_s, 1)

            def tr_scale(i):
                m = i - KT
                dve.wait_ge(tr_s, i + 1)
                dve.wait_ge(rbc_s, 1 if m < 0 else 2)
                if i >= 2:
                    dve.wait_ge(tt_s, i - 1)
                    if m < 2:
                        dve.wait_ge(tl_s, i - 1)
                    else:
                        dve.wait_ge(ml_s, m - 1)
                if m < 0:
                    dve.scalar_tensor_tensor(out=tr_h[i % 2][:], in0=bank[i % 4][:], scalar=pcol("norm_g", i),
                                             in1=rbc[:, 0:T], op0=ALU.mult, op1=ALU.mult).then_inc(th_s, 1)
                else:
                    for n in range(2):
                        c = slice(n * MEM, (n + 1) * MEM)
                        last = dve.scalar_tensor_tensor(out=tr_h[i % 2][:, c], in0=bank[5 + m % 3][:, c],
                                                        scalar=pcol("mem_g", 2 * m + n), in1=rbc[:, T:T + MEM],
                                                        op0=ALU.mult, op1=ALU.mult)
                    last.then_inc(th_s, 1)

            def tr_lo(i):
                dve.wait_ge(tt_s, i + 1)
                dve.tensor_tensor(act_a[1][:, i, :], tr_h[i % 2][:], act_a[0][:, i, :].bitcast(F32), ALU.subtract)\
                    .then_inc(tl_s, 1)

            tr_scale(0)
            for i in range(KT):
                if i + 1 < KT:
                    tr_scale(i + 1)
                tr_lo(i)
                if i == 2:
                    split_lo(dve, 0, 0)
                if i == 6:
                    split_lo(dve, 1, 1)
                if i == 11:
                    token_rstd(TB, 2, 2, TB + 2)

            n_sp = [0]

            def link(ins):
                n_sp[0] += 1
                ins.then_inc(sp_v, 1)
                dve.wait_ge(sp_v, n_sp[0])

            def lo2(g):
                split_lo(dve, 2 * g + 1, 1)
                split_lo(dve, 2 * g + 2, 0)

            def summed(g):
                dve.wait_ge(chunk_used, 2 * g + 2)

            def lower(g, dst, w, b0=0):
                summed(g)
                dve.tensor_copy(dst[:, 0, 0:w], bank[b0][:, 0:w])
                dve.tensor_copy(dst[:, 1, 0:w], bank[b0 + 1][:, 0:w]).then_inc(ev_dve, 1)

            def both_read(n):
                dve.wait_ge(ev_dve, n)
                dve.wait_ge(ev_act, n)

            def means(width, count):
                dve.tensor_scalar(rsk[:, 0:width], ssk[:, 0:width], 1.0 / count, EPS, ALU.mult, ALU.add).then_inc(ms_s, 1)

            def inverse(n, width):
                dve.wait_ge(rt2_s, n)
                link(dve.reciprocal(rsk[:, 0:width], ssk[:, 0:width]))

            def inv_root(n, width, count):
                means(width, count)
                inverse(n, width)

            def sum_sq(src, heads, dim, c0=0):
                sq = sq_w[:, 0:heads * dim].rearrange("p (h d) -> p h d", d=dim)
                link(dve.tensor_tensor(sq, src, src, ALU.mult))
                link(dve.tensor_reduce(ssk[:, c0:c0 + heads], sq, AX.X, ALU.add))

            split_lo(dve, 2, 0)
            lower(G_CKV, ckv_n, 256, 4)
            both_read(1)
            sum_sq(ckv_n[:], TB, 256)
            inv_root(1, TB, KV_RANK)
            for b in range(TB):
                last = scaled(ckv_n[:, b, :], ckv_n[:, b, :], rsk[:, b:b + 1])
            last.then_inc(sp_c, 1)
            split_lo(dve, 3, 1)
            dve.wait_ge(rb_s, 2)
            dve.tensor_copy(rbc[:, T:T + MEM], bank[4][:, 0:MEM]).then_inc(rbc_s, 1)
            for m in range(3):
                tr_scale(KT + m)
            split_lo(dve, 4, 0)
            lower(G_IK, ik_n, 80)
            for m in range(3, 6):
                tr_scale(KT + m)
            both_read(2)
            for b in range(TB):
                last = dve.bn_stats(stats[:, b, :], ik_n[:, b, 0:64])
            link(last)
            for b in range(TB):
                last = dve.bn_aggr(mv[:, b, :], stats[:, b, :])
            link(last)
            link(dve.tensor_copy(ssk[:, 0:TB], mv[:, :, 1]))
            inv_root(2, TB, 1)
            for b in range(TB):
                scaled(iw[:, 16 * b:16 * b + 16], ik_n[:, b, 64:80], (IDX_HEADS * IDX_DIM) ** -0.5)
                for e in range(2):
                    last = dve.tensor_scalar(ik_d[:, b, e, :], ik_n[:, b, 0:64], mv[:, b, 0:1], rsk[:, b:b + 1],
                                             ALU.subtract, ALU.mult)
            last.then_inc(sp_c, 1)
            split_lo(dve, 5, 1)
            for m in range(6, 8):
                tr_scale(KT + m)
            dve.wait_ge(sp_t, 1)
            scaled(ckv_f[:, 0, :], bank[4][:], pcol("kv_g", 0))
            link(scaled(ckv_f[:, 1, :], bank[5][:], pcol("kv_g", 1)))
            assert n_sp[0] == LATENT_READY, n_sp
            dve.wait_ge(sp_h, 1)
            dve.tensor_tensor(ckv_t[1][:], ckv_f[:], ckv_t[0][:].bitcast(F32), ALU.subtract).then_inc(sp_l, 1)
            split_lo(dve, 6, 0)
            lower(G_BKV, bkv_n, 256)

            def kv_out(kind):
                for b in range(TB):
                    u = kind * TB + b
                    if b < TB - 1:
                        dve.wait_ge(kv_psum, 3 * kind + b + 1)
                    else:
                        dve.wait_ge(chunk_used, 2 * G_KVUP + kind + 1)
                    dve.tensor_copy((v_nat if kind else k_nat)[:, b, 0:384], bank[2 * (u % 2)][:, 0:384]).then_inc(kv_dve, 1)

            split_lo(dve, 7, 1)
            kv_out(0)
            split_lo(dve, 8, 0)
            dve.wait_ge(ml_s, 8)
            kv_out(1)
            both_read(3)
            sq = sq_w[:, 0:512].rearrange("p (b c) -> p b c", c=128)
            link(dve.tensor_tensor(sq, bkv_n[:, :, 0:128], bkv_n[:, :, 0:128], ALU.mult))
            link(dve.tensor_reduce(ssk[:, 0:8], sq_w[:, 0:512].rearrange("p (h d) -> p h d", d=64), AX.X, ALU.add))
            inv_root(3, 8, 64)
            for b in range(TB):
                for kv in range(2):
                    for e in range(2):
                        last = scaled(kb_n[:, b, kv, e, :], bkv_n[:, b, 64 * kv:64 * kv + 64], rsk[:, 2 * b + kv:2 * b + kv + 1])
            last.then_inc(sp_c, 1)
            dve.wait_ge(sp_t, 2)
            dve.tensor_scalar(ik_t[:], bank[6][:], pcol("ik_g"), pcol("ik_b"), ALU.mult, ALU.add).then_inc(sp_o, 2)

            for m in range(4):
                g = G_MEM + m
                lo2(g)
                if m == 1:
                    dve.wait_ge(kv_act, TB)
                    dve.wait_ge(kv_dve, TB)
                    for b in range(TB):
                        sum_sq(k_nat[:, b, :].rearrange("p (h d) -> p h d", d=P), HEADS_A, P, HEADS_A * b)
                    means(24, P)
                if m == 2:
                    dve.wait_ge(sp_t, 3)
                    dve.wait_ge(sp_l, 1)
                    for kv in range(2):
                        last = scaled(kt_b[:, kv, :], bank[4 + kv][:], pcol("k_b"))
                    last.then_inc(sp_o, 1)
                    inverse(4, 24)
                    for b in range(TB):
                        for h in range(HEADS_A):
                            c = k_nat[:, b, h * P:(h + 1) * P]
                            last = scaled(c, c, rsk[:, 6 * b + h:6 * b + h + 1])
                    last.then_inc(sp_c, 1)
                summed(g)
                dst = mem_kn if m < 2 else mem_vn
                dve.tensor_copy(dst[:, 0, 256 * (m % 2):256 * (m % 2) + 256], bank[2 * (m % 2)][:, 0:256]).then_inc(ev_dve, 1)

            def proj_out(kind, g, i, s):
                summed(g)
                dve.wait_ge(staged_out[s], 16 * i + (16 if kind == "iq" else 48 if kind == "q" else 112))
                b0, b1 = bank[2 * s], bank[2 * s + 1]
                if kind == "iq":
                    dve.tensor_copy(stage[s][:, 1, :], b1[:]).then_inc(ev_dve, 1)
                elif kind == "q":
                    dve.wait_ge(qsq, 2 * i + (s + 1))
                    scaled(stage[s][:, 0, :], b0[:], qgs[:, bass.ds(4 * i + 2 * s, 1)])
                    dve.wait_ge(ev_act, g)
                    scaled(stage[s][:, 1, :], b1[:], qgs[:, bass.ds(4 * i + (2 * s + 1), 1)]).then_inc(ev_dve, 1)
                else:
                    for n_, (sm, v) in enumerate(((gth, 2 * i + (s + 1)), (ev_act, g))):
                        dve.wait_ge(sm, v)
                        last = dve.scalar_tensor_tensor(out=stage[s][:, n_, :], in0=th_g[:, n_, :], scalar=1.0,
                                                        in1=(b0, b1)[n_][:], op0=ALU.add, op1=ALU.mult)
                    last.then_inc(ev_dve, 1)

            def ssq_out(i, s):
                dve.wait_ge(qssq, 2 * i + (s + 2))
                dve.tensor_copy(ssq_q[:, bass.ds(32 * i + 16 * s, 16)], bank[4 + s][:, 0:16]).then_inc(qcp, 1)

            split_lo(dve, 2 * G_IQ + 1, 1)
            dve.wait_ge(sp_l, 1)
            for b in range(TB):
                dve.wait_ge(sp_t, 4 + b)
                bk = 4 + 2 * (b % 2)
                cols = slice(b * P, (b + 1) * P)
                scaled(kt_a[:, 0:4, cols], bank[bk][:].rearrange("p (h t) -> p h t", t=P), pcol("k_a"))
                scaled(kt_a[:, 4:6, cols], bank[bk + 1][:, 0:256].rearrange("p (h t) -> p h t", t=P), pcol("k_a"))\
                    .then_inc(sp_o, 1)
            split_lo(dve, 2 * G_IQ + 2, 0)
            both_read(5)
            sum_sq(mem_kn[:].rearrange("p b (h d) -> p (b h) d", d=P), 8, P)
            inv_root(5, 8, P)
            for b in range(2):
                for h in range(HEADS_C):
                    c = mem_kn[:, b, h * P:(h + 1) * P]
                    last = scaled(c, c, rsk[:, 4 * b + h:4 * b + h + 1])
            last.then_inc(sp_c, 1)
            proj_out("iq", G_IQ, 0, 0)
            lo2(G_IQ + 1)
            dve.wait_ge(sp_t, 8)
            for n in range(2):
                last = scaled(kt_c[:, 2 * n:2 * n + 2, :], bank[4 + n][:].rearrange("p (h t) -> p h t", t=MEM), pcol("k_c"))
            last.then_inc(sp_o, 1)
            proj_out("iq", G_IQ + 1, 0, 1)
            dve.memset(score[:], 0.0).then_inc(zero_s, 1)
            for s in range(2):
                lo2(G_IQ + 2 + s)
                proj_out("iq", G_IQ + 2 + s, 1, s)
            for s in range(2):
                lo2(G_Q + s)
                if s == 1:
                    ssq_out(0, 0)
                proj_out("q", G_Q + s, 0, s)
            with dve.Fori(1, 4) as i:
                for s in range(2):
                    g = 2 * i + (G_Q + s)
                    lo2(g)
                    ssq_out(*((i - 1, 1) if s == 0 else (i, 0)))
                    proj_out("q", g, i, s)
            lo2(G_GATE)
            ssq_out(3, 1)
            dve.wait_ge(qcp, 10)
            dve.tensor_scalar(rq[:, 0:48], ssq_q[:, 0:48], 1.0 / 64, EPS, ALU.mult, ALU.add)
            dve.tensor_scalar(rq[:, 48:128], ssq_q[:, 48:128], 1.0 / 128, EPS, ALU.mult, ALU.add).then_inc(rq_s, 1)
            proj_out("gate", G_GATE, 0, 0)
            lo2(G_GATE + 1)
            proj_out("gate", G_GATE + 1, 0, 1)
            with dve.Fori(1, 4) as i:
                for s in range(2):
                    g = 2 * i + (G_GATE + s)
                    lo2(g)
                    proj_out("gate", g, i, s)
            meet(dve, 1)

            dve.wait_ge(zero_s, 1)
            with dve.Fori(0, 4) as i:
                for par in range(2):
                    g, t = 2 * i + (G_MIX + par), 2 * i + par
                    for e in range(2):
                        for j in range(3):
                            ui, tb = 6 * t + (3 + 3 * e + j), 3 - j
                            w = P * (tb + 1)
                            dve.wait_ge(i_rel, ui + 1)
                            dve.wait_ge(i_acc, ui - 2)
                            dve.scalar_tensor_tensor(out=score[:, tb, 0:w], in0=prob[:, j, 0:w],
                                                     scalar=iw[:, bass.ds(4 * i + (16 * tb + 2 * par + e), 1)],
                                                     in1=score[:, tb, 0:w], op0=ALU.mult, op1=ALU.add).then_inc(i_acc, 1)
                        split_lo(dve, 2 * g + (1 + e), 1 - e)

            def pick(n_rounds, base):
                for r in range(n_rounds):
                    dve.wait_ge(topk_s, base + 6 * r)
                    dve.nop(nofuse=True)
                    for tb in range(1, TB):
                        dve.max(top8[:, tb - 1, :], score[:, tb, 0:P * (tb + 1)]).then_inc(topk_s, 1)
                    dve.wait_ge(topk_s, base + (6 * r + 3))
                    dve.nop(nofuse=True)
                    for tb in range(1, TB):
                        w = P * (tb + 1)
                        dve.match_replace(score[:, tb, 0:w], top8[:, tb - 1, :], score[:, tb, 0:w], TAKEN).then_inc(topk_s, 1)

            def soft_a(kind, it, k, rqc=None, par=0, sink=None):
                u, tb = 4 * it + k, tb_of(k)
                w, dst, src = width_of(kind, k), prob[:, k, :], bank[Q_BANK[k % 2]]
                dve.wait_ge(s_ready, u + 1)
                if kind in ("A2", "N2"):
                    dve.nop(nofuse=True)
                if kind == "B":
                    c0 = BAND0(k)
                    for e in range(2):
                        c, cb = slice(256 * e + c0, 256 * e + 256), slice(ROW_B * e + c0, ROW_B * e + 256)
                        last = dve.scalar_tensor_tensor(out=dst[:, c], in0=src[:, c], scalar=rqc(tb, e), in1=bb1[par][:, cb],
                                                        op0=ALU.mult, op1=ALU.add)
                    last.then_inc(l_ready, 1)
                    dve.wait_ge(l_ready, u + 1)
                    b0 = 3 * (u - 8) if isinstance(u, int) else 3 * u - 24
                    dve.tensor_reduce(mx[:, k, :], dst.rearrange("p (e c) -> p e c", e=2)[:, :, c0:256], AX.X, ALU.max)\
                        .then_inc(va, 1)
                    dve.wait_ge(va, b0 + 1)
                    dve.tensor_tensor(mx2[:, k, :], mx[:, k, :], sink, ALU.max).then_inc(va, 1)
                    dve.wait_ge(va, b0 + 2)
                    scaled(nmx[:, k, :], mx2[:, k, :], -1.0).then_inc(va, 1)
                    dve.wait_ge(va, b0 + 3)
                    dve.tensor_tensor(sd[:, k, :], sink, nmx[:, k, :], ALU.add).then_inc(m_ready, 1)
                    return
                if kind == "A":
                    dve.scalar_tensor_tensor(out=dst[:, 0:w], in0=src[:, 0:w], scalar=rqc(tb, 0),
                                             in1=bb1[par][:, 384 - P * tb:384 - P * tb + w], op0=ALU.mult, op1=ALU.add).then_inc(va, 1)
                    dve.wait_ge(va, u + 25)
                    dve.nop(nofuse=True)
                    dve.tensor_tensor_reduce(out=dst[:, 0:w], in0=dst[:, 0:w], in1=score[:, tb, 0:w], scale=1.0,
                                             scalar=-3.4e38, op0=ALU.add, op1=ALU.max, accum_out=mx[:, k, 0:1]).then_inc(l_ready, 1)
                elif kind == "C":
                    dve.tensor_scalar(dst[:, 0:w], src[:, 0:w], rqc(tb, 0), -3.4e38, ALU.mult, ALU.max,
                                      accum_out=mx[:, k, 0:1]).then_inc(l_ready, 1)
                elif kind == "A2":
                    dve.tensor_tensor_reduce(out=dst, in0=src[:], in1=b2[par][:, 384 - P * tb:896 - P * tb], scale=1.0,
                                             scalar=-3.4e38, op0=ALU.add, op1=ALU.max, accum_out=mx[:, k, 0:1]).then_inc(l_ready, 1)
                else:
                    dve.tensor_tensor_reduce(out=dst[:, 0:w], in0=src[:, 0:w],
                                             in1=nb[par][:, k, :, :].rearrange("p a b -> p (a b)"), scale=1.0,
                                             scalar=-3.4e38, op0=ALU.add, op1=ALU.max, accum_out=mx[:, k, 0:1]).then_inc(l_ready, 1)
                dve.wait_ge(l_ready, u + 1)
                scaled(nmx[:, k, 0:1], mx[:, k, 0:1], -1.0).then_inc(m_ready, 1)

            def soft_b(kind, it, k):
                u = 4 * it + k
                dve.wait_ge(e_ready, u + 1)
                if kind == "B":
                    dve.tensor_tensor(den[:, k, :], rs[:, k, :], es[:, k, :], ALU.add).then_inc(vb, 1)
                    dve.wait_ge(vb, 2 * u - 15)
                    dve.reciprocal(rden[:, k, :], den[:, k, :]).then_inc(vb, 1)
                    dve.wait_ge(vb, 2 * u - 14)
                    for e in range(2):
                        c = slice(256 * e + BAND0(k), 256 * e + 256)
                        last = scaled(prob[:, k, c], prob[:, k, c], rden[:, k, e:e + 1])
                else:
                    w = width_of(kind, k)
                    dve.reciprocal(rden[:, k, 0:1], rs[:, k, 0:1]).then_inc(vb, 1)
                    dve.wait_ge(vb, u + 17)
                    last = scaled(prob[:, k, 0:w], prob[:, k, 0:w], rden[:, k, 0:1])
                last.then_inc(p_ready, 1)

            def turned_dve(kind, it, k):
                dve.wait_ge(t_ready, 4 * it + k + 1)
                n = len(blocks_of(kind, k))
                dve.tensor_copy(prob_t[0][:, 0:n, :], bank[T_BANK[0]][:, 0:n * P].rearrange("p (a b) -> p a b", b=P))\
                    .then_inc(pt_dve, 1)

            def att_dve(kind, it, hs, **kw):
                if hs == 0:
                    soft_a(kind, it, 0, **kw)
                    soft_a(kind, it, 1, **kw)
                    soft_b(kind, it, 0)
                    soft_b(kind, it, 1)
                elif hs == 1:
                    soft_a(kind, it, 2, **kw)
                    soft_a(kind, it, 3, **kw)
                    turned_dve(kind, it, 0)
                    soft_b(kind, it, 2)
                    soft_b(kind, it, 3)
                elif hs == 2:
                    turned_dve(kind, it, 2)

            for kind, it0, n in (("B", 2, ITEMS_B), ("C", 8, ITEMS_C), ("A", 12, ITEMS_A)):
                if kind == "B":
                    dve.wait_ge(rt_s, 3)
                    dve.reciprocal(rq[:], ssq_q[:]).then_inc(rq_s, 1)
                    dve.wait_ge(rq_s, 2)
                    dve.wait_ge(cz_s, 3)
                    dve.sem_inc(topk_s, 1)
                if kind == "A":
                    dve.wait_ge(topk_s, 97)
                    for tb in range(1, TB):
                        w = P * (tb + 1)
                        last = dve.tensor_scalar(score[:, tb, 0:w], score[:, tb, 0:w], -3.2e38, NEG, ALU.is_gt, ALU.mult)
                    last.then_inc(topk_s, 1)
                    dve.wait_ge(topk_s, 98)
                with dve.Fori(0, n // 2) as i:
                    for par in range(2):
                        it = 2 * i + (it0 + par)
                        g = 2 * i + (G_MIX + 6 + it0 + par)
                        ri = 16 * i + (8 * (it0 - 2))
                        dve.wait_ge(it_loaded[par], 64 * i + 32 * it0)
                        if kind == "B":
                            dve.wait_ge(b_loaded[par], 16 * i + 16)
                        if kind == "A":
                            dve.wait_ge(b_loaded[par], 16 * i + 64)
                        kw = {"par": par, "rqc": lambda tb, e: rq[:, bass.ds(ri + (4 * tb + 2 * par + e), 1)],
                              "sink": params[:, bass.ds(4 * i + (PAR["sink"][0] + 2 * par), 2)]}
                        for hs in range(4):
                            att_dve(kind, it, hs, **kw)
                            if hs == 0:
                                split_lo(dve, 2 * g + 1, 1)
                            elif hs == 2:
                                split_lo(dve, 2 * g + 2, 0)
                                if kind == "B":
                                    pick(1, 24 * i + (12 * par + 1))
                            elif hs == 3 and kind == "B":
                                pick(1, 24 * i + (12 * par + 7))
                            if hs == 2:
                                if kind == "C":
                                    pick(1, 12 * i + (6 * par + 73))
                        dve.wait_ge(pv_ready, it + 1)
                        dve.wait_ge(o_out[par], 16 * i + 8 * it0)
                        dve.scalar_tensor_tensor(out=o_st[par][:], in0=bank[O_BANK][:], scalar=0.5, in1=gb1[par][:],
                                                 op0=ALU.mult, op1=ALU.mult).then_inc(o_ready, 1)
            meet(dve, 2)

            def part_lo(parts, p, before):
                k0, k1 = parts[p]
                dve.wait_ge(oh_s, before + p + 1)
                dve.tensor_tensor(act_b[1][:, k0:k1, :], o_raw[:, k0:k1, :], act_b[0][:, k0:k1, :].bitcast(F32),
                                  ALU.subtract).then_inc(olo_s, 1)

            for p in range(len(PARTS_1)):
                part_lo(PARTS_1, p, 0)
            with dve.Fori(0, 8) as j:
                g = j + G_UP

                def gated(c, dst):
                    for n in range(2):
                        last = dve.scalar_tensor_tensor(out=dst[:, n, :], in0=mixg[:, c, n, :], scalar=1.0,
                                                        in1=bank[2 * c + n][:], op0=ALU.add, op1=ALU.mult)
                    last.then_inc(up_ev, 1)

                split_lo(dve, 2 * g + 1, 1)
                dve.wait_ge(mg_loaded, 16 * j + 16)
                dve.wait_ge(up_psum, 2 * j + 1)
                dve.wait_ge(up_lo, j + 1)
                gated(0, m_acc)
                split_lo(dve, 2 * g + 2, 0)
                dve.wait_ge(up_psum, 2 * j + 2)
                gated(1, m_tmp)
                dve.wait_ge(up_ev, 3 * j + 5)
                dve.tensor_tensor(m_acc[:], m_acc[:], m_tmp[:], ALU.add).then_inc(up_ch, 1)
                dve.wait_ge(up_ch, 5 * j + 1)
                summed(g)
                gated(2, m_tmp)
                dve.wait_ge(up_ev, 3 * j + 6)
                dve.tensor_tensor(m_acc[:], m_acc[:], m_tmp[:], ALU.add).then_inc(up_ch, 4)
                dve.wait_ge(up_hi, j + 1)
                dve.scalar_tensor_tensor(out=act_a[1][:, bass.ds(2 * j, 2), :].rearrange("p a b -> p (a b)"),
                                         in0=m_acc[:].rearrange("p a b -> p (a b)"), scalar=0.5,
                                         in1=act_a[0][:, bass.ds(2 * j, 2), :].rearrange("p a b -> p (a b)").bitcast(F32),
                                         op0=ALU.mult, op1=ALU.subtract).then_inc(up_lo, 1)

            with dve.Fori(0, 4) as i:
                for s in range(2):
                    g = 2 * i + (G_WO + s)
                    lo2(g)
                    summed(g)
                    dve.wait_ge(x1_out[s], 16 * i + 16)
                    dve.wait_ge(x1h_s, 2 * i + (s + 1))
                    for n in range(2):
                        dve.tensor_copy(stage[s][:, n, :], bank[2 * s + n][:]).then_inc(x1f_s, 1)
                    dve.wait_ge(x1h_s, 2 * i + (s + 3))
                    dve.tensor_tensor(act_b[1][:, bass.ds(4 * i + 2 * s, 2), :], stage[s][:],
                                      act_b[0][:, bass.ds(4 * i + 2 * s, 2), :].bitcast(F32), ALU.subtract).then_inc(x1l_s, 1)

            def proj2_out(g, i, j, att):
                s = j % 2
                summed(g)
                dve.wait_ge(staged_out[s], staged_before(i, j))
                if j < 3:
                    ins = scaled(*q_rows(i, att, stage[s][:, 1, :], bank[1][:]), HD2 ** -0.5) if j == 0 else \
                        dve.tensor_copy(stage[s][:, 1, :], bank[1][:])
                    ins.then_inc(ev_dve, 1)
                else:
                    for n, (sm, v) in enumerate(((gth, gate2_tanh(i)), (ev_act, g - 16))):
                        dve.wait_ge(sm, v)
                        last = dve.scalar_tensor_tensor(out=stage[s][:, n, :], in0=th_2[:, n, :], scalar=1.0,
                                                        in1=bank[n][:], op0=ALU.add, op1=ALU.mult)
                    last.then_inc(ev_dve, 1)

            def quad(i, att, gemm=True):
                for j in range(4):
                    par, e = j // 2, j % 2
                    it = 4 * i + (14 + j)
                    g = 4 * i + (G_IN2 + j)
                    if att:
                        if att == "A2":
                            dve.wait_ge(b_loaded[e], bias2_loaded(i, j))
                        else:
                            dve.wait_ge(nb_ready[e], nb_count(i, j))
                    for hs in range(4):
                        if att:
                            att_dve(att, it, hs, par=e)
                        if gemm and hs == 0:
                            split_lo(dve, 2 * g + 1, 1)
                        elif gemm and hs == 2:
                            split_lo(dve, 2 * g + 2, 0)
                    if att and e == 1:
                        dve.wait_ge(pv_ready, it + 1)
                        dve.wait_ge(g2_loaded[par], 16 * i)
                        dve.wait_ge(o_out[par], 16 * i + 128)
                        if att == "A2":
                            last = dve.scalar_tensor_tensor(out=o_st[par][:], in0=bank[O_BANK][:], scalar=0.5,
                                                            in1=qkvg[par][3][:], op0=ALU.mult, op1=ALU.mult)
                        else:
                            for cb in range(4):
                                ov, gv = (t[:].rearrange("p (r c) -> p r c", c=64)[:, :, 16 * cb:16 * cb + 16]
                                          for t in (o_st[par], qkvg[par][3]))
                                last = dve.scalar_tensor_tensor(
                                    out=ov, in0=bank[O_BANK][:, P * cb:P * cb + P].rearrange("p (r c) -> p r c", c=16),
                                    scalar=0.5, in1=gv, op0=ALU.mult, op1=ALU.mult)
                        last.then_inc(o_ready, 1)
                    if gemm:
                        proj2_out(g, i, j, att)
                    elif j:
                        part_lo(PARTS_2, j - 1, len(PARTS_1))

            for s in range(2):
                dve.wait_ge(x1_out[s], 80)
            quad(0, None)
            with dve.Fori(1, 4) as i:
                quad(i, "A2")
            quad(4, "A2")
            with dve.Fori(5, 8) as i:
                quad(i, "N2")
            quad(8, "N2", gemm=False)
            meet(dve, 3)

            for p in (3, 4):
                part_lo(PARTS_2, p, len(PARTS_1))

            def rows_out(i, s, last_group=False):
                g = 2 * i + (G_OUT2 + s)
                split_lo(dve, 2 * g + 1, 1)
                if not last_group:
                    split_lo(dve, 2 * g + 2, 0)
                summed(g)
                for b in range(2, TB):
                    last = dve.tensor_copy(z[:, b, bass.ds(512 * i + 256 * s, 256)], bank[4 * s + b][:, 0:GC])
                last.then_inc(ev_dve, 1)
                dve.wait_ge(ev_dve, g - 40)
                dve.wait_ge(ev_act, g - 16)
                for b in range(TB):
                    last = dve.bn_stats(st_z[:, b, bass.ds(12 * i + 6 * s, 6)], z[:, b, bass.ds(512 * i + 256 * s, 256)])
                last.then_inc(st_s, 1)

            with dve.Fori(0, 3) as i:
                for s in range(2):
                    rows_out(i, s)
            rows_out(3, 0)
            rows_out(3, 1, last_group=True)
            dve.wait_ge(st_s, 8)
            for b in range(TB):
                last = dve.bn_aggr(mv[:, b, :], st_z[:, b, :])
            last.then_inc(ln_s, 1)
            dve.wait_ge(ln_s, 1)
            dve.tensor_scalar(rsk[:, 0:TB], mv[:, :, 1], LN_EPS, None, ALU.add).then_inc(ln_s, 1)
            dve.wait_ge(rt2_s, 6)
            dve.reciprocal(rsk[:, 0:TB], ssk[:, 0:TB]).then_inc(ln_s, 1)
            dve.wait_ge(ln_s, 3)
            dve.scalar_tensor_tensor(out=nmr[:], in0=mv[:, :, 0], scalar=-1.0, in1=rsk[:, 0:TB], op0=ALU.mult,
                                     op1=ALU.mult).then_inc(ln_s, 1)
            dve.wait_ge(ln_loaded, 32)
            for b in range(TB):
                dve.wait_ge(ln_a, b + 1)
                dve.tensor_tensor(z[:, b, :], z[:, b, :], ln_g[:], ALU.mult).then_inc(ln_m, 1)
                if b >= 2:
                    dve.wait_ge(ln_m, b + 1)
                    dve.tensor_tensor(z[:, b, :], z[:, b, :], ln_b[:], ALU.add).then_inc(ln_v, 1)
            meet(dve, 4)

        @block.gpsimd
        def _(pool):
            for n, done in enumerate(staged_out + o_out + x1_out):
                pool.dma_start(first_d[n:n + 1, :], con_in[n:n + 1, 0:16]).then_inc(done, 16)
            pool.wait_ge(pe_s, 6)
            for dst, src in ((rows_a, rows_1a[:]), (rows_b, rows_1b[:]), (rows_2d, rows_2[:]),
                             (rows_n, rpb_in.rearrange("h r c -> h (r c)"))):
                pool.dma_start(dst.ap(), src.unsqueeze(1).to_broadcast(list(dst.shape))).then_inc(brow_out, 16)
            pool.wait_ge(brow_out, 64)
            for m in range(8):
                pool.wait_ge(tt_s, KT + m + 1)
                pool.tensor_tensor(mem_t[1][:, 2 * m:2 * m + 2, :].rearrange("p a b -> p (a b)"), tr_h[m % 2][:],
                                   mem_t[0][:, 2 * m:2 * m + 2, :].rearrange("p a b -> p (a b)").bitcast(F32),
                                   ALU.subtract).then_inc(ml_s, 1)

            pool.wait_ge(ev_act, 3)
            pool.wait_ge(ev_dve, 3)
            for j in range(ITEMS_B):
                pool.dma_start(v_d[j].rearrange("p (b c) -> p b c", c=P),
                               bkv_n[:, :, 64 + 64 * (j // 3):192 + 64 * (j // 3)]).then_inc(kst_v, 16)
            pool.wait_ge(kv_act, 8)
            pool.wait_ge(kv_dve, 8)
            for h in range(HEADS_A):
                pool.dma_start(v_d[10 + h].rearrange("p (b c) -> p b c", c=P),
                               v_nat[:, :, h * P:(h + 1) * P]).then_inc(kst_v, 16)
            pool.wait_ge(sp_o, 3)
            for j in range(ITEMS_B):
                pool.dma_start(k_d[j], kt_b[:, j // 3, :]).then_inc(kst_k, 16)
            pool.wait_ge(ev_act, 7)
            pool.wait_ge(ev_dve, 7)
            for h in range(HEADS_C):
                pool.dma_start(v_d[6 + h, :, 0:256].rearrange("p (b c) -> p b c", c=P),
                               mem_vn[:, :, h * P:(h + 1) * P]).then_inc(kst_v, 16)
            pool.wait_ge(sp_o, 7)
            for h in range(HEADS_A):
                pool.dma_start(k_d[10 + h], kt_a[:, h, :]).then_inc(kst_k, 16)
            pool.wait_ge(sp_o, 8)
            for h in range(HEADS_C):
                pool.dma_start(k_d[6 + h, :, 0:256], kt_c[:, h, :]).then_inc(kst_k, 16)

            def tiles(dst, i):
                return dst[bass.ds(i, 2)].rearrange("n p t -> p n t")

            for dst, g0, n in ((iq_d, G_IQ, 4), (q_d, G_Q, 8), (g_d, G_GATE, 8)):
                with pool.Fori(0, n // 2) as i:
                    for s in range(2):
                        g = 2 * i + (g0 + s)
                        pool.wait_ge(ev_act, g)
                        pool.wait_ge(ev_dve, g)
                        pool.nop(nofuse=True)
                        pool.dma_start(tiles(dst, 4 * i + 2 * s), stage[s][:]).then_inc(staged_out[s], 16)
                if g0 == G_IQ:
                    for par in range(2):
                        pool.wait_ge(staged_out[par], 48)
                    for par in range(2):
                        pool.dma_start(qb1[par][:], iq_d[par]).then_inc(iq_loaded[par], 16)
            meet(pool, 1)
            for s in range(2):
                pool.wait_ge(staged_out[s], 176)

            def mix_store(g, i, par, t0):
                pool.wait_ge(ev_act, g)
                pool.nop(nofuse=True)
                pool.dma_start(mix_d[2 * i + (t0 + par)], stage[par][:].rearrange("p n t -> p (n t)")).then_inc(staged_out[par], 16)

            def load_item(n, par):
                pool.dma_start(qb1[par][:], q_d[n]).then_inc(it_loaded[par], 16)
                pool.dma_start(kb1[par][:], k_d[n]).then_inc(it_loaded[par], 16)
                pool.dma_start(vb1[par][:].rearrange("p a b -> p (a b)"), v_d[n]).then_inc(it_loaded[par], 16)
                pool.dma_start(gb1[par][:], g_d[n]).then_inc(it_loaded[par], 16)

            def load_c(n, par):
                pool.dma_start(qb1[par][:], q_d[n]).then_inc(it_loaded[par], 16)
                pool.dma_start(kb1[par][:, 0:MEM], k_d[n, :, 0:MEM]).then_inc(it_loaded[par], 16)
                pool.dma_start(vb1[par][:, 0:2, :].rearrange("p a b -> p (a b)"), v_d[n, :, 0:2 * P]).then_inc(it_loaded[par], 16)
                pool.dma_start(gb1[par][:], g_d[n]).then_inc(it_loaded[par], 16)

            def shifted(rows, h, at, width, row_step):
                L = rows.shape[2]
                return bass.AP(rows, at + h * (COPIES * L), [[L - row_step, 8], [L - 1, 16], [1, width]])

            def bias_b(j, par):
                pool.dma_start(bb1[par][:], shifted(rows_b, j, 127, 2 * ROW_B - P, 16)).then_inc(b_loaded[par], 16)

            def bias_a(h, par):
                pool.dma_start(bb1[par][:, 0:T], shifted(rows_a, h, 127, T, 16)).then_inc(b_loaded[par], 16)

            def iq_step(i, par, load=True):
                t = 2 * i + par
                if load:
                    pool.wait_ge(i_psum, 6 * t + 9)
                    pool.dma_start(qb1[par][:], iq_d[2 * i + (par + 2)]).then_inc(iq_loaded[par], 16)
                mix_store(2 * i + (G_MIX + par), i, par, 0)

            with pool.Fori(0, 3) as i:
                for par in range(2):
                    iq_step(i, par)
            bias_b(0, 0)
            bias_b(1, 1)
            for par in range(2):
                pool.wait_ge(i_psum, 45 + 6 * par)
                pool.nop(nofuse=True)
                load_item(par, par)
                iq_step(3, par, load=False)
            pool.wait_ge(i_acc, 51)
            for tb in range(1, TB):
                d = score[:, tb, tb * P:(tb + 1) * P]
                pool.affine_select(out=d, in_=d, compare_op=ALU.is_ge, fill=FILL, base=0, pattern=[[-1, P]],
                                   channel_multiplier=1).then_inc(cz_s, 1)

            def step(n_it, i, par, g, nxt):
                mix_store(g, i, par, n_it)
                pool.wait_ge(o_ready, 2 * i + (n_it - 5 + par))
                pool.nop(nofuse=True)
                pool.dma_start(o_d[2 * i + (n_it - 8 + par)], o_st[par][:]).then_inc(o_out[par], 16)
                if nxt:
                    nxt(2 * i + (n_it - 6 + par), par)

            def next_b(n, par):
                load_item(n, par)
                bias_b(n, par)

            def next_a(n, par):
                load_item(n, par)
                bias_a(n - 10, par)

            def load_part(src, parts, p):
                k0, k1 = parts[p]
                pool.dma_start(o_raw[:, k0:k1, :], src[k0:k1].rearrange("n p t -> p n t")).then_inc(ol_s[p], 16)

            for n_it, count, same, after in ((8, ITEMS_B, next_b, load_c), (14, ITEMS_C, load_c, next_a),
                                             (18, ITEMS_A, next_a, None)):
                with pool.Fori(0, count // 2 - 1) as i:
                    for par in range(2):
                        step(n_it, i, par, 2 * i + (G_MIX + n_it + par), same)
                if not after:
                    pool.drain().then_inc(barrier, 1)
                    for s in range(2):
                        pool.wait_ge(o_out[s], 128)
                    for p in range(4):
                        load_part(o_d, PARTS_1, p)
                i = count // 2 - 1
                for par in range(2):
                    step(n_it, i, par, 2 * i + (G_MIX + n_it + par), after)
            pool.wait_ge(o_out[0], 144)
            load_part(o_d, PARTS_1, 4)
            pool.wait_ge(barrier, 8)

            def load_gates(j):
                pool.dma_start(mixg[:].rearrange("p c n t -> p c (n t)"),
                               mix_d[bass.ds(3 * j, 3)].rearrange("c p t -> p c t")).then_inc(mg_loaded, 16)

            for s in range(2):
                pool.wait_ge(staged_out[s], 368)
            load_gates(0)
            pool.wait_ge(o_out[1], 144)
            load_part(o_d, PARTS_1, 5)
            with pool.Fori(1, 8) as j:
                pool.wait_ge(up_ev, 3 * j + 3)
                pool.nop(nofuse=True)
                load_gates(j)

            pool.wait_ge(up_lo, 9)
            with pool.Fori(0, 4) as i:
                for s in range(2):
                    pool.wait_ge(chunk_used, 4 * i + (2 * (G_WO + s) - 2))
                    pool.nop(nofuse=True)
                    pool.dma_start(xc[s][:], x_cols[:, :, bass.ds(512 * i + 256 * s, 256)]).then_inc(xr_loaded[s], 16)
                for s in range(2):
                    pool.wait_ge(x1f_s, 4 * i + (2 * s + 6))
                    pool.nop(nofuse=True)
                    pool.dma_start(x1_d[2 * i + s], stage[s][:]).then_inc(x1_out[s], 16)
            for s in range(2):
                pool.wait_ge(x1_out[s], 80)

            def load_pair(quad_, p):
                for c in range(3):
                    pool.dma_start(qkvg[p][c][:], qkvg_d[quad_, c, p]).then_inc(it_loaded[p], 16)

            def next_bias(kind, i, j):
                e = (j + 1) % 2
                h = 4 * i + (j - 3)
                pool.wait_ge(l_ready, 16 * i + (56 + 4 * j))
                pool.nop(nofuse=True)
                if kind == "A2":
                    pool.dma_start(b2[e][:], shifted(rows_2d, h, 127, 896, 16)).then_inc(b_loaded[e], 16)
                else:
                    pool.dma_start(nl[e][:].rearrange("p a b -> p (a b)"),
                                   shifted(rows_n, h - HEADS_2, 7 * 64 + 15, T, 64)).then_inc(b_loaded[e], 16)
                    pool.wait_ge(b_loaded[e], bias2_loaded(i, j + 1))
                    pool.nop(nofuse=True)
                    for cb in range(4):
                        c0 = BLK_START[cb] - 16 * cb + 16
                        m = con[:, CON["nmask"][0] + 32 * cb:CON["nmask"][0] + 32 * cb + 32]
                        last = pool.tensor_tensor(nb[e][:, cb, :, :], nl[e][:, :, c0:c0 + 32],
                                                  m.unsqueeze(1).to_broadcast([P, 8, 32]), ALU.add)
                    last.then_inc(nb_ready[e], 1)

            def windows(i, p):
                pool.wait_ge(it_loaded[p], pair_loaded(i))
                pool.nop(nofuse=True)
                for cb in range(4):
                    last = pool.tensor_copy(v_win[p][:, 256 * cb:256 * cb + 256].rearrange("p (r c) -> p r c", c=32),
                                            qkvg[p][2][:].rearrange("p (r c) -> p r c", c=64)[:, :, BLK_START[cb]:BLK_START[cb] + 32])
                last.then_inc(vw_ready, 1)

            def stored(i, j):
                pool.wait_ge(staged_out[j % 2], 32 * i + (16 * (j // 2) + 384))
                pool.nop(nofuse=True)

            def quad(i, att, bias_next, gemm=True):
                for j in range(4):
                    par, e = j // 2, j % 2
                    g = 4 * i + (G_IN2 + j)
                    if j == 0 and att:
                        stored(i - 1, 3)
                        pool.dma_start(qkvg[0][3][:], qkvg_d[i - 1, 3, 0]).then_inc(g2_loaded[0], 16)
                        pool.wait_ge(o_ready, outs_before(i, 0))
                        pool.nop(nofuse=True)
                        load_pair(i - 1, 1)
                        pool.dma_start(qkvg[1][3][:], qkvg_d[i - 1, 3, 1]).then_inc(g2_loaded[1], 16)
                    if j == 3 and gemm:
                        stored(i, 0)
                        stored(i, 1)
                        stored(i, 2)
                        load_pair(i, 0)
                        if bias_next == "N2":
                            windows(i + 1, 0)
                    if j < 3 and att:
                        next_bias(att, i, j)
                    if j == 0 and att == "N2":
                        windows(i, 1)
                    if j == 3 and bias_next:
                        next_bias(bias_next, i, j)
                    if att and e == 1:
                        pool.wait_ge(o_ready, outs_before(i, par) + 1)
                        pool.nop(nofuse=True)
                        pool.dma_start(y_d[2 * i + (par - 2)], o_st[par][:]).then_inc(o_out[par], 16)
                    if not gemm:
                        if j == 0:
                            pool.wait_ge(chunk_used, 2 * G_OUT2)
                            for s in range(2):
                                pool.wait_ge(o_out[s], 256)
                        if j == 3:
                            pool.wait_ge(o_out[0], 272)
                        load_part(y_d, PARTS_2, j)
                    if gemm:
                        pool.wait_ge(ev_act, g - 16)
                        pool.wait_ge(ev_dve, g - 40)
                        pool.nop(nofuse=True)
                        pool.dma_start(qkvg_d[i, j].rearrange("n p t -> p n t"), stage[j % 2][:]).then_inc(staged_out[j % 2], 16)

            quad(0, None, "A2")
            with pool.Fori(1, 4) as i:
                quad(i, "A2", "A2")
            quad(4, "A2", "N2")
            with pool.Fori(5, 8) as i:
                quad(i, "N2", "N2")
            pool.drain().then_inc(barrier, 1)
            quad(8, "N2", None, gemm=False)
            pool.wait_ge(barrier, 12)

            def load_x1(i, s):
                pool.dma_start(xr[s][:], x1_d[2 * i + s]).then_inc(xr_loaded[s], 16)

            for s in range(2):
                load_x1(0, s)
            pool.wait_ge(o_out[1], 272)
            load_part(y_d, PARTS_2, 4)
            pool.dma_start(ln_g[:], lng_in.partition_broadcast(P)).then_inc(ln_loaded, 16)
            pool.dma_start(ln_b[:], lnb_in.partition_broadcast(P)).then_inc(ln_loaded, 16)
            with pool.Fori(1, 4) as i:
                for s in range(2):
                    pool.wait_ge(chunk_used, 4 * i + (2 * (G_OUT2 + s) - 2))
                    pool.nop(nofuse=True)
                    load_x1(i, s)
            for b in range(TB):
                if b < 2:
                    pool.wait_ge(ln_m, b + 1)
                    pool.tensor_tensor(z[:, b, :], z[:, b, :], ln_b[:], ALU.add).then_inc(ln_p, 1)
                    pool.wait_ge(ln_p, b + 1)
                else:
                    pool.wait_ge(ln_v, b - 1)
                pool.dma_start(out_v[b], z[:, b, :]).then_inc(fin_out, 16)
            pool.wait_ge(fin_out, 64)
            meet(pool, 4)


def chunks_of(w):
    n = w.shape[1] // GC
    return w.reshape(2, CK, P, n, GC).transpose(3, 0, 2, 1, 4).reshape(2 * n, P, CK * GC)


def padded(w):
    return np.pad(w, ((0, 0), (0, 0), (0, CK * GC - w.shape[2])))


def weight_stream(a):
    w_in, w_in2 = a["w_in"][0], a["w_in_2"][0]
    cut = np.cumsum([0, A_W, KV_RANK, 1024, 64, 16, A_W, B_W, 128, 128, B_W, C_W, C_W, 3 * D]).tolist()
    a_q, ckv, i_q, i_k, i_w, a_g, b_q, b_k, b_v, b_g, c_q, c_g, mix = (w_in[:, p:q] for p, q in zip(cut, cut[1:]))
    ik = np.concatenate([i_k, i_w], 1).reshape(2, CK, P, 80).transpose(0, 2, 1, 3).reshape(2, P, CK * 80)
    kv_up = a["w_kv_up"][0].reshape(2, P, 2, A_W).transpose(2, 1, 0, 3).reshape(2, P, 2 * A_W)
    mix = mix.reshape(D, 3, 8, GC)[:, [1, 2, 0]].transpose(0, 2, 1, 3).reshape(D, 3 * D)
    up = np.concatenate([a["w_up_b"][0], a["w_up_c"][0], a["w_up_a"][0]], 0)
    in2 = w_in2.reshape(D, 2, 4, 4, GC).transpose(0, 1, 3, 2, 4).reshape(D, 4 * D)
    return np.concatenate([
        chunks_of(ckv), padded(ik), chunks_of(np.concatenate([b_k, b_v], 1)), padded(kv_up), chunks_of(a["w_mem_kv"][0]),
        chunks_of(i_q), chunks_of(np.concatenate([b_q, c_q, a_q], 1)), chunks_of(np.concatenate([b_g, c_g, a_g], 1)),
        chunks_of(mix), chunks_of(up), chunks_of(a["w_o"][0]), chunks_of(in2), chunks_of(a["w_out_2"][0])], 0)


def parameters(a):
    twice = lambda g: np.concatenate([g, g]).reshape(P, 1)
    col = lambda g: g.reshape(P, 1)
    tiles = lambda g: g.reshape(-1, P).T
    q_g = np.concatenate([np.repeat(twice(a["q_norm_b"][0]), 6, 1), np.repeat(col(a["q_norm_c"][0]), 4, 1),
                          np.repeat(col(a["q_norm_a"][0]), 6, 1)], 1)
    gate_b = a["gate_bias"][0].reshape(3, 8, GC)[[1, 2, 0]].transpose(1, 0, 2).reshape(-1)
    return np.concatenate([
        tiles(a["norm_g"][0]), tiles(a["mem_norm_g"][0]), tiles(a["kv_norm_g"][0]), twice(a["idx_k_ln_g"][0]),
        twice(a["idx_k_ln_b"][0]), col(a["k_norm_a"][0]), twice(a["k_norm_b"][0]), col(a["k_norm_c"][0]), q_g,
        tiles(gate_b), np.repeat(a["sinks_b"][0].reshape(1, HEADS_B), P, 0)], 1)


def kernel(**inputs):
    from concourse import bacc
    from concourse.bass_utils import run_bass_kernel_spmd

    a = {n: np.asarray(v) for n, v in inputs.items()}
    with_one = lambda t: np.concatenate([t, np.ones((1, t.shape[1]), t.dtype)], 0)
    arrays = {
        "wst": weight_stream(a), "x_rows": a["x"][0], "mem_rows": a["mem"][0], "params": parameters(a),
        "consts": constants(), "positions": position_tables(), "tab_1": with_one(a["rel_bias"]),
        "tab_2": with_one(a["t5_bias_2"]), "rpb": np.pad(a["na_rpb_2"][0], ((0, 0), (0, 1), (16, 17))),
        "ln_gain": a["ln_gain_2"][0], "ln_bias": a["ln_bias_2"][0],
    }
    arrays = {n: np.ascontiguousarray(v) for n, v in arrays.items()}
    nc = bacc.Bacc("TRN2", target_bir_lowering=False, num_devices=1)
    aps = [nc.dram_tensor(n, v.shape, mybir.dt.from_np(v.dtype), kind="ExternalInput").ap() for n, v in arrays.items()]
    out = nc.dram_tensor("out", (1, T, D), F32, kind="ExternalOutput").ap()
    build_kernel(nc, *aps, out)
    r = run_bass_kernel_spmd(nc, [arrays], core_ids=[0])
    return r.results[0]["out"]
```
